# Optimizing a Trainium2 kernel written in Bass

```python
import jax, jax.numpy as jnp
from jax import lax
import numpy as np

D_MODEL = 1024
BATCH = 1
SEQ = 512
DEPTH = 1

CHUNK = 64
POOL_WINDOWS = (2, 4, 8, 16)
POOL_GROUPS = len(POOL_WINDOWS)
D_POOL = D_MODEL // 2
POOL_GC = D_POOL // POOL_GROUPS
RWKV_HEAD = 64
D_RWKV = D_MODEL
RWKV_HEADS = D_RWKV // RWKV_HEAD
D_DECAY_LORA = 64
D_AAA_LORA = 64
D_GATE_LORA = 160
D_FF = 4 * D_MODEL
N_BRANCH = 2
D_SHIFTED = 3 * D_RWKV + D_DECAY_LORA + D_AAA_LORA + D_GATE_LORA
D_IN = D_POOL + D_SHIFTED + N_BRANCH * D_MODEL
SHIFT_SPLITS = (D_RWKV, 2 * D_RWKV, 3 * D_RWKV, 3 * D_RWKV + D_DECAY_LORA,
                3 * D_RWKV + D_DECAY_LORA + D_AAA_LORA)
ALPHA = (2 * DEPTH) ** 0.25
BETA = (8 * DEPTH) ** -0.25
LN_EPS = 1e-5
GN_EPS = 64e-5

kernel_name = "hybrid_pool_rwkv7_adaln_deepnorm"

def layer_norm(x, g, b, eps):
    xf = x.astype(jnp.float32)
    mu = jnp.mean(xf, axis=-1, keepdims=True)
    var = jnp.mean(jnp.square(xf - mu), axis=-1, keepdims=True)
    return (xf - mu) * lax.rsqrt(var + eps) * g.astype(jnp.float32) + b.astype(jnp.float32)

def token_shift(p):
    return jnp.pad(p, ((0, 0), (1, 0), (0, 0)))[:, :-1]

def multiscale_pool(u):
    b, s, _ = u.shape
    ug = u.astype(jnp.float32).reshape(b, s, POOL_GROUPS, POOL_GC)
    cs = jnp.cumsum(ug, axis=1)
    count = jnp.arange(1, s + 1, dtype=jnp.float32)
    outs = []
    for gi, w in enumerate(POOL_WINDOWS):
        cg = cs[:, :, gi]
        lag = jnp.pad(cg[:, : s - w], ((0, 0), (w, 0), (0, 0)))
        cnt = jnp.minimum(count, float(w))
        outs.append((cg - lag) / cnt[None, :, None] - ug[:, :, gi])
    return jnp.stack(outs, axis=2)

def pool_branch(u, pool_mix, pool_scale, w_up):
    b, s, _ = u.shape
    m = multiscale_pool(u)
    m = jnp.einsum('bsgc,gcd->bsgd', m, pool_mix.astype(jnp.float32)).reshape(b, s, D_POOL)
    m = (m * pool_scale.astype(jnp.float32)).astype(u.dtype)
    return m @ w_up

def wkv7_scan(r, decay, k, v, kk, a):
    b, s, h, n = r.shape

    def to_chunks(z):
        return jnp.moveaxis(z, 1, 0).reshape(s // CHUNK, CHUNK, b, h, n)

    seqs = tuple(to_chunks(z) for z in (r, decay, k, v, -kk, kk * a))

    def step(state, inp):
        r_t, w_t, k_t, v_t, a_t, b_t = inp
        sa = jnp.einsum('bhvk,bhk->bhv', state, a_t)
        state = (state * w_t[:, :, None, :] + sa[..., None] * b_t[:, :, None, :]
                 + v_t[..., None] * k_t[:, :, None, :])
        return state, jnp.einsum('bhvk,bhk->bhv', state, r_t)

    def chunk_step(state, chunk_inp):
        return lax.scan(step, state, chunk_inp)

    state0 = jnp.zeros((b, h, n, n), jnp.float32)
    _, out = lax.scan(chunk_step, state0, seqs)
    return jnp.moveaxis(out.reshape(s, b, h, n), 0, 1)

def rwkv7_branch(ps, mu, w0, w_decay_up, a0, w_aaa_up, w_gate_up, k_k, k_a, r_k, gn_g, gn_b, w_up):
    b, s, _ = ps.shape
    xs = ps + (token_shift(ps) - ps) * mu
    r, k, v, xw, xa, xg = jnp.split(xs, SHIFT_SPLITS, axis=-1)
    w = -jax.nn.softplus(-(w0 + jnp.tanh(xw) @ w_decay_up)) - 0.5
    decay = jnp.exp(-jnp.exp(w.astype(jnp.float32)))
    a = jax.nn.sigmoid(a0 + xa @ w_aaa_up)
    g = jax.nn.sigmoid(xg) @ w_gate_up

    def heads(z):
        return z.astype(jnp.float32).reshape(b, s, RWKV_HEADS, RWKV_HEAD)

    kk = heads(k * k_k)
    kk = kk / jnp.maximum(jnp.linalg.norm(kk, axis=-1, keepdims=True), 1e-12)
    k = k * (1 + (a - 1) * k_a)
    rh, kh, vh = heads(r), heads(k), heads(v)
    o = wkv7_scan(rh, heads(decay), kh, vh, kk, heads(a))
    o = layer_norm(o, gn_g.reshape(RWKV_HEADS, RWKV_HEAD), gn_b.reshape(RWKV_HEADS, RWKV_HEAD), GN_EPS)
    o = o + jnp.sum(rh * kh * r_k.astype(jnp.float32), axis=-1, keepdims=True) * vh
    o = (o.reshape(b, s, D_RWKV) * g.astype(jnp.float32)).astype(ps.dtype)
    return o @ w_up

def setup_inputs(seed: int = 0) -> dict:
    key = jax.random.key(seed)
    ks = jax.random.split(key, 28)
    L = DEPTH

    def nrm(k, shape, scale):
        return jax.random.normal(k, shape, jnp.float32) * scale

    return {
        "x": nrm(ks[0], (BATCH, SEQ, D_MODEL), 1.0),
        "c": nrm(ks[1], (BATCH, D_MODEL), 1.0),
        "w_ada": nrm(ks[2], (L, D_MODEL, 6 * D_MODEL), 0.5 * D_MODEL ** -0.5),
        "b_ada": nrm(ks[3], (L, 6 * D_MODEL), 0.02),
        "w_in": nrm(ks[4], (L, D_MODEL, D_IN), D_MODEL ** -0.5),
        "mu_shift": jax.random.uniform(ks[5], (L, D_SHIFTED), jnp.float32),
        "pool_mix": nrm(ks[6], (L, POOL_GROUPS, POOL_GC, POOL_GC), POOL_GC ** -0.5),
        "pool_scale": 1.0 + nrm(ks[7], (L, D_POOL), 0.1),
        "w_pool_up": nrm(ks[8], (L, D_POOL, D_MODEL), D_POOL ** -0.5),
        "w0": jax.random.uniform(ks[9], (L, D_RWKV), jnp.float32, -4.0, 1.0),
        "w_decay_up": nrm(ks[10], (L, D_DECAY_LORA, D_RWKV), 0.5 * D_DECAY_LORA ** -0.5),
        "a0": nrm(ks[11], (L, D_RWKV), 0.5),
        "w_aaa_up": nrm(ks[12], (L, D_AAA_LORA, D_RWKV), 0.5 * D_AAA_LORA ** -0.5),
        "w_gate_up": nrm(ks[13], (L, D_GATE_LORA, D_RWKV), D_GATE_LORA ** -0.5),
        "k_k": 0.85 + nrm(ks[14], (L, D_RWKV), 0.05),
        "k_a": 1.0 + nrm(ks[15], (L, D_RWKV), 0.05),
        "r_k": nrm(ks[16], (L, RWKV_HEADS, RWKV_HEAD), 0.1),
        "gn_g": 1.0 + nrm(ks[17], (L, D_RWKV), 0.05),
        "gn_b": nrm(ks[18], (L, D_RWKV), 0.02),
        "w_rwkv_up": nrm(ks[19], (L, D_RWKV, D_MODEL), D_RWKV ** -0.5),
        "w_out": nrm(ks[20], (L, D_MODEL, D_MODEL), BETA * D_MODEL ** -0.5),
        "ln1_g": 1.0 + nrm(ks[21], (L, D_MODEL), 0.05),
        "ln1_b": nrm(ks[22], (L, D_MODEL), 0.02),
        "w_ff1": nrm(ks[23], (L, D_MODEL, D_FF), D_MODEL ** -0.5),
        "w_ff2": nrm(ks[24], (L, D_FF, D_MODEL), BETA * D_FF ** -0.5),
        "ln2_g": 1.0 + nrm(ks[25], (L, D_MODEL), 0.05),
        "ln2_b": nrm(ks[26], (L, D_MODEL), 0.02),
    }

def reference(x, c, w_ada, b_ada, w_in, mu_shift, pool_mix, pool_scale, w_pool_up, w0, w_decay_up,
              a0, w_aaa_up, w_gate_up, k_k, k_a, r_k, gn_g, gn_b, w_rwkv_up, w_out, ln1_g, ln1_b,
              w_ff1, w_ff2, ln2_g, ln2_b):
    cond = jax.nn.silu(c)
    for l in range(DEPTH):
        mod = (cond @ w_ada[l] + b_ada[l])[:, None, :]
        sh1, sc1, gt1, sh2, sc2, gt2 = jnp.split(mod, 6, axis=-1)
        h = x * (1 + sc1) + sh1
        p = h @ w_in[l]
        p_pool, p_rwkv, p_gate = jnp.split(p, (D_POOL, D_POOL + D_SHIFTED), axis=-1)
        y_pool = pool_branch(p_pool, pool_mix[l], pool_scale[l], w_pool_up[l])
        y_rwkv = rwkv7_branch(p_rwkv, mu_shift[l], w0[l], w_decay_up[l], a0[l], w_aaa_up[l],
                              w_gate_up[l], k_k[l], k_a[l], r_k[l], gn_g[l], gn_b[l], w_rwkv_up[l])
        g_pool, g_rwkv = jnp.split(jax.nn.sigmoid(p_gate), 2, axis=-1)
        mixed = (g_pool * y_pool + g_rwkv * y_rwkv) @ w_out[l]
        x = layer_norm(ALPHA * x + (1 + gt1) * mixed, ln1_g[l], ln1_b[l], LN_EPS).astype(x.dtype)
        h = x * (1 + sc2) + sh2
        f = jnp.square(jax.nn.relu(h @ w_ff1[l])) @ w_ff2[l]
        x = layer_norm(ALPHA * x + (1 + gt2) * f, ln2_g[l], ln2_b[l], LN_EPS).astype(x.dtype)
    return x


_drawn_inputs = setup_inputs


def setup_inputs(seed=0):
    import zlib

    import numpy as np

    out = dict(_drawn_inputs(seed))
    spreads = {}
    factors = {'w_decay_up': 5.059,
     'k_k': 8.0,
     'k_a': 5.424,
     'gn_g': 7.825,
     'gn_b': 28.394,
     'ln1_b': 2.713,
     'ln2_b': 2.806,
     'pool_scale': 3.348}
    for name, (base, spread) in spreads.items():
        noise = np.random.default_rng([zlib.crc32(name.encode()), seed]).standard_normal(out[name].shape)
        drawn = base * np.exp(spread * noise) if base else spread * noise
        out[name] = __import__('jax').numpy.asarray(drawn.astype(out[name].dtype))
    for name, factor in factors.items():
        out[name] = (out[name] * factor).astype(out[name].dtype)
    return out
```

```python
from contextlib import ExitStack

import concourse.bass as bass
from concourse import mybir

P = 128
ALU = mybir.AluOpType
ACT = mybir.ActivationFunctionType
AX_X = mybir.AxisListType.X
F32 = mybir.dt.float32
F32R = mybir.dt.float32r


def build(nc, x, c, w_ada, b_ada, w_in, mu_shift, pool_mix, pool_scale, w_pool_up, w0, w_decay_up, a0,
          w_aaa_up, w_gate_up, k_k, k_a, r_k, gn_g, gn_b, w_rwkv_up, w_out, ln1_g, ln1_b, w_ff1, w_ff2,
          ln2_g, ln2_b, out):
    S, D = x.shape[1], x.shape[2]
    KT = D // P
    TB = S // P
    H = r_k.shape[1]
    N = r_k.shape[2]
    PAIRS = H * N // P
    C = 64
    NCH = S // C
    DP = pool_scale.shape[1]
    DW, DG = w_decay_up.shape[1], w_gate_up.shape[1]
    DG1 = DG - P
    COL_R = DP
    COL_K, COL_V = COL_R + D, COL_R + 2 * D
    COL_WA = COL_R + 3 * D
    COL_G0 = COL_WA + 2 * DW
    COL_G1 = COL_G0 + P
    EXPM = float(2.718281828459045 ** -0.5)
    ALPHA = 2.0 ** 0.25
    GN_EPS, LN_EPS = 64e-5, 1e-5
    SHIFT_TAIL = COL_G1 + DG1 - DP - 26 * P

    rows1 = dict(b_ada=0, mu=48, w0=74, a0=82, k_k=90, k_a=98, r_k=106, gn_g=114)
    rows2 = dict(gn_b=0, pool_scale=8, ln1_g=12, ln1_b=20, ln2_g=28, ln2_b=36, mu_tail=44)
    NP1, NP2 = 122, 45

    ctx = ExitStack()
    with ctx:
        def sb(name, shape, dt=F32):
            return ctx.enter_context(nc.sbuf_tensor(name, shape, dt))

        sems = {}

        def sem(name):
            if name not in sems:
                sems[name] = ctx.enter_context(nc.semaphore(name))
            return sems[name]

        h_hi, h_lo = sb("h_hi", [P, KT, S], F32R), sb("h_lo", [P, KT, S], F32R)
        y_hi, y_lo = sb("y_hi", [P, KT, S], F32R), sb("y_lo", [P, KT, S], F32R)
        RING = 2
        w_raw = [sb(f"w_raw{s}", [P, KT, P]) for s in range(RING)]
        w_hi = [sb(f"w_hi{s}", [P, KT, P], F32R) for s in range(RING)]
        w_lo = [sb(f"w_lo{s}", [P, KT, P], F32R) for s in range(RING)]
        lup = sb("lup", [P, 3, P])
        ident = sb("ident", [P, P])
        ones_all = sb("ones_all", [P, P])
        ones_col = sb("ones_col", [P, 1])
        ones_head = sb("ones_head", [P, P])
        params = sb("params", [P, 2 * P])
        p2 = P
        derived = sb("derived", [P, 96])
        mod = sb("mod", [P, 48])
        OMM, OMKA, HW0, HA0, CCOL, CS = 0, 27, 35, 43, 51, 59
        HM = 67
        xk, xr, aa, t1 = (sb(n, [P, S]) for n in ("xk", "xr", "aa", "t1"))
        wk = ExitStack()

        def wb(name, shape, dt=F32):
            return wk.enter_context(nc.sbuf_tensor(name, shape, dt))

        m16T = wb("m16T", [P, P])
        m16 = wb("m16", [P, P])
        m32 = wb("m32", [P, P])
        m64 = wb("m64", [P, P])
        mlow = wb("mlow", [P, P])
        mupi = wb("mupi", [P, P])
        scanm = wb("scanm", [P, S])
        xwa, xg0, xg1 = wb("xwa", [P, S]), wb("xg0", [P, S]), wb("xg1", [DG1, S])
        xv, sg, t2, t3, t4 = (wb(n, [P, S]) for n in ("xv", "sg", "t2", "t3", "t4"))
        At, Bt, Kt, Rf = (wb(n, [P, S]) for n in ("At", "Bt", "Kt", "Rf"))
        Apad, Rpad = wb("Apad", [P, 2, S]), wb("Rpad", [P, 2, S])
        DC = wb("DC", [P, NCH])
        Rc, DCc, bonus_c = wb("Rc", [P, S]), wb("DCc", [P, NCH]), wb("bonus_c", [P, S])
        A0, A0T, A1, A1T, MAB, MAK, TT, PT, MRB, MRK = (
            [wb(f"{n}{e}", [P, TB, P]) for e in range(2)]
            for n in ("A0", "A0T", "A1", "A1T", "MAB", "MAK", "TT", "PT", "MRB", "MRK"))
        AHT, Atok, Btok, Ktok = (wb(n, [P, TB, P]) for n in ("AHT", "Atok", "Btok", "Ktok"))
        Vpad = wb("Vpad", [P, 2, TB, P])
        bonus, gate = wb("bonus", [P, S]), wb("gate", [P, S])
        OC, SQ = wb("OC", [P, TB, P]), wb("SQ", [P, TB, P])
        Sbd, Stmp, SApad = wb("Sbd", [P, P]), wb("Stmp", [P, P]), wb("SApad", [P, 2, P])
        gn = wb("gn", [P, 4, 8])
        wk.close()
        st = ExitStack()

        def stb(name, shape, dt=F32):
            return st.enter_context(nc.sbuf_tensor(name, shape, dt))

        skip = stb("skip", [P, 6 * P + S])
        xtok = stb("xtok", [P, TB, D])
        ptab = stb("ptab", [P, 2, P])
        ada = [stb(f"ada{s}", [P, D]) for s in range(4)]
        acc = stb("acc", [P, 2, D])
        hf = [stb(f"hf{s}", [P, S]) for s in range(2)]
        crow = stb("crow", [KT, P])
        st.close()
        pt = ExitStack()

        def pb(name, shape, dt=F32):
            return pt.enter_context(nc.sbuf_tensor(name, shape, dt))

        for s in (2, 3):
            w_raw.append(pb(f"w_raw{s}", [P, KT, P]))
            w_hi.append(pb(f"w_hi{s}", [P, KT, P], F32R))
            w_lo.append(pb(f"w_lo{s}", [P, KT, P], F32R))
        mix_hi, mix_lo = pb("mix_hi", [P, KT, S], F32R), pb("mix_lo", [P, KT, S], F32R)
        res = pb("res", [P, KT, S])
        GP = DP // P
        wmix = pb("wmix", [P, GP, P])
        rec = pb("rec", [P, 16])
        f1, f2, f3 = (pb(n, [P, S]) for n in ("f1", "f2", "f3"))
        lnv = pb("lnv", [P, S])
        small = pb("small", [P, 64])
        stat = pb("stat", [P, 2 * TB, 6])
        ada2 = pb("ada_late", [P, D])
        acc2 = pb("acc2", [P, D])
        tail = ExitStack()
        mp_hi, mp_lo = (tail.enter_context(nc.sbuf_tensor(n, [P, GP, S], F32R)) for n in ("mp_hi", "mp_lo"))
        tail.close()
        xt2 = pb("xt2", [P, TB, D])
        pt.close()

        bank = [ctx.enter_context(nc.psum_tensor(f"bank{b}", [P, 512], F32)) for b in range(8)]
        G0, G1, CH, OB = bank[0], bank[1], bank[6], bank[7]

        def stage_bank(e, s_global):
            return bank[2 + 2 * e + s_global % 2]

        def blk(ap):
            return ap.rearrange("p (j t) -> p j t", j=TB)

        def over_blocks(mask):
            return mask[:, :].unsqueeze(1).to_broadcast([P, TB, P])

        STAGES = ["MabT", "Mab", "Mak", "Q1", "Q2", "Q3", "Q4", "U1", "Q5", "MrbT", "MrkT", "U2", "U3",
                  "X1", "Tr1", "Y1", "X2", "Tr2", "Y2", "PT", "AHT"]
        NS = len(STAGES)
        BY_DVE = {"MabT", "Mab", "Mak", "MrbT", "MrkT", "U1", "U2", "U3", "Y1", "Y2"}
        ND = len(BY_DVE)
        NA = NS - ND

        def evacuated(eng, e, i, name):
            at = STAGES.index(name)
            n = sum((m in BY_DVE) == (name in BY_DVE) for m in STAGES[:at + 1])
            if name in BY_DVE:
                eng.wait_ge(sem(f"taken_by_dve{e}"), ND * i + n)
            else:
                eng.wait_ge(sem(f"taken_by_act{e}"), NA * i + n)

        chunk_cols = [(COL_WA, P), (COL_G0, P), (COL_G1, DG1)]
        for n in range(PAIRS):
            chunk_cols += [(col + n * P, P) for col in (COL_K, COL_R, COL_V)]
        NCHUNK = len(chunk_cols)
        def w_cols(w, c0, width=P, r0=0, kts=KT):
            return w[0, r0:r0 + kts * P, c0:c0 + width].rearrange("(kt p) n -> p kt n", p=P)

        chunks = [(w_cols(w_in, c0, width), k % 2) for k, (c0, width) in enumerate(chunk_cols)]
        for g in range(GP):
            chunks.append((w_cols(w_in, g * P), len(chunks) % 2))
        FIRST_B = len(chunks)
        COL_GP = COL_G1 + DG1
        for n in range(KT):
            for src in (w_cols(w_in, COL_GP + n * P), w_cols(w_in, COL_GP + D + n * P), w_cols(w_rwkv_up, n * P),
                        w_cols(w_pool_up, n * P, kts=GP)):
                chunks.append((src, (len(chunks) - FIRST_B + 2) % 4))
        K_OUT = len(chunks)
        for n in range(KT):
            chunks.append((w_cols(w_out, n * P), (len(chunks) - FIRST_B + 2) % 4))
        K_FF = len(chunks)
        DFF = w_ff1.shape[2]
        NQ = DFF // D
        for q in range(NQ):
            for n in range(KT):
                chunks.append((w_cols(w_ff1, (q * KT + n) * P), (len(chunks) - FIRST_B + 2) % 4))
            for n in range(KT):
                chunks.append((w_cols(w_ff2, n * P, r0=q * D), (len(chunks) - FIRST_B + 2) % 4))
        NALL = len(chunks)
        K_GATE = lambda n: FIRST_B + 4 * n
        before, uses, seen = [], [], {}
        for k, (_, slot) in enumerate(chunks):
            before.append(seen[slot][0] if slot in seen else None)
            uses.append(seen[slot][1] + 1 if slot in seen else 1)
            seen[slot] = (k, uses[-1])

        g1_jobs = []
        for i in range(-1, PAIRS + 1):
            for s, job in ((4, "decay"), (5, "aaa"), (8, "norm"), (9, "tokA"), (10, "tokB"), (11, "tokK"),
                           (12, "tokV"), (13, "outT"), (15, "gate"), (18, "bonus")):
                n = i + {"t": 0, "g": 0, "o": -1}.get(job[0], 1)
                if 0 <= n < PAIRS:
                    g1_jobs.append((job, n))
        g1_at = {key: k for k, key in enumerate(g1_jobs)}

        POOLED_AT = [(PAIRS, 6), (PAIRS, 12), (PAIRS, 18), (PAIRS + 1, 6)]
        UP = [xk, xr, aa, t1]

        def per_slot(emit):
            for i in range(-1, PAIRS + 1):
                for s in range(NS):
                    emit(i, s)

        block = ctx.enter_context(nc.Block())

        def col(idx):
            return params[:, idx:idx + 1]

        def der(idx):
            return derived[:, idx:idx + 1]


        def part_of(k, buf):
            src, slot = chunks[k]
            return buf[slot][:, 0:src.shape[1], 0:src.shape[2]]

        def load_chunk(sp, k):
            src, slot = chunks[k]
            if before[k] is not None:
                sp.wait_ge(sem("lo_ready"), before[k] + 1)
            if k == FIRST_B:
                sp.wait_ge(sem("so_done"), NCH * PAIRS)
                sp.wait_ge(sem("y_lo_ready"), PAIRS)
            sp.dma_start(part_of(k, w_raw), src).then_inc(sem(f"w_in{slot}"), 16)

        def lup_next(sp, n):
            if n >= 1:
                sp.wait_ge(sem("g1_done"), g1_at[("aaa", n - 1)] + 1)
            cols = slice(n * P, (n + 1) * P)
            sp.dma_start(lup[0:DW, 0, :], w_decay_up[0, :, cols]).then_inc(sem("lup_in"), 16)
            sp.dma_start(lup[DW:P, 0, :], w_aaa_up[0, :, cols]).then_inc(sem("lup_in"), 16)

        def gup_next(sp, n):
            if n >= 1:
                sp.wait_ge(sem("g1_done"), g1_at[("gate", n - 1)] + 1)
            cols = slice(n * P, (n + 1) * P)
            sp.dma_start(lup[:, 1, :], w_gate_up[0, 0:P, cols]).then_inc(sem("gup_in"), 16)
            sp.dma_start(lup[0:DG1, 2, :], w_gate_up[0, P:DG, cols]).then_inc(sem("gup_in"), 16)

        @block.sync
        def _(sp):
            sp.wait_ge(sem("ptab_zero"), 1)
            def prow(tab, at, ap, n):
                sp.dma_start(ptab[at:at + n, tab, :], ap.rearrange("o (r f) -> (o r) f", f=P)).then_inc(sem("params_in"), 16)
            sp.dma_start(crow[:, :], c.rearrange("o (r f) -> (o r) f", f=P)).then_inc(sem("params_in"), 16)
            prow(0, 0, b_ada, 48)
            prow(0, 48, mu_shift[:, 0:26 * P], 26)
            prow(0, 74, w0, 8)
            prow(0, 82, a0, 8)
            prow(0, 90, k_k, 8)
            prow(0, 98, k_a, 8)
            sp.dma_start(ptab[106:114, 0, :], r_k.rearrange("o (r h) n -> (o r) (h n)", h=2)).then_inc(sem("params_in"), 16)
            prow(0, 114, gn_g, 8)
            prow(1, 0, gn_b, 8)
            prow(1, 8, pool_scale, 4)
            prow(1, 12, ln1_g, 8)
            prow(1, 20, ln1_b, 8)
            prow(1, 28, ln2_g, 8)
            prow(1, 36, ln2_b, 8)
            sp.dma_start(ptab[44:45, 1, 0:DG1], mu_shift[:, 26 * P:26 * P + DG1]).then_inc(sem("params_in"), 16)
            for j in range(TB):
                sp.dma_start(xtok[:, j, :], x[0, j * P:(j + 1) * P, :]).then_inc(sem("x_in"), 16)
            for q in range(2 * KT):
                sec, kt = (1, 0)[q // KT], q % KT
                if q >= 4:
                    sp.wait_ge(sem("ada_used"), q - 3)
                sp.dma_start(ada[q % 4][:, :], w_ada[0, kt * P:(kt + 1) * P, sec * D:(sec + 1) * D]).then_inc(sem(f"ada_in{q % 4}"), 16)
                if q == 3:
                    for k in range(RING):
                        load_chunk(sp, k)
            lup_next(sp, 0)
            gup_next(sp, 0)
            for k in range(RING, FIRST_B):
                load_chunk(sp, k)
                if k >= 6 and k % 3 == 0 and k < NCHUNK:
                    lup_next(sp, k // 3 - 1)
                if k >= 9 and k % 3 == 0 and k < NCHUNK:
                    gup_next(sp, k // 3 - 2)
            gup_next(sp, PAIRS - 1)
            for k in range(FIRST_B, FIRST_B + 2):
                load_chunk(sp, k)
            for g in range(GP):
                sp.dma_start(wmix[:, g, :], pool_mix[0, g]).then_inc(sem("wmix_in"), 16)
            for j in range(TB):
                sp.dma_start(xt2[:, j, :], x[0, j * P:(j + 1) * P, :]).then_inc(sem("x_again"), 16)
            na = 0
            for k in range(FIRST_B + 2, NALL):
                load_chunk(sp, k)
                for _ in range(2 if k >= K_GATE(1) + 3 else 0):
                    if na < 8 * KT:
                        sec, kt, half = 2 + na // (2 * KT), na // 2 % KT, na % 2
                        if na >= 2:
                            sp.wait_ge(sem("ada2_used"), na - 1)
                        sp.dma_start(ada2[:, half * S:(half + 1) * S],
                                     w_ada[0, kt * P:(kt + 1) * P, sec * D + half * S:sec * D + (half + 1) * S]
                                     ).then_inc(sem(f"ada2_in{half}"), 16)
                        na += 1
            sp.wait_ge(sem("ada2_used"), 8 * KT)
            sp.wait_ge(sem("mod2"), 4)
            sp.dma_start(acc2[:, :], ln2_g.to_broadcast([P, D])).then_inc(sem("ln2_in"), 16)
            sp.dma_start(ada2[:, :], ln2_b.to_broadcast([P, D])).then_inc(sem("ln2_in"), 16)
            for j in range(TB):
                sp.wait_ge(sem("out_ready"), j + 1)
                sp.dma_start(out[0, j * P:(j + 1) * P, :], xt2[:, j, :]).then_inc(sem("stored"), 16)
            sp.wait_ge(sem("stored"), 16 * TB)

        @block.gpsimd
        def _(pool):
            step = [0]

            def link(ins, name=None):
                s = sem(name or "pool_step")
                key = name or "pool_step"
                counts[key] = counts.get(key, 0) + 1
                ins.then_inc(s, 1)
                pool.wait_ge(s, counts[key])

            counts = {}
            link(pool.memset(ptab[:, :, :], 0.0), "ptab_zero")
            link(pool.memset(ident[:, :], 0.0))
            link(pool.affine_select(out=ident[:, :], in_=ident[:, :], compare_op=ALU.not_equal, fill=1.0, base=0,
                                    pattern=[[-1, P]], channel_multiplier=1), "ident_ready")

            def blocks(m, size, fill=0.0):
                v = m[:, :].rearrange("p (b t) -> p b t", t=size)
                link(pool.affine_select(out=v, in_=v, compare_op=ALU.is_ge, fill=fill, base=0,
                                        pattern=[[-size, P // size], [0, size]], channel_multiplier=1))
                link(pool.affine_select(out=v, in_=v, compare_op=ALU.is_ge, fill=fill, base=size - 1,
                                        pattern=[[size, P // size], [0, size]], channel_multiplier=-1))

            def below(m, base):
                link(pool.affine_select(out=m[:, :], in_=m[:, :], compare_op=ALU.is_ge, fill=0.0, base=base,
                                        pattern=[[-1, P]], channel_multiplier=1))

            def above(m, base):
                link(pool.affine_select(out=m[:, :], in_=m[:, :], compare_op=ALU.is_ge, fill=0.0, base=base,
                                        pattern=[[1, P]], channel_multiplier=-1))

            for m in (m16T, m16, m32, m64, mlow, mupi, ones_head):
                link(pool.memset(m[:, :], 1.0))
            link(pool.memset(ones_all[:, :], 1.0 / D))
            link(pool.memset(ones_col[:, :], 1.0))
            blocks(m16T, 16)
            above(m16T, -1)
            blocks(m16, 16)
            below(m16, -1)
            blocks(m32, 32)
            blocks(m64, 64)
            blocks(mlow, 64)
            below(mlow, -1)
            blocks(mupi, 64)
            above(mupi, 0)
            blocks(ones_head, N)
            for m, size in ((m32, 32), (m64, 64)):
                v = m[:, :].rearrange("p (b h t) -> p b h t", h=2, t=size // 2)
                link(pool.memset(v[:, :, 1, :], 0.0))
                w = m[:, :].rearrange("p (b t) -> p b t", t=size)
                link(pool.affine_select(out=w, in_=w, compare_op=ALU.is_ge, fill=0.0, base=-(size // 2),
                                        pattern=[[-size, P // size], [0, size]], channel_multiplier=1))
            link(pool.memset(scanm[:, :], 1.0))
            link(pool.memset(scanm[:, :].rearrange("p (c t) -> p c t", t=C)[:, :, 0:1], 0.0))
            hm = derived[:, HM:HM + 2]
            link(pool.memset(hm, 1.0))
            link(pool.affine_select(out=hm[:, 0:1], in_=hm[:, 0:1], compare_op=ALU.is_ge, fill=0.0, base=N - 1,
                                    pattern=[[0, 1]], channel_multiplier=-1))
            link(pool.affine_select(out=hm[:, 1:2], in_=hm[:, 1:2], compare_op=ALU.is_ge, fill=0.0, base=-N,
                                    pattern=[[0, 1]], channel_multiplier=1), "consts_ready")

            def split_lo(k):
                pool.wait_ge(sem("hi_ready"), k + 1)
                link(pool.tensor_tensor(part_of(k, w_lo), part_of(k, w_raw), part_of(k, w_hi).bitcast(F32), ALU.subtract),
                     "lo_ready")

            for k in range(2):
                split_lo(k)
            pool.wait_ge(sem("h_ready"), KT)
            link(pool.memset(Vpad[:, :, :, :], 0.0))
            link(pool.memset(SApad[:, :, :], 0.0), "wkv_zeroed")
            split_lo(2)
            split_lo(3)

            def slot(i, s):
                name = STAGES[s]
                for e in range(2):
                    if 0 <= i < PAIRS and name == "Q1":
                        evacuated(pool, e, i, "Mab")
                        link(pool.tensor_tensor(A0[e][:, :, :], MAB[e][:, :, :], over_blocks(m16), ALU.mult), f"pooled{e}")
                    if 0 <= i < PAIRS and name == "U3":
                        pool.wait_ge(sem(f"multiplied{e}"), NS * i + STAGES.index("U2") + 1)
                        link(pool.tensor_tensor(A0[e][:, :, :], MAB[e][:, :, :], over_blocks(m32), ALU.mult), f"pooled{e}")
                    if 0 <= i < PAIRS and name == "Y1":
                        pool.wait_ge(sem(f"multiplied{e}"), NS * i + STAGES.index("X1") + 1)
                        link(pool.tensor_tensor(A0[e][:, :, :], MAB[e][:, :, :], over_blocks(m64), ALU.mult), f"pooled{e}")
                n = i + 1
                if n < PAIRS:
                    if s == 7:
                        pool.wait_ge(sem("scanned"), n + 1)
                        link(pool.tensor_tensor(sg[:, :], t3[:, :], sg[:, :], ALU.subtract), "before_sum")
                if s in (0, 6, 12) and 3 * n + 4 + s // 6 < FIRST_B:
                    split_lo(3 * n + 4 + s // 6)
                if i >= 1 and s == 16:
                    pool.wait_ge(sem("y_hi_ready"), i)
                    link(pool.tensor_tensor(y_lo[:, i - 1, :], SQ[:, :, :].rearrange("p j t -> p (j t)"), y_hi[:, i - 1, :].bitcast(F32), ALU.subtract), "y_lo_ready")

            per_slot(slot)
            for t in range(16):
                link(pool.memset(rec[:, t:t + 1], 1.0 / (t + 1)), "rec_ready")
            for k in range(FIRST_B, NALL):
                split_lo(k)

        @block.scalar
        def _(act):
            counts = {}

            def link(ins, name=None):
                key = name or "act_step"
                counts[key] = counts.get(key, 0) + 1
                ins.then_inc(sem(key), 1)
                act.wait_ge(sem(key), counts[key])

            def split_hi(k):
                slot = chunks[k][1]
                act.wait_ge(sem(f"w_in{slot}"), 16 * uses[k])
                if before[k] is not None:
                    act.wait_ge(sem("w_used"), before[k] + 1)
                link(act.activation(part_of(k, w_hi), part_of(k, w_raw), ACT.Copy), "hi_ready")

            def shift_first(k, dst, mucol, rows=P):
                act.wait_ge(sem("w_used"), k + 1)
                link(act.activation(dst[0:rows, :], G0[0:rows, :], ACT.Copy, scale=derived[0:rows, OMM + mucol:OMM + mucol + 1]), "kept")

            act.wait_ge(sem("c_cols"), 1)
            link(act.activation(derived[:, CS:CS + KT], derived[:, CCOL:CCOL + KT], ACT.Tanh, scale=0.5), "c_tanh")
            for k in range(2):
                split_hi(k)
            for f in range(KT):
                act.wait_ge(sem("h_f32"), f + 1)
                link(act.activation(h_hi[:, f, :], hf[f % 2][:, :], ACT.Copy), "h_hi_ready")
            for k, (dst, mucol, rows) in enumerate(((xwa, 24, P), (xg0, 25, P), (xg1, 26, DG1))):
                shift_first(k, dst, mucol, rows)
                if k < 2:
                    split_hi(2 + k)
                act.wait_ge(sem("shifted"), k + 1)
                if k == 0:
                    link(act.activation(xwa[0:DW, :], xwa[0:DW, :], ACT.Tanh), "lora_act")
                else:
                    link(act.activation(dst[0:rows, :], dst[0:rows, :], ACT.Tanh, scale=0.5), "lora_act")

            def take(e, i, s):
                name = STAGES[s]
                dst = {"Q1": A1, "Q2": A1T, "Q3": A0, "Q4": A0T, "Q5": A1, "X1": A1T, "Tr1": A1, "X2": A1T,
                       "Tr2": A1, "PT": PT}.get(name)
                act.wait_ge(sem(f"multiplied{e}"), NS * i + s + 1)
                src = blk(stage_bank(e, NS * i + s)[:, :])
                if name == "AHT":
                    rows = slice(N * e, N * e + N)
                    link(act.activation(AHT[rows, :, :], src[rows], ACT.Copy), f"taken_by_act{e}")
                else:
                    link(act.activation(dst[e][:, :, :], src, ACT.Copy), f"taken_by_act{e}")

            def slot(i, s):
                name = STAGES[s]
                n = i + 1
                if n < PAIRS and s in (6, 12, 18):
                    k = 3 + 3 * n + s // 6 - 1
                    shift_first(k, (xk, xr, xv)[s // 6 - 1], ((8, 0, 16)[s // 6 - 1]) + n)
                if i >= 1 and s < NCH:
                    z = s % 2
                    act.wait_ge(sem("sa_done"), NCH * (i - 1) + s + 1)
                    rows = slice(C * z, C * z + C)
                    link(act.activation(SApad[rows, z, :], CH[rows, 0:P], ACT.Copy), "sa_taken")
                if 0 <= i < PAIRS and name not in BY_DVE:
                    for e in range(2):
                        take(e, i, s)
                if s in (0, 6, 12) and 3 * n + 4 + s // 6 < FIRST_B:
                    split_hi(3 * n + 4 + s // 6)
                if (n, s) in POOLED_AT:
                    g = POOLED_AT.index((n, s))
                    act.wait_ge(sem("w_used"), NCHUNK + g + 1)
                    link(act.activation(UP[g][:, :], G0[:, :], ACT.Copy), "pool_in")
                if n < PAIRS:
                    if s == 4:
                        act.wait_ge(sem("g1_done"), g1_at[("decay", n)] + 1)
                        link(act.activation(sg[:, :], G1[:, :], ACT.Tanh, bias=der(HW0 + n), scale=0.5), "decay_taken")
                    if s == 5:
                        act.wait_ge(sem("g1_done"), g1_at[("aaa", n)] + 1)
                        link(act.activation(aa[:, :], G1[:, :], ACT.Tanh, bias=der(HA0 + n), scale=0.5), "aaa_taken")
                    if s == 7:
                        act.wait_ge(sem("shifted"), 3 + 3 * n + 1)
                        link(act.activation(t1[:, :], xk[:, :], ACT.Square, scale=col(rows1["k_k"] + n)), "squared")
                    if s == 8:
                        act.wait_ge(sem("g1_done"), g1_at[("norm", n)] + 1)
                        link(act.activation(t1[:, :], G1[:, :], ACT.Sqrt), "norm_taken")
                    if s == 10:
                        act.wait_ge(sem("before_sum"), n + 1)
                        link(act.activation(sg[:, :], sg[:, :], ACT.Exp, scale=-EXPM))
                        link(act.activation(t4[:, :], t3[:, :], ACT.Exp, scale=-EXPM))
                        link(act.activation(t3[:, :], t3[:, :], ACT.Exp, scale=EXPM), "exps")
                if 0 <= i < PAIRS and s == 8:
                    if i >= 1:
                        act.wait_ge(sem("so_done"), NCH * i)
                        act.wait_ge(sem("s_taken"), NCH * i)
                    act.wait_ge(sem("prepared"), i + 1)
                    link(act.activation(Rc[:, :], Rf[:, :], ACT.Copy), "carried")
                    link(act.activation(DCc[:, :], DC[:, :], ACT.Copy), "carried")
                if 0 <= i < PAIRS and s == 15:
                    act.wait_ge(sem("g1_done"), g1_at[("gate", i)] + 1)
                    if i >= 1:
                        act.wait_ge(sem("y_ready"), i)
                    link(act.activation(gate[:, :], G1[:, :], ACT.Copy), "gate_taken")
                    link(act.activation(bonus_c[:, :], bonus[:, :], ACT.Copy), "bonus_carried")
                if 0 <= i < PAIRS and s in (9, 10, 11):
                    job, dst = (("tokA", Atok), ("tokB", Btok), ("tokK", Ktok))[s - 9]
                    act.wait_ge(sem("g1_done"), g1_at[(job, i)] + 1)
                    link(act.activation(dst[:, :, :], blk(G1[:, :]), ACT.Copy), "tok_taken")
                if 0 <= i < PAIRS and s == 12:
                    act.wait_ge(sem("g1_done"), g1_at[("tokV", i)] + 1)
                    for z in range(2):
                        rows = slice(C * z, C * z + C)
                        link(act.activation(Vpad[rows, z, :, :], blk(G1[:, :])[rows], ACT.Copy), "v_taken")
                if i >= 1:
                    if s == 9:
                        act.wait_ge(sem("centred"), i)
                        if i >= 2:
                            act.wait_ge(sem("y_lo_ready"), i - 1)
                        link(act.activation(SQ[:, :, :], OC[:, :, :], ACT.Square), "o_squared")
                    if s == 10:
                        act.wait_ge(sem("o_var"), i)
                        link(act.activation(gn[:, 2, :], gn[:, 1, :], ACT.Sqrt), "o_std")
                    if s == 13:
                        act.wait_ge(sem("g1_done"), g1_at[("outT", i - 1)] + 1)
                        link(act.activation(SQ[:, :, :], blk(G1[:, :]), ACT.Identity, scale=col(rows1["gn_g"] + i - 1),
                                            bias=params[:, P + rows2["gn_b"] + i - 1:P + rows2["gn_b"] + i]), "out_taken")
                    if s == 15:
                        act.wait_ge(sem("y_ready"), i)
                        link(act.activation(y_hi[:, i - 1, :], SQ[:, :, :].rearrange("p j t -> p (j t)"), ACT.Copy), "y_hi_ready")

            per_slot(slot)
            for k in range(FIRST_B, FIRST_B + 3):
                split_hi(k)

            for n in range(KT):
                act.wait_ge(sem("x_turned2"), n + 1)
                link(act.activation(res[:, n, :], bank[4 + n % 2][:, :], ACT.Copy, scale=ALPHA), "res_ready")

            def gate_block(n):
                k = K_GATE(n)
                for m in range(2):
                    split_hi(k + m + 3)
                    act.wait_ge(sem("w_used"), k + m + 1)
                    if n >= 1:
                        act.wait_ge(sem("mixed"), n)
                    link(act.activation((f1, f2)[m][:, :], bank[m][:, :], ACT.Sigmoid), "gated")
                split_hi(k + 5)
                if n == 0:
                    for g in range(GP):
                        act.wait_ge(sem("pool_mixed"), g + 1)
                        if g >= 1:
                            act.wait_ge(sem("mp_ready"), g)
                        link(act.activation(lnv[:, :], bank[6 + g % 2][:, :], ACT.Copy,
                                            scale=params[:, P + 8 + g:P + 9 + g]), "pool_scaled")
                        link(act.activation(mp_hi[:, g, :], lnv[:, :], ACT.Copy), "mp_hi_ready")
                split_hi(k + 6)
                act.wait_ge(sem("mix_sum"), n + 1)
                link(act.activation(mix_hi[:, n, :], f3[:, :], ACT.Copy), "mixed_hi")

            for n in range(KT):
                gate_block(n)
            for n in range(KT):
                split_hi(K_OUT + n + 3)
            for f in range(KT):
                act.wait_ge(sem("ln1_centred"), f + 1)
                if f >= 2:
                    act.wait_ge(sem("ln1_var"), f - 1)
                link(act.activation((f1, f2)[f % 2][:, :], res[:, f, :], ACT.Square), "ln1_squared")
            act.wait_ge(sem("ln1_eps"), 1)
            link(act.activation(lnv[:, :], lnv[:, :], ACT.Sqrt), "ln1_std")
            for f in range(KT):
                act.wait_ge(sem("h2_f32"), f + 1)
                link(act.activation(h_hi[:, f, :], (f1, f2)[f % 2][:, :], ACT.Copy), "h2_hi")
                act.wait_ge(sem("h2_normed"), f + 1)
                link(act.activation(res[:, f, :], res[:, f, :], ACT.Identity, scale=small[:, f:f + 1], bias=small[:, 8 + f:9 + f]),
                     "res_ready")
            for q in range(NQ):
                hid = (y_hi, mix_hi)[q % 2]
                for n in range(KT):
                    k, m = K_FF + 2 * KT * q + n, KT * q + n
                    if k + 3 < NALL:
                        split_hi(k + 3)
                    act.wait_ge(sem("w_used"), k + 1)
                    if m >= 2:
                        act.wait_ge(sem("hidden"), m - 1)
                    link(act.activation((f1, f2)[m % 2][:, :], bank[k % 4][:, :], ACT.Relu), "relu")
                    link(act.activation(hid[:, n, :], (f1, f2)[m % 2][:, :], ACT.Square), "hidden_hi")
                for n in range(KT):
                    k = K_FF + 2 * KT * q + KT + n
                    if k + 3 < NALL:
                        split_hi(k + 3)
                    if q == NQ - 1:
                        act.wait_ge(sem("turned_back"), n + 1)
                        link(act.activation(xt2[:, :, n * P:(n + 1) * P], blk(bank[4 + n % 2][:, :]), ACT.Copy), "out_tokens")
            act.wait_ge(sem("ln2_eps"), 1)
            link(act.activation(small[:, 32:36], small[:, 28:32], ACT.Sqrt), "ln2_std")
            for j in range(TB):
                act.wait_ge(sem("ln2_cols"), 1)
                link(act.activation(xt2[:, j, :], xt2[:, j, :], ACT.Identity, scale=small[:, 36 + j:37 + j], bias=small[:, 40 + j:41 + j]),
                     "ln2_normed")

        @block.vector
        def _(dve):
            counts = {}

            def link(ins, name=None):
                key = name or "dve_step"
                counts[key] = counts.get(key, 0) + 1
                ins.then_inc(sem(key), 1)
                dve.wait_ge(sem(key), counts[key])

            dve.wait_ge(sem("param_cols"), 1)
            link(dve.tensor_copy(params[:, 0:P], bank[0][:, 0:P]))
            link(dve.tensor_copy(params[:, P:2 * P], bank[0][:, P:2 * P]))
            link(dve.tensor_copy(derived[:, CCOL:CCOL + KT], bank[0][:, 2 * P:2 * P + KT]), "c_cols")
            link(dve.tensor_scalar(derived[:, OMM:OMM + 26], params[:, 48:74], -1.0, 1.0, ALU.mult, ALU.add))
            link(dve.tensor_scalar(der(OMM + 26), params[:, P + 44:P + 45], -1.0, 1.0, ALU.mult, ALU.add))
            link(dve.tensor_scalar(derived[:, OMKA:OMKA + 8], params[:, 98:106], -1.0, 1.0, ALU.mult, ALU.add))
            link(dve.tensor_scalar(derived[:, HW0:HW0 + 8], params[:, 74:82], 0.5, None, ALU.mult))
            link(dve.tensor_scalar(derived[:, HA0:HA0 + 8], params[:, 82:90], 0.5, None, ALU.mult))
            dve.wait_ge(sem("c_tanh"), 1)
            link(dve.tensor_scalar(derived[:, CS:CS + KT], derived[:, CS:CS + KT], 0.5, 0.5, ALU.mult, ALU.add))
            link(dve.tensor_tensor(derived[:, CS:CS + KT], derived[:, CS:CS + KT], derived[:, CCOL:CCOL + KT], ALU.mult))
            for q in range(2 * KT):
                kt, half = q % KT, q // KT
                dve.wait_ge(sem(f"ada_in{q % 4}"), 16 * (q // 4 + 1))
                if kt == 0:
                    link(dve.tensor_scalar(acc[:, half, :], ada[q % 4][:, :], der(CS), None, ALU.mult), "ada_used")
                else:
                    link(dve.scalar_tensor_tensor(out=acc[:, half, :], in0=ada[q % 4][:, :], scalar=der(CS + kt),
                                                  in1=acc[:, half, :], op0=ALU.mult, op1=ALU.add), "ada_used")
            dve.wait_ge(sem("mod_done"), 1)
            link(dve.tensor_tensor(mod[:, 8:16], bank[1][:, 0:8], params[:, 8:16], ALU.add))
            link(dve.tensor_scalar(mod[:, 8:16], mod[:, 8:16], 1.0, None, ALU.add))
            link(dve.tensor_tensor(mod[:, 0:8], bank[1][:, 8:16], params[:, 0:8], ALU.add))
            for f in range(KT):
                dve.wait_ge(sem("x_turned"), f + 1)
                if f >= 2:
                    dve.wait_ge(sem("h_hi_ready"), f - 1)
                link(dve.tensor_scalar(hf[f % 2][:, :], bank[2 + f % 4][:, :], mod[:, 8 + f:9 + f], mod[:, f:f + 1], ALU.mult, ALU.add), "h_f32")
                dve.wait_ge(sem("h_hi_ready"), f + 1)
                link(dve.tensor_tensor(h_lo[:, f, :], hf[f % 2][:, :], h_hi[:, f, :].bitcast(F32), ALU.subtract), "h_ready")

            def shift_rest(k, dst, mu_ap, rows=P):
                dve.wait_ge(sem("kept"), k + 1)
                link(dve.scalar_tensor_tensor(out=dst[0:rows, 1:S], in0=G0[0:rows, 0:S - 1], scalar=mu_ap,
                                              in1=dst[0:rows, 1:S], op0=ALU.mult, op1=ALU.add), "shifted")

            for k, (dst, mu_ap, rows) in enumerate(((xwa, col(48 + 24), P), (xg0, col(48 + 25), P),
                                                    (xg1, params[0:DG1, P + 44:P + 45], DG1))):
                shift_rest(k, dst, mu_ap, rows)
                dve.wait_ge(sem("lora_act"), k + 1)
                if k:
                    link(dve.tensor_scalar(dst[0:rows, :], dst[0:rows, :], 0.5, 0.5, ALU.mult, ALU.add), "lora_ready")
                else:
                    link(dve.memset(gn[:, :, :], 0.0), "lora_ready")

            def take(e, i, s):
                name = STAGES[s]
                dve.wait_ge(sem(f"multiplied{e}"), NS * i + s + 1)
                src = blk(stage_bank(e, NS * i + s)[:, :])
                key = f"taken_by_dve{e}"
                if name == "MabT":
                    link(dve.tensor_tensor(A0T[e][:, :, :], src, over_blocks(m16T), ALU.mult))
                    link(dve.tensor_tensor(TT[e][:, :, :], A0T[e][:, :, :], over_blocks(ident), ALU.add), key)
                elif name in ("Mab", "Mak"):
                    link(dve.tensor_tensor((MAB if name == "Mab" else MAK)[e][:, :, :], src, over_blocks(mlow), ALU.mult), key)
                elif name in ("MrbT", "MrkT"):
                    link(dve.tensor_tensor((MRB if name == "MrbT" else MRK)[e][:, :, :], src, over_blocks(mupi), ALU.mult), key)
                else:
                    link(dve.tensor_tensor(TT[e][:, :, :], src, TT[e][:, :, :], ALU.add), key)

            def slot(i, s):
                name = STAGES[s]
                n = i + 1
                if n < PAIRS and s in (6, 12, 18):
                    k = 3 + 3 * n + s // 6 - 1
                    shift_rest(k, (xk, xr, xv)[s // 6 - 1], col(48 + (8, 0, 16)[s // 6 - 1] + n))
                if 0 <= i < PAIRS and name in BY_DVE:
                    for e in range(2):
                        take(e, i, s)
                if i >= 1 and s < NCH:
                    dve.wait_ge(sem("so_done"), NCH * (i - 1) + s + 1)
                    link(dve.tensor_tensor(Stmp[:, :], CH[:, 2 * P:3 * P], Sbd[:, :], ALU.add))
                    link(dve.scalar_tensor_tensor(out=Sbd[:, :], in0=Stmp[:, :], scalar=DCc[:, s:s + 1], in1=ones_head[:, :],
                                                  op0=ALU.mult, op1=ALU.mult), "s_taken")
                if n < PAIRS:
                    if s == 5:
                        dve.wait_ge(sem("decay_taken"), n + 1)
                        link(dve.tensor_scalar(sg[:, :], sg[:, :], 0.5, 0.5, ALU.mult, ALU.add))
                        link(dve.tensor_tensor_scan(t3[:, :], scanm[:, :], sg[:, :], 0.0, ALU.mult, ALU.add), "scanned")
                    if s == 6:
                        dve.wait_ge(sem("aaa_taken"), n + 1)
                        link(dve.tensor_scalar(aa[:, :], aa[:, :], 0.5, 0.5, ALU.mult, ALU.add))
                    if s == 9:
                        dve.wait_ge(sem("norm_taken"), n + 1)
                        link(dve.tensor_scalar(t1[:, :], t1[:, :], 1e-12, None, ALU.max))
                    if 9 <= s <= 12:
                        qq = slice((s - 9) * P, (s - 8) * P)
                        link(dve.reciprocal(t2[:, qq], t1[:, qq]))
                    if s == 13:
                        link(dve.scalar_tensor_tensor(out=t1[:, :], in0=xk[:, :], scalar=col(90 + n), in1=t2[:, :], op0=ALU.mult, op1=ALU.mult))
                        link(dve.tensor_scalar(t2[:, :], aa[:, :], col(98 + n), der(OMKA + n), ALU.mult, ALU.add))
                    if s == 14:
                        link(dve.tensor_tensor(t2[:, :], xk[:, :], t2[:, :], ALU.mult))
                        link(dve.scalar_tensor_tensor(out=xk[:, :], in0=xr[:, :], scalar=col(106 + n), in1=t2[:, :], op0=ALU.mult, op1=ALU.mult), "rk_ready")
                    if s == 15:
                        dve.wait_ge(sem("exps"), n + 1)
                        link(dve.scalar_tensor_tensor(out=At[:, :], in0=t1[:, :], scalar=-1.0, in1=sg[:, :], op0=ALU.mult, op1=ALU.mult))
                        for e in range(2):
                            link(dve.tensor_scalar(Apad[:, e, :], At[:, :], der(HM + e), None, ALU.mult))
                    if s == 16:
                        if n >= 1:
                            dve.wait_ge(sem("carried"), 2 * n)
                        link(dve.tensor_tensor(Rf[:, :], xr[:, :], t4[:, :], ALU.mult))
                        link(dve.tensor_copy(DC[:, :], t4[:, :].rearrange("p (c t) -> p c t", t=C)[:, :, C - 1]))
                        for e in range(2):
                            link(dve.tensor_scalar(Rpad[:, e, :], Rf[:, :], der(HM + e), None, ALU.mult))
                    if s == 17:
                        link(dve.tensor_tensor(aa[:, :], t1[:, :], aa[:, :], ALU.mult))
                        link(dve.tensor_tensor(Bt[:, :], aa[:, :], t3[:, :], ALU.mult))
                    if s == 18:
                        dve.wait_ge(sem("g1_done"), g1_at[("bonus", n)] + 1)
                        if n >= 1:
                            dve.wait_ge(sem("bonus_carried"), n)
                        link(dve.tensor_tensor(bonus[:, :], G1[:, :], xv[:, :], ALU.mult), "bonus_taken")
                    if s == 19:
                        link(dve.tensor_tensor(Kt[:, :], t2[:, :], t3[:, :], ALU.mult), "prepared")
                if i >= 1:
                    g8 = lambda ap: ap.rearrange("p j (e v) -> p (j e) v", e=2)
                    ob = OB[:, :].rearrange("p (g v) -> p g v", v=N)
                    if s == 8:
                        link(dve.tensor_reduce(gn[:, 0, :], ob, AX_X, ALU.add))
                        link(dve.tensor_scalar(gn[:, 0, :], gn[:, 0, :], 1.0 / N, None, ALU.mult))
                        link(dve.tensor_tensor(OC[:, :, :].rearrange("p j (e v) -> p (j e) v", e=2), ob,
                                               gn[:, 0, :].unsqueeze(2).to_broadcast([P, 8, N]), ALU.subtract), "centred")
                    if s == 9:
                        dve.wait_ge(sem("o_squared"), i)
                        link(dve.tensor_reduce(gn[:, 1, :], SQ[:, :, :].rearrange("p j (e v) -> p (j e) v", e=2), AX_X, ALU.add))
                        link(dve.tensor_scalar(gn[:, 1, :], gn[:, 1, :], 1.0 / N, GN_EPS, ALU.mult, ALU.add), "o_var")
                    if s == 11:
                        dve.wait_ge(sem("o_std"), i)
                        link(dve.reciprocal(gn[:, 3, :], gn[:, 2, :]))
                        oc = OC[:, :, :].rearrange("p j (e v) -> p (j e) v", e=2)
                        link(dve.tensor_tensor(oc, oc, gn[:, 3, :].unsqueeze(2).to_broadcast([P, 8, N]), ALU.mult), "o_normed")
                    if s == 14:
                        dve.wait_ge(sem("out_taken"), i)
                        sq = SQ[:, :, :].rearrange("p j t -> p (j t)")
                        link(dve.tensor_tensor(sq, sq, bonus_c[:, :], ALU.add))
                        link(dve.tensor_tensor(sq, sq, gate[:, :], ALU.mult), "y_ready")
                if s == 20 and i >= 0 and i < PAIRS:
                    link(dve.memset(Sbd[:, :], 0.0), "s_zero")

            per_slot(slot)
            def mod_section(m):
                dve.wait_ge(sem("ada_turned"), m + 1)
                for half in range(2):
                    link(dve.tensor_reduce(mod[:, 16 + 8 * m + 4 * half:20 + 8 * m + 4 * half], blk(bank[6 + half][:, :]), AX_X, ALU.add))
                link(dve.tensor_tensor(mod[:, 16 + 8 * m:24 + 8 * m], mod[:, 16 + 8 * m:24 + 8 * m],
                                       params[:, 16 + 8 * m:24 + 8 * m], ALU.add), "mod2")

            dve.wait_ge(sem("rec_ready"), 16)
            for g in range(GP):
                w = 2 << g
                dve.wait_ge(sem("pool_in"), g + 1)
                u, cur, nxt = UP[g], acc2[:, 0:S], acc2[:, S:2 * S]
                link(dve.tensor_copy(cur[:, 0:1], u[:, 0:1]))
                link(dve.tensor_tensor(cur[:, 1:S], u[:, 1:S], u[:, 0:S - 1], ALU.add))
                d = 2
                while d < w:
                    link(dve.tensor_copy(nxt[:, 0:d], cur[:, 0:d]))
                    link(dve.tensor_tensor(nxt[:, d:S], cur[:, d:S], cur[:, 0:S - d], ALU.add))
                    cur, nxt, d = nxt, cur, 2 * d
                link(dve.tensor_tensor(cur[:, 0:w], cur[:, 0:w], rec[:, 0:w], ALU.mult))
                link(dve.tensor_tensor(u[:, 0:w], cur[:, 0:w], u[:, 0:w], ALU.subtract))
                link(dve.scalar_tensor_tensor(out=u[:, w:S], in0=cur[:, w:S], scalar=1.0 / w, in1=u[:, w:S],
                                              op0=ALU.mult, op1=ALU.subtract), "pooled_up")

            def ada_tile(tile):
                kt = tile % KT
                if kt == 0 and tile:
                    dve.wait_ge(sem("ada_turned"), tile // KT)
                for half in range(2):
                    cols = slice(half * S, (half + 1) * S)
                    dve.wait_ge(sem(f"ada2_in{half}"), 16 * (tile + 1))
                    if kt == 0:
                        link(dve.tensor_scalar(acc2[:, cols], ada2[:, cols], der(CS), None, ALU.mult), "ada2_used")
                    else:
                        link(dve.scalar_tensor_tensor(out=acc2[:, cols], in0=ada2[:, cols], scalar=der(CS + kt), in1=acc2[:, cols],
                                                      op0=ALU.mult, op1=ALU.add), "ada2_used")

            for n in range(KT):
                k = K_GATE(n)
                if n == 0:
                    for g in range(GP):
                        dve.wait_ge(sem("mp_hi_ready"), g + 1)
                        link(dve.tensor_tensor(mp_lo[:, g, :], lnv[:, :], mp_hi[:, g, :].bitcast(F32), ALU.subtract), "mp_ready")
                if n >= 1:
                    ada_tile(4 * n - 4)
                    ada_tile(4 * n - 3)
                dve.wait_ge(sem("gated"), 2 * n + 2)
                dve.wait_ge(sem("w_used"), k + 3)
                link(dve.tensor_tensor(f2[:, :], f2[:, :], bank[2][:, :], ALU.mult), "ru_taken")
                if n >= 1:
                    ada_tile(4 * n - 2)
                dve.wait_ge(sem("w_used"), k + 4)
                link(dve.tensor_tensor(f1[:, :], f1[:, :], bank[3][:, :], ALU.mult), "pu_taken")
                link(dve.tensor_tensor(f3[:, :], f1[:, :], f2[:, :], ALU.add), "mix_sum")
                if n >= 1:
                    ada_tile(4 * n - 1)
                    if n % 2 == 0:
                        mod_section(n // 2 - 1)
                dve.wait_ge(sem("mixed_hi"), n + 1)
                link(dve.tensor_tensor(mix_lo[:, n, :], f3[:, :], mix_hi[:, n, :].bitcast(F32), ALU.subtract), "mixed")
            for na in range(4 * KT - 4, 4 * KT):
                ada_tile(na)
            mod_section(3)
            link(dve.tensor_scalar(mod[:, 16:24], mod[:, 16:24], 1.0, None, ALU.add))
            link(dve.tensor_scalar(mod[:, 40:48], mod[:, 40:48], 1.0, None, ALU.add))
            link(dve.tensor_scalar(mod[:, 32:40], mod[:, 32:40], 1.0, None, ALU.add))
            link(dve.tensor_scalar(small[:, 0:8], params[:, P + 12:P + 20], ALPHA, None, ALU.mult))
            link(dve.tensor_scalar(small[:, 8:16], params[:, P + 20:P + 28], ALPHA, None, ALU.mult))
            link(dve.tensor_tensor(small[:, 16:24], params[:, P + 20:P + 28], mod[:, 32:40], ALU.mult))
            link(dve.tensor_tensor(mod[:, 24:32], small[:, 16:24], mod[:, 24:32], ALU.add))
            link(dve.tensor_tensor(mod[:, 32:40], params[:, P + 12:P + 20], mod[:, 32:40], ALU.mult))
            for n in range(KT):
                dve.wait_ge(sem("w_used"), K_OUT + n + 1)
                dve.wait_ge(sem("res_ready"), n + 1)
                link(dve.scalar_tensor_tensor(out=res[:, n, :], in0=bank[(K_OUT + n) % 4][:, :], scalar=mod[:, 16 + n:17 + n],
                                              in1=res[:, n, :], op0=ALU.mult, op1=ALU.add), "out_taken2")
            dve.wait_ge(sem("ln1_mean"), KT)
            for f in range(KT):
                link(dve.tensor_tensor(res[:, f, :], res[:, f, :], bank[4][:, :], ALU.subtract), "ln1_centred")
            dve.wait_ge(sem("ln1_var"), KT)
            link(dve.tensor_scalar(lnv[:, :], bank[5][:, :], LN_EPS, None, ALU.add), "ln1_eps")
            dve.wait_ge(sem("ln1_std"), 1)
            link(dve.reciprocal(f3[:, :], lnv[:, :]))
            for f in range(KT):
                link(dve.tensor_tensor(res[:, f, :], res[:, f, :], f3[:, :], ALU.mult), "h2_pre")
                if f >= 2:
                    dve.wait_ge(sem("h2_hi"), f - 1)
                hb = (f1, f2)[f % 2]
                link(dve.tensor_scalar(hb[:, :], res[:, f, :], mod[:, 32 + f:33 + f], mod[:, 24 + f:25 + f], ALU.mult, ALU.add), "h2_f32")
                link(dve.memset(small[:, 60:61], 0.0), "h2_normed")
                dve.wait_ge(sem("h2_hi"), f + 1)
                link(dve.tensor_tensor(h_lo[:, f, :], hb[:, :], h_hi[:, f, :].bitcast(F32), ALU.subtract), "h2_ready")

            def statistics(half):
                for j in range(TB):
                    link(dve.bn_stats(stat[:, 2 * j + half, :], xt2[:, j, half * S:(half + 1) * S]))

            for q in range(NQ):
                hh, hl = ((y_hi, y_lo), (mix_hi, mix_lo))[q % 2]
                for n in range(KT):
                    m = KT * q + n
                    dve.wait_ge(sem("relu"), m + 1)
                    r = (f1, f2)[m % 2]
                    link(dve.tensor_tensor(f3[:, :], r[:, :], r[:, :], ALU.mult))
                    dve.wait_ge(sem("hidden_hi"), m + 1)
                    link(dve.tensor_tensor(hl[:, n, :], f3[:, :], hh[:, n, :].bitcast(F32), ALU.subtract), "hidden")
                for n in range(KT):
                    k = K_FF + 2 * KT * q + KT + n
                    dve.wait_ge(sem("w_used"), k + 1)
                    dve.wait_ge(sem("res_ready"), KT + n + 1)
                    link(dve.scalar_tensor_tensor(out=res[:, n, :], in0=bank[k % 4][:, :], scalar=mod[:, 40 + n:41 + n],
                                                  in1=res[:, n, :], op0=ALU.mult, op1=ALU.add), "ff_taken")
                    if q == NQ - 1 and n == KT - 2:
                        dve.wait_ge(sem("out_tokens"), KT // 2)
                        statistics(0)
            dve.wait_ge(sem("out_tokens"), KT)
            statistics(1)
            for j in range(TB):
                link(dve.bn_aggr(small[:, 20 + 2 * j:22 + 2 * j], stat[:, 2 * j:2 * j + 2, :]))
            mv = small[:, 20:28].rearrange("p (j two) -> p j two", two=2)
            link(dve.tensor_scalar(small[:, 28:32], mv[:, :, 1], LN_EPS, None, ALU.add), "ln2_eps")
            dve.wait_ge(sem("ln2_std"), 1)
            link(dve.reciprocal(small[:, 36:40], small[:, 32:36]))
            link(dve.scalar_tensor_tensor(out=small[:, 40:44], in0=mv[:, :, 0], scalar=-1.0, in1=small[:, 36:40],
                                          op0=ALU.mult, op1=ALU.mult), "ln2_cols")
            dve.wait_ge(sem("ln2_in"), 32)
            for j in range(TB):
                dve.wait_ge(sem("ln2_normed"), j + 1)
                link(dve.tensor_tensor(xt2[:, j, :], xt2[:, j, :], acc2[:, :], ALU.mult))
                link(dve.tensor_tensor(xt2[:, j, :], xt2[:, j, :], ada2[:, :], ALU.add), "out_ready")

        @block.tensor
        def _(pe):
            pe.wait_ge(sem("ident_ready"), 1)
            pe.wait_ge(sem("params_in"), 16 * 16)
            for tab in range(2):
                pe.transpose(bank[0][:, tab * P:(tab + 1) * P], ptab[:, tab, :], ident[:, :])
            pe.transpose(bank[0][:, 2 * P:2 * P + KT], crow[:, :], ident[0:KT, 0:KT]).then_inc(sem("param_cols"), 1)
            pe.wait_ge(sem("consts_ready"), 1)

            def turn_x(f):
                if f >= 4:
                    pe.wait_ge(sem("h_f32"), f - 3)
                for j in range(TB):
                    mm = pe.transpose(bank[2 + f % 4][:, j * P:(j + 1) * P], xtok[:, j, f * P:(f + 1) * P], ident[:, :])
                mm.then_inc(sem("x_turned"), 1)

            pe.wait_ge(sem("x_in"), 16 * TB)
            for f in range(4):
                turn_x(f)
            for half in range(2):
                pe.wait_ge(sem("ada_used"), KT * (half + 1))
                for f in range(KT):
                    mm = pe.matmul(bank[1][:, 8 * half + f:8 * half + f + 1], acc[:, half, f * P:(f + 1) * P],
                                   ones_col[:, :], start=True, stop=True)
            mm.then_inc(sem("mod_done"), 1)
            for f in range(4, KT):
                turn_x(f)

            def gemm(k, kts):
                width = chunk_cols[k][1]
                if 0 in kts:
                    pe.wait_ge(sem("lo_ready"), k + 1)
                    if k >= 1:
                        pe.wait_ge(sem("shifted"), k)
                for kt in kts:
                    terms = [(w_hi, h_hi), (w_hi, h_lo), (w_lo, h_hi)]
                    for m, (w, hx) in enumerate(terms):
                        mm = pe.matmul(G0[0:width, :], w[k % RING][:, kt, 0:width], hx[:, kt, :],
                                       start=(kt == 0 and m == 0), stop=(kt == KT - 1 and m == 2))
                if KT - 1 in kts:
                    mm.then_inc(sem("w_used"), 1)

            G1_TAKEN = {"decay": ("decay_taken", 1), "aaa": ("aaa_taken", 1), "norm": ("norm_taken", 1), "tokA": ("tok_taken", 3, 1),
                        "tokB": ("tok_taken", 3, 2), "tokK": ("tok_taken", 3, 3), "tokV": ("v_taken", 2, 2), "outT": ("out_taken", 1),
                        "gate": ("gate_taken", 1), "bonus": ("bonus_taken", 1)}

            def g1_free(job, n):
                at = g1_at[(job, n)]
                if at:
                    before, m = g1_jobs[at - 1]
                    name, per, *k = G1_TAKEN[before]
                    pe.wait_ge(sem(name), per * m + (k[0] if k else 1))

            pe.wait_ge(sem("h_ready"), KT)
            for k in range(3):
                gemm(k, range(KT))

            def stage(e, i, s):
                name = STAGES[s]
                if s >= 2:
                    evacuated(pe, e, i, STAGES[s - 2])
                elif i >= 1:
                    evacuated(pe, e, i - 1, STAGES[NS + s - 2])
                dep = {"Q3": ["Q2"], "Q4": [], "Q5": ["Q4"], "U1": ["MabT"], "U2": ["U1"], "U3": ["U2", "Q5"], "X1": ["U3"],
                       "Tr1": [], "Y1": ["Tr1"], "X2": ["Y1"], "Tr2": [], "Y2": ["Tr2"], "PT": ["Y2"], "AHT": []}
                for d in dep.get(name, []):
                    evacuated(pe, e, i, d)
                if name == "MabT":
                    pe.wait_ge(sem("prepared"), i + 1)
                if name == "Q1":
                    pe.wait_ge(sem(f"pooled{e}"), 3 * i + 1)
                if name == "X1":
                    pe.wait_ge(sem(f"pooled{e}"), 3 * i + 2)
                if name == "X2":
                    pe.wait_ge(sem(f"pooled{e}"), 3 * i + 3)
                if name == "AHT":
                    pe.wait_ge(sem("tok_taken"), 3 * i + 1)
                b = stage_bank(e, NS * i + s)
                for j in range(TB):
                    tb = slice(j * P, (j + 1) * P)
                    o = b[:, tb]
                    if name in ("Tr1", "Tr2"):
                        mm = pe.transpose(o, TT[e][:, j, :], ident[:, :])
                        continue
                    if name == "AHT":
                        o = b[N * e:N * e + N, tb]
                    lhs, rhs = {
                        "MabT": (Bt[:, tb], Apad[:, e, tb]), "Mab": (Apad[:, e, tb], Bt[:, tb]), "Mak": (Apad[:, e, tb], Kt[:, tb]),
                        "MrbT": (Bt[:, tb], Rpad[:, e, tb]), "MrkT": (Kt[:, tb], Rpad[:, e, tb]),
                        "Q1": (A0T[e][:, j, :], A0[e][:, j, :]), "Q2": (A0[e][:, j, :], A0T[e][:, j, :]),
                        "Q3": (A1T[e][:, j, :], A1[e][:, j, :]), "Q4": (A1[e][:, j, :], A1T[e][:, j, :]),
                        "U1": (A1[e][:, j, :], TT[e][:, j, :]), "Q5": (A0T[e][:, j, :], A0[e][:, j, :]),
                        "U2": (A0[e][:, j, :], TT[e][:, j, :]), "U3": (A1[e][:, j, :], TT[e][:, j, :]),
                        "X1": (A0[e][:, j, :], TT[e][:, j, :]), "X2": (A0[e][:, j, :], TT[e][:, j, :]),
                        "Y1": (A1[e][:, j, :], A1T[e][:, j, :]), "Y2": (A1[e][:, j, :], A1T[e][:, j, :]),
                        "PT": (MAK[e][:, j, :], TT[e][:, j, :]), "AHT": (Atok[:, j, N * e:N * e + N], TT[e][:, j, :]),
                    }[name]
                    mm = pe.matmul(o, lhs, rhs, start=True, stop=True)
                mm.then_inc(sem(f"multiplied{e}"), 1)

            def chain_sa(i, c):
                j, z = c // 2, c % 2
                rows, cols = slice(C * z, C * z + C), slice(c * C, (c + 1) * C)
                if c == 0:
                    pe.wait_ge(sem("s_zero"), i + 1)
                    evacuated(pe, 0, i, "AHT")
                    evacuated(pe, 1, i, "AHT")
                    pe.wait_ge(sem("v_taken"), 2 * i + 2)
                if NCH * i + c:
                    pe.wait_ge(sem("s_taken"), NCH * i + c)
                pe.matmul(CH[rows, 0:P], AHT[:, j, C * z:C * z + C], Sbd[:, :], start=True, stop=False, skip_group_check=True)
                for e in range(2):
                    mm = pe.matmul(CH[rows, N * e:N * e + N], PT[e][:, j, C * z:C * z + C], Vpad[:, z, j, N * e:N * e + N],
                                   start=False, stop=(e == 1), skip_group_check=True)
                mm.then_inc(sem("sa_done"), 1)

            def chain_so(i, c):
                j, z = c // 2, c % 2
                rows, cols = slice(C * z, C * z + C), slice(c * C, (c + 1) * C)
                tb = slice(j * P, (j + 1) * P)
                pe.wait_ge(sem("sa_taken"), NCH * i + c + 1)
                pe.matmul(CH[:, 2 * P:3 * P], Btok[:, j, :], SApad[:, z, :], start=True, stop=False, skip_group_check=True)
                pe.matmul(CH[:, 2 * P:3 * P], Ktok[:, j, :], Vpad[:, z, j, :], start=False, stop=True, skip_group_check=True)
                if c == 0 and i >= 1:
                    pe.wait_ge(sem("centred"), i)
                pe.matmul(OB[rows, tb], Rc[:, cols], Sbd[:, :], start=True, stop=False, skip_group_check=True)
                for e in range(2):
                    o = OB[rows, j * P + N * e:j * P + N * e + N]
                    pe.matmul(o, MRB[e][:, j, C * z:C * z + C], SApad[:, z, N * e:N * e + N], start=False, stop=False, skip_group_check=True)
                    mm = pe.matmul(o, MRK[e][:, j, C * z:C * z + C], Vpad[:, z, j, N * e:N * e + N], start=False, stop=(e == 1), skip_group_check=True)
                mm.then_inc(sem("so_done"), 1)

            def slot(i, s):
                n = i + 1
                if i == 0 and s == 0:
                    pe.wait_ge(sem("wkv_zeroed"), 1)
                if i >= 1 and s < NCH:
                    chain_sa(i - 1, s)
                if 0 <= i < PAIRS:
                    for e in range(2):
                        stage(e, i, s)
                if i >= 1 and s < NCH:
                    chain_so(i - 1, s)
                if n < PAIRS:
                    if s == 4:
                        pe.wait_ge(sem("lup_in"), 32 * (n + 1))
                        pe.wait_ge(sem("lora_ready"), 3)
                        g1_free("decay", n)
                        pe.matmul(G1[:, :], lup[0:DW, 0, :], xwa[0:DW, :], start=True, stop=True).then_inc(sem("g1_done"), 1)
                    if s == 5:
                        g1_free("aaa", n)
                        pe.matmul(G1[:, :], lup[DW:P, 0, :], xwa[DW:P, :], start=True, stop=True).then_inc(sem("g1_done"), 1)
                    if s == 8:
                        g1_free("norm", n)
                        pe.wait_ge(sem("squared"), n + 1)
                        pe.matmul(G1[:, :], ones_head[:, :], t1[:, :], start=True, stop=True).then_inc(sem("g1_done"), 1)
                    if s == 18:
                        g1_free("bonus", n)
                        pe.wait_ge(sem("rk_ready"), n + 1)
                        pe.matmul(G1[:, :], ones_head[:, :], xk[:, :], start=True, stop=True).then_inc(sem("g1_done"), 1)
                if 0 <= i < PAIRS and 9 <= s <= 12:
                    job, src = (("tokA", At), ("tokB", Bt), ("tokK", Kt), ("tokV", xv))[s - 9]
                    g1_free(job, i)
                    for j in range(TB):
                        mm = pe.transpose(G1[:, j * P:(j + 1) * P], src[:, j * P:(j + 1) * P], ident[:, :])
                    mm.then_inc(sem("g1_done"), 1)
                if i >= 1 and s == 13:
                    g1_free("outT", i - 1)
                    pe.wait_ge(sem("o_normed"), i)
                    for j in range(TB):
                        mm = pe.transpose(G1[:, j * P:(j + 1) * P], OC[:, j, :], ident[:, :])
                    mm.then_inc(sem("g1_done"), 1)
                if 0 <= i < PAIRS and s == 15:
                    g1_free("gate", i)
                    pe.wait_ge(sem("gup_in"), 32 * (i + 1))
                    pe.matmul(G1[:, :], lup[:, 1, :], xg0[:, :], start=True, stop=False)
                    pe.matmul(G1[:, :], lup[0:DG1, 2, :], xg1[:, :], start=False, stop=True).then_inc(sem("g1_done"), 1)
                if s < 18 and 3 + 3 * n + s // 6 < FIRST_B:
                    gemm_piece(3 + 3 * n + s // 6, s % 6)

            def gemm_piece(k, part):
                if part == 0:
                    pe.wait_ge(sem("lo_ready"), k + 1)
                    if k > NCHUNK:
                        pe.wait_ge(sem("pool_in"), k - NCHUNK)
                    else:
                        pe.wait_ge(sem("shifted"), k)
                for m in range(4 * part, 4 * part + 4):
                    kt, term = m // 3, m % 3
                    w, hx = ((w_hi, h_hi), (w_hi, h_lo), (w_lo, h_hi))[term]
                    mm = pe.matmul(G0[:, :], w[k % RING][:, kt, :], hx[:, kt, :], start=(m == 0), stop=(m == 23))
                if part == 5:
                    mm.then_inc(sem("w_used"), 1)

            per_slot(slot)
            def turn_back(n):
                pe.wait_ge(sem("ff_taken"), KT * (NQ - 1) + n + 1)
                if n >= 2:
                    pe.wait_ge(sem("out_tokens"), n - 1)
                for j in range(TB):
                    mm = pe.transpose(bank[4 + n % 2][:, j * P:(j + 1) * P], res[:, n, j * P:(j + 1) * P], ident[:, :])
                mm.then_inc(sem("turned_back"), 1)

            def product(k, o, hi, lo, free, ready=None):
                kts = chunks[k][0].shape[1]
                pe.wait_ge(sem("lo_ready"), k + 1)
                free()
                for kt in range(kts):
                    if ready:
                        ready(kt)
                    for m, (w, hx) in enumerate(((w_hi, hi), (w_hi, lo), (w_lo, hi))):
                        mm = pe.matmul(o, w[chunks[k][1]][:, kt, :], hx[:, kt, :], start=(kt == 0 and m == 0),
                                       stop=(kt == kts - 1 and m == 2))
                mm.then_inc(sem("w_used"), 1)

            def taken(name, n):
                return lambda: pe.wait_ge(sem(name), n) if n > 0 else None

            def turn_section(m):
                pe.wait_ge(sem("ada2_used"), 2 * KT * (m + 1))
                if m:
                    pe.wait_ge(sem("mod2"), m)
                for f in range(KT):
                    mm = pe.transpose(bank[6 + f // 4][:, f % 4 * P:(f % 4 + 1) * P], acc2[:, f * P:(f + 1) * P], ident[:, :])
                mm.then_inc(sem("ada_turned"), 1)

            for n in range(KT):
                k = K_GATE(n)
                if n == 0:
                    pe.wait_ge(sem("pool_in"), GP)
                    pe.wait_ge(sem("y_lo_ready"), PAIRS)
                    pe.wait_ge(sem("x_again"), 16 * TB)
                    for f in range(KT):
                        if f >= 2:
                            pe.wait_ge(sem("res_ready"), f - 1)
                        for j in range(TB):
                            mm = pe.transpose(bank[4 + f % 2][:, j * P:(j + 1) * P], xt2[:, j, f * P:(f + 1) * P], ident[:, :])
                        mm.then_inc(sem("x_turned2"), 1)
                product(k, bank[0][:, :], h_hi, h_lo, taken("gated", 2 * n - 1))
                product(k + 1, bank[1][:, :], h_hi, h_lo, taken("gated", 2 * n))
                product(k + 2, bank[2][:, :], y_hi, y_lo, taken("ru_taken", n))
                if n == 0:
                    pe.wait_ge(sem("wmix_in"), 16 * GP)
                    for g in range(GP):
                        pe.wait_ge(sem("pooled_up"), g + 1)
                        if g >= 2:
                            pe.wait_ge(sem("pool_scaled"), g - 1)
                        pe.matmul(bank[6 + g % 2][:, :], wmix[:, g, :], UP[g][:, :], start=True, stop=True).then_inc(sem("pool_mixed"), 1)
                product(k + 3, bank[3][:, :], mp_hi, mp_lo, taken("pu_taken", n), lambda kt: pe.wait_ge(sem("mp_ready"), kt + 1))
                if n >= 2 and n % 2 == 0:
                    turn_section(n // 2 - 1)

            def mean_of(f):
                pe.wait_ge(sem("out_taken2"), f + 1)
                pe.matmul(bank[4][:, :], ones_all[:, :], res[:, f, :], start=(f == 0), stop=(f == KT - 1)).then_inc(sem("ln1_mean"), 1)

            pe.wait_ge(sem("res_ready"), KT)
            pe.wait_ge(sem("gated"), 2 * KT)
            for n in range(KT):
                def free(n=n):
                    pe.wait_ge(sem("mixed"), KT)
                    if n >= 4:
                        pe.wait_ge(sem("out_taken2"), n - 3)
                product(K_OUT + n, bank[(K_OUT + n) % 4][:, :], mix_hi, mix_lo, free)
                if n == 0:
                    turn_section(3)
                if n >= 2:
                    mean_of(n - 2)
            mean_of(KT - 2)
            mean_of(KT - 1)
            for f in range(KT):
                pe.wait_ge(sem("ln1_squared"), f + 1)
                pe.matmul(bank[5][:, :], ones_all[:, :], (f1, f2)[f % 2][:, :], start=(f == 0), stop=(f == KT - 1)).then_inc(sem("ln1_var"), 1)
            for q in range(NQ):
                hid = ((y_hi, y_lo), (mix_hi, mix_lo))[q % 2]
                for n in range(KT):
                    k = K_FF + 2 * KT * q + n
                    def free(q=q, n=n):
                        if n >= 4:
                            pe.wait_ge(sem("relu"), KT * q + n - 3)
                        elif q:
                            pe.wait_ge(sem("ff_taken"), KT * (q - 1) + KT + n - 3)
                    product(k, bank[k % 4][:, :], h_hi, h_lo, free, (lambda kt: pe.wait_ge(sem("h2_ready"), kt + 1)) if q + n == 0 else None)
                for n in range(KT):
                    k = K_FF + 2 * KT * q + KT + n
                    def free(q=q, n=n):
                        if n >= 4:
                            pe.wait_ge(sem("ff_taken"), KT * q + n - 3)
                        else:
                            pe.wait_ge(sem("relu"), KT * q + KT + n - 3)
                    product(k, bank[k % 4][:, :], hid[0], hid[1], free,
                            (lambda kt, q=q: pe.wait_ge(sem("hidden"), KT * q + kt + 1)) if n == 0 else None)
                    if q == NQ - 1 and n >= 1:
                        turn_back(n - 1)
            turn_back(KT - 1)


_INS = ['x', 'c', 'w_ada', 'b_ada', 'w_in', 'mu_shift', 'pool_mix', 'pool_scale', 'w_pool_up', 'w0', 'w_decay_up', 'a0',
        'w_aaa_up', 'w_gate_up', 'k_k', 'k_a', 'r_k', 'gn_g', 'gn_b', 'w_rwkv_up', 'w_out', 'ln1_g', 'ln1_b', 'w_ff1',
        'w_ff2', 'ln2_g', 'ln2_b']
_OUTS = [((1, 512, 1024), 'float32')]


def kernel(**inputs):
    import numpy as _np
    import concourse.bacc as _bacc
    from concourse import mybir as _mybir
    from concourse.bass_utils import run_bass_kernel_spmd as _run

    nc = _bacc.Bacc("TRN2", target_bir_lowering=False, num_devices=1)
    arrays, args = {}, []
    for name in _INS:
        a = _np.ascontiguousarray(inputs[name])
        arrays[f"in_{name}_dram"] = a
        args.append(nc.dram_tensor(f"in_{name}_dram", a.shape, _mybir.dt.from_np(a.dtype), kind="ExternalInput").ap())
    for i, (shape, dtype) in enumerate(_OUTS):
        dt = _mybir.dt.from_np(_np.dtype(dtype))
        args.append(nc.dram_tensor(f"out_{i}_dram", shape, dt, kind="ExternalOutput").ap())
    build(nc, *args)
    r = _run(nc, [arrays], core_ids=[0])
    got = tuple(r.results[0][f"out_{i}_dram"] for i in range(len(_OUTS)))
    return got[0]
```

```python
from contextlib import ExitStack

import concourse.bass as bass
from concourse import mybir

P = 128
ALU = mybir.AluOpType
ACT = mybir.ActivationFunctionType
AX_X = mybir.AxisListType.X
F32 = mybir.dt.float32
F32R = mybir.dt.float32r


def build(nc, x, c, w_ada, b_ada, w_in, mu_shift, pool_mix, pool_scale, w_pool_up, w0, w_decay_up, a0,
          w_aaa_up, w_gate_up, k_k, k_a, r_k, gn_g, gn_b, w_rwkv_up, w_out, ln1_g, ln1_b, w_ff1, w_ff2,
          ln2_g, ln2_b, out):
    S, D = x.shape[1], x.shape[2]
    KT = D // P
    TB = S // P
    H = r_k.shape[1]
    N = r_k.shape[2]
    PAIRS = H * N // P
    C = 64
    NCH = S // C
    DP = pool_scale.shape[1]
    DW, DG = w_decay_up.shape[1], w_gate_up.shape[1]
    DG1 = DG - P
    COL_R = DP
    COL_K, COL_V = COL_R + D, COL_R + 2 * D
    COL_WA = COL_R + 3 * D
    COL_G0 = COL_WA + 2 * DW
    COL_G1 = COL_G0 + P
    EXPM = float(2.718281828459045 ** -0.5)
    ALPHA = 2.0 ** 0.25
    GN_EPS, LN_EPS = 64e-5, 1e-5
    SHIFT_TAIL = COL_G1 + DG1 - DP - 26 * P

    rows1 = dict(b_ada=0, mu=48, w0=74, a0=82, k_k=90, k_a=98, r_k=106, gn_g=114)
    rows2 = dict(gn_b=0, pool_scale=8, ln1_g=12, ln1_b=20, ln2_g=28, ln2_b=36, mu_tail=44)
    NP1, NP2 = 122, 45

    ctx = ExitStack()
    with ctx:
        def sb(name, shape, dt=F32):
            return ctx.enter_context(nc.sbuf_tensor(name, shape, dt))

        sems = {}

        def sem(name):
            if name not in sems:
                sems[name] = ctx.enter_context(nc.semaphore(name))
            return sems[name]

        over = ExitStack()
        x_again = over.enter_context(nc.sbuf_tensor("x_again", [P, TB, D], F32))
        over.close()
        h_hi, h_lo = sb("h_hi", [P, KT, S], F32R), sb("h_lo", [P, KT, S], F32R)
        y_hi, y_lo = sb("y_hi", [P, KT, S], F32R), sb("y_lo", [P, KT, S], F32R)
        RING = 2
        w_raw = [sb(f"w_raw{s}", [P, KT, P]) for s in range(RING)]
        w_hi = [sb(f"w_hi{s}", [P, KT, P], F32R) for s in range(RING)]
        w_lo = [sb(f"w_lo{s}", [P, KT, P], F32R) for s in range(RING)]
        lup = sb("lup", [P, 3, P])
        ident = sb("ident", [P, P])
        ones_all = sb("ones_all", [P, P])
        ones_col = sb("ones_col", [P, 1])
        ones_head = sb("ones_head", [P, P])
        params = sb("params", [P, 2 * P])
        p2 = P
        derived = sb("derived", [P, 96])
        mod = sb("mod", [P, 48])
        OMM, OMKA, HW0, HA0, CCOL, CS = 0, 27, 35, 43, 51, 59
        HM = 67
        rec = sb("rec", [P, 16])
        xk, xr, aa, t1 = (sb(n, [P, S]) for n in ("xk", "xr", "aa", "t1"))
        wk = ExitStack()

        def wb(name, shape, dt=F32):
            return wk.enter_context(nc.sbuf_tensor(name, shape, dt))

        m16T = wb("m16T", [P, P])
        m16 = wb("m16", [P, P])
        m32 = wb("m32", [P, P])
        m64 = wb("m64", [P, P])
        mlow = wb("mlow", [P, C])
        mupi = wb("mupi", [P, C])
        scanm = wb("scanm", [P, S])
        xwa, xg0, xg1 = wb("xwa", [P, S]), wb("xg0", [P, S]), wb("xg1", [DG1, S])
        xv, sg, t2, t3, t4 = (wb(n, [P, S]) for n in ("xv", "sg", "t2", "t3", "t4"))
        At, Bt, Kt, Rf = (wb(n, [P, S]) for n in ("At", "Bt", "Kt", "Rf"))
        Apad, Rpad, Bpad, Kpad = (wb(n, [P, 2, S]) for n in ("Apad", "Rpad", "Bpad", "Kpad"))
        DC = wb("DC", [P, NCH])
        Rc, DCc, bonus_c = wb("Rc", [P, S]), wb("DCc", [P, NCH]), wb("bonus_c", [P, S])
        A0, A0T, A1, A1T, TT = ([wb(f"{n}{e}", [P, TB, P]) for e in range(2)] for n in ("A0", "A0T", "A1", "A1T", "TT"))
        MAB, MAK = (wb(n, [P, TB, 2, C]) for n in ("MAB", "MAK"))
        AHT, Atok = (wb(n, [P, TB, P]) for n in ("AHT", "Atok"))
        SV = wb("SV", [P, NCH, P])
        BK = wb("BK", [P, NCH, P])
        MR = wb("MR", [P, NCH, 2, C])
        PT = [wb(f"PT{e}", [P, NCH, C]) for e in range(2)]
        bonus, gate = wb("bonus", [P, S]), wb("gate", [P, S])
        OC, SQ = wb("OC", [P, TB, P]), wb("SQ", [P, TB, P])
        Sbd, Stmp = wb("Sbd", [P, P]), wb("Stmp", [P, P])
        gn = wb("gn", [P, 4, 8])
        wk.close()
        st = ExitStack()
        NADA = 10

        def stb(name, shape, dt=F32):
            return st.enter_context(nc.sbuf_tensor(name, shape, dt))

        skip = stb("skip", [P, 6 * P + S])
        xtok = stb("xtok", [P, TB, D])
        ptab = stb("ptab", [P, 2, P])
        ada = [stb(f"ada{s}", [P, D]) for s in range(NADA)]
        acc = stb("acc", [P, 2, D])
        hf = [stb(f"hf{s}", [P, S]) for s in range(4)]
        crow = stb("crow", [KT, P])
        st.close()
        pt = ExitStack()

        def pb(name, shape, dt=F32):
            return pt.enter_context(nc.sbuf_tensor(name, shape, dt))

        for s in (2, 3):
            w_raw.append(pb(f"w_raw{s}", [P, KT, P]))
            w_hi.append(pb(f"w_hi{s}", [P, KT, P], F32R))
            w_lo.append(pb(f"w_lo{s}", [P, KT, P], F32R))
        mix_hi, mix_lo = pb("mix_hi", [P, KT, S], F32R), pb("mix_lo", [P, KT, S], F32R)
        res = pb("res", [P, KT, S])
        GP = DP // P
        wmix = pb("wmix", [P, GP, P])
        f1, f2, f3 = (pb(n, [P, S]) for n in ("f1", "f2", "f3"))
        lnv = pb("lnv", [P, S])
        small = pb("small", [P, 64])
        stat = pb("stat", [P, 3 * TB, 6])
        ada2 = pb("ada_late", [P, D])
        acc2 = pb("acc2", [P, D])
        tail = ExitStack()
        mp_hi, mp_lo = (tail.enter_context(nc.sbuf_tensor(n, [P, GP, S], F32R)) for n in ("mp_hi", "mp_lo"))
        tail.close()
        xt2 = pb("xt2", [P, TB, D])
        pt.close()

        bank = [ctx.enter_context(nc.psum_tensor(f"bank{b}", [P, 512], F32)) for b in range(8)]
        G0, G1, CH, OB = bank[0], bank[1], bank[6], bank[7]
        GATE_BANKS = [[bank[b] for b in ((4, 5, 7, 6) if n == 1 else (2, 3, 1, 0))] for n in range(KT)]
        OUT_BANKS = [bank[2], bank[3], bank[0], bank[1]]
        IN_BANKS = [bank[6], bank[7], bank[1], G0, bank[2], bank[3]]

        def in_bank(k):
            return IN_BANKS[k] if k < len(IN_BANKS) else G0

        def stage_bank(e, s_global):
            return bank[2 + 2 * e + s_global % 2]

        def blk(ap):
            return ap.rearrange("p (j t) -> p j t", j=TB)

        def halves(t, e):
            return t[:, 2 * e:2 * e + 2, :, :].rearrange("p j h c -> p (j h) c")

        def both_chunks(t, h):
            return t[:, :, h, :].unsqueeze(2).to_broadcast([P, TB, 2, C])

        def as_chunks(m):
            return m.rearrange("p j (z c) -> p j z c", z=2)

        def chunk_masks(m, blocks):
            return m[:, :].rearrange("p (z c) -> p z c", z=2).unsqueeze(1).to_broadcast([P, blocks, 2, C])

        def over_blocks(mask):
            return mask[:, :].unsqueeze(1).to_broadcast([P, TB, P])

        STAGES = ["MabT", "Mab", "Mak", "Q1", "Q2", "Q3", "Q4", "U1", "Q5", "Mr0", "Mr1", "U2", "U3",
                  "X1", "Tr1", "Y1", "X2", "Tr2", "Y2", "PT", "AHT"]
        NS = len(STAGES)
        BY_DVE = {"MabT", "Mab", "Mak", "Mr0", "Mr1", "U1", "U2", "U3", "Y1", "Y2"}
        ND = len(BY_DVE)
        PACKED = ("MabT", "Mab", "Mak", "Mr0", "Mr1")
        NA = NS - ND

        def evacuated(eng, e, i, name):
            at = STAGES.index(name)
            n = sum((m in BY_DVE) == (name in BY_DVE) for m in STAGES[:at + 1])
            if name in BY_DVE:
                eng.wait_ge(sem(f"taken_by_dve{e}"), ND * i + n)
            else:
                eng.wait_ge(sem(f"taken_by_act{e}"), NA * i + n)

        chunk_cols = [(COL_WA, P), (COL_G0, P), (COL_G1, DG1)]
        for n in range(PAIRS):
            chunk_cols += [(col + n * P, P) for col in (COL_K, COL_R, COL_V)]
        NCHUNK = len(chunk_cols)
        def w_cols(w, c0, width=P, r0=0, kts=KT):
            return w[0, r0:r0 + kts * P, c0:c0 + width].rearrange("(kt p) n -> p kt n", p=P)

        chunks = [(w_cols(w_in, c0, width), k % 2) for k, (c0, width) in enumerate(chunk_cols)]
        for g in range(GP):
            chunks.append((w_cols(w_in, g * P), len(chunks) % 2))
        FIRST_B = len(chunks)
        COL_GP = COL_G1 + DG1
        K_GP, K_GR, K_RU, K_PU = ([FIRST_B + at for at in first] + [FIRST_B + 4 * n + m for n in range(2, KT)]
                                  for m, first in enumerate(((0, 2), (1, 3), (4, 5), (6, 7))))
        gate_src = {}
        for n in range(KT):
            gate_src[K_GP[n]] = w_cols(w_in, COL_GP + n * P)
            gate_src[K_GR[n]] = w_cols(w_in, COL_GP + D + n * P)
            gate_src[K_RU[n]] = w_cols(w_rwkv_up, n * P)
            gate_src[K_PU[n]] = w_cols(w_pool_up, n * P, kts=GP)
        K_WIDE = FIRST_B + 6

        def slot_of(k):
            return k % 2 if k < K_WIDE else (2, 3, 1, 0)[(k - K_WIDE) % 4]

        for k in range(FIRST_B, FIRST_B + 4 * KT):
            chunks.append((gate_src[k], slot_of(k)))
        K_OUT = len(chunks)
        for n in range(KT):
            chunks.append((w_cols(w_out, n * P), slot_of(len(chunks))))
        K_FF = len(chunks)
        K_H2 = K_FF + 3
        DFF = w_ff1.shape[2]
        NQ = DFF // D
        for q in range(NQ):
            for n in range(KT):
                chunks.append((w_cols(w_ff1, (q * KT + n) * P), slot_of(len(chunks))))
            for n in range(KT):
                chunks.append((w_cols(w_ff2, n * P, r0=q * D), slot_of(len(chunks))))
        NALL = len(chunks)
        before, uses, seen = [], [], {}
        for k, (_, slot) in enumerate(chunks):
            before.append(seen[slot][0] if slot in seen else None)
            uses.append(seen[slot][1] + 1 if slot in seen else 1)
            seen[slot] = (k, uses[-1])

        g1_jobs = []
        for i in range(-1, PAIRS + 1):
            for s, job in ((4, "decay"), (5, "aaa"), (8, "norm"), (9, "tokA"), (10, "tokBK0"), (11, "tokBK1"),
                           (12, "tokV0"), (13, "outT"), (14, "tokV1"), (15, "gate"), (18, "bonus")):
                n = i + {"t": 0, "g": 0, "o": -1}.get(job[0], 1)
                if 0 <= n < PAIRS:
                    g1_jobs.append((job, n))
        g1_at = {key: k for k, key in enumerate(g1_jobs)}

        POOLED_AT = [(PAIRS, 6), (PAIRS, 12), (PAIRS, 18), (PAIRS + 1, 3)]
        POOL_STEPS = {}
        for g, (i, first) in enumerate(((PAIRS - 1, 7), (PAIRS - 1, 13), (PAIRS - 1, 19), (PAIRS, 3))):
            for step in range(g + 2):
                at = i * NS + first + step
                POOL_STEPS[at // NS, at % NS] = (g, step)
        SPLIT_AT = {(PAIRS, slot): FIRST_B + m for m, slot in enumerate((0, 3, 6, 8, 14))}
        UP = [xk, xr, aa, t1]
        SUM1, SUM2 = UP[0], UP[1]

        def per_slot(emit):
            for i in range(-1, PAIRS + 1):
                for s in range(NS):
                    emit(i, s)

        block = ctx.enter_context(nc.Block())

        def col(idx):
            return params[:, idx:idx + 1]

        def der(idx):
            return derived[:, idx:idx + 1]


        def part_of(k, buf):
            src, slot = chunks[k]
            return buf[slot][:, 0:src.shape[1], 0:src.shape[2]]

        def load_chunk(sp, k):
            src, slot = chunks[k]
            if before[k] is not None:
                sp.wait_ge(sem("lo_ready"), before[k] + 1)
            sp.dma_start(part_of(k, w_raw), src).then_inc(sem(f"w_in{slot}"), 16)

        def lup_next(sp, n):
            if n >= 1:
                sp.wait_ge(sem("g1_done"), g1_at[("aaa", n - 1)] + 1)
            cols = slice(n * P, (n + 1) * P)
            sp.dma_start(lup[0:DW, 0, :], w_decay_up[0, :, cols]).then_inc(sem("lup_in"), 16)
            sp.dma_start(lup[DW:P, 0, :], w_aaa_up[0, :, cols]).then_inc(sem("lup_in"), 16)

        def gup_next(sp, n):
            if n >= 1:
                sp.wait_ge(sem("g1_done"), g1_at[("gate", n - 1)] + 1)
            cols = slice(n * P, (n + 1) * P)
            sp.dma_start(lup[:, 1, :], w_gate_up[0, 0:P, cols]).then_inc(sem("gup_in"), 16)
            sp.dma_start(lup[0:DG1, 2, :], w_gate_up[0, P:DG, cols]).then_inc(sem("gup_in"), 16)

        @block.sync
        def _(sp):
            def prow(ap):
                return ap.rearrange("o (r f) -> (o r) f", f=P)

            rows = [(0, rows1["b_ada"], prow(b_ada)), (0, rows1["mu"], prow(mu_shift[:, 0:26 * P])), (0, rows1["w0"], prow(w0)),
                    (0, rows1["a0"], prow(a0)), (0, rows1["k_k"], prow(k_k)), (0, rows1["k_a"], prow(k_a)),
                    (0, rows1["r_k"], r_k.rearrange("o (r h) n -> (o r) (h n)", h=2)), (0, rows1["gn_g"], prow(gn_g)),
                    (1, rows2["gn_b"], prow(gn_b)), (1, rows2["pool_scale"], prow(pool_scale)), (1, rows2["ln1_g"], prow(ln1_g)),
                    (1, rows2["ln1_b"], prow(ln1_b)), (1, rows2["ln2_g"], prow(ln2_g)), (1, rows2["ln2_b"], prow(ln2_b)),
                    (1, rows2["mu_tail"], mu_shift[:, 26 * P:26 * P + DG1])]
            for q in range(2 * KT):
                sec, kt = (1, 0)[q // KT], q % KT
                if q >= NADA:
                    sp.wait_ge(sem("ada_used"), q - NADA + 1)
                if q == 2:
                    sp.wait_ge(sem("ptab_zero"), 1)
                if 2 <= q < 2 + len(rows):
                    tab, at, src = rows[q - 2]
                    sp.dma_start(ptab[at:at + src.shape[0], tab, 0:src.shape[1]], src).then_inc(sem("params_in"), 16)
                sp.dma_start(ada[q % NADA][:, :], w_ada[0, kt * P:(kt + 1) * P, sec * D:(sec + 1) * D]).then_inc(sem(f"ada_in{q % NADA}"), 16)
                if q == KT - 1:
                    for j in range(TB):
                        sp.dma_start(xtok[:, j, :], x[0, j * P:(j + 1) * P, :]).then_inc(sem("x_in"), 16)
            for tab, at, src in rows[2 * KT - 2:]:
                sp.dma_start(ptab[at:at + src.shape[0], tab, 0:src.shape[1]], src).then_inc(sem("params_in"), 16)
            for k in range(RING):
                load_chunk(sp, k)
            lup_next(sp, 0)
            gup_next(sp, 0)
            for k in range(RING, K_WIDE):
                load_chunk(sp, k)
                if k >= 6 and k % 3 == 0 and k < NCHUNK:
                    lup_next(sp, k // 3 - 1)
                if k >= 9 and k % 3 == 0 and k < NCHUNK:
                    gup_next(sp, k // 3 - 2)
                if k == FIRST_B:
                    gup_next(sp, PAIRS - 1)
            sp.wait_ge(sem("y_lo_ready"), PAIRS)
            for g in range(GP):
                sp.dma_start(wmix[:, g, :], pool_mix[0, g]).then_inc(sem("wmix_in"), 16)
            na = 0
            for k in range(K_WIDE, NALL):
                load_chunk(sp, k)
                for _ in range(2 if k >= FIRST_B + 9 else 0):
                    if na < 8 * KT:
                        sec, kt, half = 2 + na // (2 * KT), na // 2 % KT, na % 2
                        if na >= 2:
                            sp.wait_ge(sem("ada2_used"), na - 1)
                        sp.dma_start(ada2[:, half * S:(half + 1) * S],
                                     w_ada[0, kt * P:(kt + 1) * P, sec * D + half * S:sec * D + (half + 1) * S]
                                     ).then_inc(sem(f"ada2_in{half}"), 16)
                        na += 1
            sp.wait_ge(sem("ada2_used"), 8 * KT)
            sp.wait_ge(sem("mod2"), 4)
            sp.dma_start(acc2[:, :], ln2_g.to_broadcast([P, D])).then_inc(sem("ln2_in"), 16)
            sp.dma_start(ada2[:, :], ln2_b.to_broadcast([P, D])).then_inc(sem("ln2_in"), 16)
            for j in (0, 1, 3, 2):
                if j < TB - 1:
                    sp.wait_ge(sem("out_ready"), j + 1)
                else:
                    sp.wait_ge(sem("last_out_ready"), 1)
                sp.dma_start(out[0, j * P:(j + 1) * P, :], xt2[:, j, :]).then_inc(sem("stored"), 16)
            sp.wait_ge(sem("stored"), 16 * TB)

        @block.gpsimd
        def _(pool):
            step = [0]

            def link(ins, name=None):
                s = sem(name or "pool_step")
                key = name or "pool_step"
                counts[key] = counts.get(key, 0) + 1
                ins.then_inc(s, 1)
                pool.wait_ge(s, counts[key])

            counts = {}
            link(pool.memset(ptab[:, :, :], 0.0), "ptab_zero")
            link(pool.memset(ident[:, :], 0.0))
            link(pool.affine_select(out=ident[:, :], in_=ident[:, :], compare_op=ALU.not_equal, fill=1.0, base=0,
                                    pattern=[[-1, P]], channel_multiplier=1), "ident_ready")

            def blocks(m, size, fill=0.0):
                v = m[:, :].rearrange("p (b t) -> p b t", t=size)
                link(pool.affine_select(out=v, in_=v, compare_op=ALU.is_ge, fill=fill, base=0,
                                        pattern=[[-size, P // size], [0, size]], channel_multiplier=1))
                link(pool.affine_select(out=v, in_=v, compare_op=ALU.is_ge, fill=fill, base=size - 1,
                                        pattern=[[size, P // size], [0, size]], channel_multiplier=-1))

            def below(m, base):
                link(pool.affine_select(out=m[:, :], in_=m[:, :], compare_op=ALU.is_ge, fill=0.0, base=base,
                                        pattern=[[-1, P]], channel_multiplier=1))

            def above(m, base):
                link(pool.affine_select(out=m[:, :], in_=m[:, :], compare_op=ALU.is_ge, fill=0.0, base=base,
                                        pattern=[[1, P]], channel_multiplier=-1))

            for m in (m16T, m16, m32, m64, mlow, mupi, ones_head):
                link(pool.memset(m[:, :], 1.0))
            link(pool.memset(ones_all[:, :], 1.0 / D))
            link(pool.memset(ones_col[:, :], 1.0))
            for t in range(16):
                link(pool.memset(rec[:, t:t + 1], 1.0 / (t + 1)))
            blocks(m16T, 16)
            above(m16T, -1)
            blocks(m16, 16)
            below(m16, -1)
            blocks(m32, 32)
            blocks(m64, 64)
            for z in range(P // C):
                for m, sign, base in ((mlow, 1, -1), (mupi, -1, 0)):
                    part = m[z * C:(z + 1) * C, :]
                    link(pool.affine_select(out=part, in_=part, compare_op=ALU.is_ge, fill=0.0, base=base,
                                            pattern=[[-sign, C]], channel_multiplier=sign))
            blocks(ones_head, N)
            for m, size in ((m32, 32), (m64, 64)):
                v = m[:, :].rearrange("p (b h t) -> p b h t", h=2, t=size // 2)
                link(pool.memset(v[:, :, 1, :], 0.0))
                w = m[:, :].rearrange("p (b t) -> p b t", t=size)
                link(pool.affine_select(out=w, in_=w, compare_op=ALU.is_ge, fill=0.0, base=-(size // 2),
                                        pattern=[[-size, P // size], [0, size]], channel_multiplier=1))
            link(pool.memset(scanm[:, :], 1.0))
            link(pool.memset(scanm[:, :].rearrange("p (c t) -> p c t", t=C)[:, :, 0:1], 0.0))
            hm = derived[:, HM:HM + 2]
            link(pool.memset(hm, 1.0))
            link(pool.affine_select(out=hm[:, 0:1], in_=hm[:, 0:1], compare_op=ALU.is_ge, fill=0.0, base=N - 1,
                                    pattern=[[0, 1]], channel_multiplier=-1))
            link(pool.affine_select(out=hm[:, 1:2], in_=hm[:, 1:2], compare_op=ALU.is_ge, fill=0.0, base=-N,
                                    pattern=[[0, 1]], channel_multiplier=1), "consts_ready")

            def split_lo(k):
                pool.wait_ge(sem("hi_ready"), k + 1)
                link(pool.tensor_tensor(part_of(k, w_lo), part_of(k, w_raw), part_of(k, w_hi).bitcast(F32), ALU.subtract),
                     "lo_ready")

            for k in range(2):
                split_lo(k)
            for f in range(1, KT, 2):
                pool.wait_ge(sem("h_f32"), f + 1)
                pool.wait_ge(sem("h_hi_ready"), f + 1)
                link(pool.tensor_tensor(h_lo[:, f, :], hf[f % 4][:, :], h_hi[:, f, :].bitcast(F32), ALU.subtract), "h_lo_by_pool")
            pool.wait_ge(sem("h_lo_by_dve"), KT // 2)
            split_lo(2)
            split_lo(3)

            def slot(i, s):
                name = STAGES[s]
                for e in range(2):
                    if 0 <= i < PAIRS and name == "Q1":
                        for half in range(2):
                            evacuated(pool, half, i, "Mab")
                        link(pool.tensor_tensor(as_chunks(A0[e][:, :, :]), both_chunks(MAB, e), chunk_masks(m16, TB), ALU.mult), f"pooled{e}")
                    if 0 <= i < PAIRS and name == "U3":
                        pool.wait_ge(sem(f"multiplied{e}"), NS * i + STAGES.index("U2") + 1)
                        link(pool.tensor_tensor(as_chunks(A0[e][:, :, :]), both_chunks(MAB, e), chunk_masks(m32, TB), ALU.mult), f"pooled{e}")
                    if 0 <= i < PAIRS and name == "Y1":
                        pool.wait_ge(sem(f"multiplied{e}"), NS * i + STAGES.index("X1") + 1)
                        link(pool.tensor_tensor(as_chunks(A0[e][:, :, :]), both_chunks(MAB, e), chunk_masks(m64, TB), ALU.mult), f"pooled{e}")
                n = i + 1
                if n < PAIRS:
                    if s == 7:
                        pool.wait_ge(sem("scanned"), n + 1)
                        link(pool.tensor_tensor(sg[:, :], t3[:, :], sg[:, :], ALU.subtract), "before_sum")
                if s in (0, 6, 12) and 3 * n + 4 + s // 6 < FIRST_B:
                    split_lo(3 * n + 4 + s // 6)
                if (i, s) in SPLIT_AT:
                    split_lo(SPLIT_AT[i, s])
                if i >= 1 and s == 16:
                    pool.wait_ge(sem("y_hi_ready"), i)
                    link(pool.tensor_tensor(y_lo[:, i - 1, :], SQ[:, :, :].rearrange("p j t -> p (j t)"), y_hi[:, i - 1, :].bitcast(F32), ALU.subtract), "y_lo_ready")

            per_slot(slot)
            for k in range(K_WIDE - 1, K_H2):
                split_lo(k)
            for f in range(1, KT, 2):
                pool.wait_ge(sem("h2_hi"), f + 1)
                link(pool.tensor_tensor(h_lo[:, f, :], (f1, f2)[f % 2][:, :], h_hi[:, f, :].bitcast(F32), ALU.subtract), "h2_lo_by_pool")
            for k in range(K_H2, NALL):
                split_lo(k)
            pool.wait_ge(sem("ln2_in"), 32)
            pool.wait_ge(sem("ln2_normed"), 1)
            link(pool.tensor_tensor(xt2[:, TB - 1, :], xt2[:, TB - 1, :], acc2[:, :], ALU.mult))
            link(pool.tensor_tensor(xt2[:, TB - 1, :], xt2[:, TB - 1, :], ada2[:, :], ALU.add), "last_out_ready")

        @block.scalar
        def _(act):
            counts = {}

            def link(ins, name=None):
                key = name or "act_step"
                counts[key] = counts.get(key, 0) + 1
                ins.then_inc(sem(key), 1)
                act.wait_ge(sem(key), counts[key])

            def split_hi(k):
                slot = chunks[k][1]
                act.wait_ge(sem(f"w_in{slot}"), 16 * uses[k])
                if before[k] is not None:
                    act.wait_ge(sem("w_used"), before[k] + 1)
                link(act.activation(part_of(k, w_hi), part_of(k, w_raw), ACT.Copy), "hi_ready")

            def shift_first(k, dst, mucol, rows=P):
                act.wait_ge(sem("w_used"), k + 1)
                link(act.activation(dst[0:rows, :], in_bank(k)[0:rows, :], ACT.Copy, scale=derived[0:rows, OMM + mucol:OMM + mucol + 1]), "kept")

            act.dma_start(crow[:, :], c.rearrange("o (r f) -> (o r) f", f=P)).then_inc(sem("c_in"), 16)
            act.wait_ge(sem("c_cols"), 1)
            link(act.activation(derived[:, CS:CS + KT], derived[:, CCOL:CCOL + KT], ACT.Tanh, scale=0.5), "c_tanh")
            for k in range(2):
                split_hi(k)
            for f in range(KT):
                act.wait_ge(sem("h_f32"), f + 1)
                link(act.activation(h_hi[:, f, :], hf[f % 4][:, :], ACT.Copy), "h_hi_ready")
            for k, (dst, mucol, rows) in enumerate(((xwa, 24, P), (xg0, 25, P), (xg1, 26, DG1))):
                shift_first(k, dst, mucol, rows)
                if k < 2:
                    split_hi(2 + k)
                act.wait_ge(sem("shifted"), k + 1)
                if k == 0:
                    link(act.activation(xwa[0:DW, :], xwa[0:DW, :], ACT.Tanh), "lora_act")
                else:
                    link(act.activation(dst[0:rows, :], dst[0:rows, :], ACT.Tanh, scale=0.5), "lora_act")

            def take(e, i, s):
                name = STAGES[s]
                dst = {"Q1": A1, "Q2": A1T, "Q3": A0, "Q4": A0T, "Q5": A1, "X1": A1T, "Tr1": A1, "X2": A1T,
                       "Tr2": A1}.get(name)
                act.wait_ge(sem(f"multiplied{e}"), NS * i + s + 1)
                src = blk(stage_bank(e, NS * i + s)[:, :])
                if name == "PT":
                    link(act.activation(PT[e][C:P, :, :], stage_bank(e, NS * i + s)[C:P, :].rearrange("p (m c) -> p m c", c=C),
                                        ACT.Copy), f"taken_by_act{e}")
                elif name == "AHT":
                    rows = slice(N * e, N * e + N)
                    link(act.activation(AHT[rows, :, :], src[rows], ACT.Copy), f"taken_by_act{e}")
                else:
                    link(act.activation(dst[e][:, :, :], src, ACT.Copy), f"taken_by_act{e}")

            def slot(i, s):
                name = STAGES[s]
                n = i + 1
                if n < PAIRS and s in (6, 12, 18):
                    k = 3 + 3 * n + s // 6 - 1
                    shift_first(k, (xk, xr, xv)[s // 6 - 1], ((8, 0, 16)[s // 6 - 1]) + n)
                if i >= 1 and s < NCH:
                    act.wait_ge(sem("sa_done"), NCH * (i - 1) + s + 1)
                    link(act.activation(SV[0:C, s, :], CH[0:C, 0:P], ACT.Copy), "sa_taken")
                if 0 <= i < PAIRS and name not in BY_DVE:
                    for e in range(2):
                        take(e, i, s)
                if s in (0, 6, 12) and 3 * n + 4 + s // 6 < FIRST_B:
                    split_hi(3 * n + 4 + s // 6)
                if (n, s) in POOLED_AT:
                    g = POOLED_AT.index((n, s))
                    act.wait_ge(sem("w_used"), NCHUNK + g + 1)
                    link(act.activation(UP[g][:, :], G0[:, :], ACT.Copy), "pool_in")
                if (i, s) in SPLIT_AT and s < 14:
                    split_hi(SPLIT_AT[i, s])
                if n < PAIRS:
                    if s == 4:
                        act.wait_ge(sem("g1_done"), g1_at[("decay", n)] + 1)
                        link(act.activation(sg[:, :], G1[:, :], ACT.Tanh, bias=der(HW0 + n), scale=0.5), "decay_taken")
                    if s == 5:
                        act.wait_ge(sem("g1_done"), g1_at[("aaa", n)] + 1)
                        link(act.activation(aa[:, :], G1[:, :], ACT.Tanh, bias=der(HA0 + n), scale=0.5), "aaa_taken")
                    if s == 7:
                        act.wait_ge(sem("shifted"), 3 + 3 * n + 1)
                        link(act.activation(t1[:, :], xk[:, :], ACT.Square, scale=col(rows1["k_k"] + n)), "squared")
                    if s == 8:
                        act.wait_ge(sem("g1_done"), g1_at[("norm", n)] + 1)
                        link(act.activation(t1[:, :], G1[:, :], ACT.Sqrt), "norm_taken")
                    if s == 10:
                        act.wait_ge(sem("before_sum"), n + 1)
                        link(act.activation(sg[:, :], sg[:, :], ACT.Exp, scale=-EXPM))
                        link(act.activation(t4[:, :], t3[:, :], ACT.Exp, scale=-EXPM))
                        link(act.activation(t3[:, :], t3[:, :], ACT.Exp, scale=EXPM), "exps")
                    if s in (18, 20):
                        src, dst, made, done = ((Bt, Bpad, "b_made", "b_padded"), (Kt, Kpad, "prepared", "k_padded"))[s // 20]
                        act.wait_ge(sem(made), n + 1)
                        for e in range(2):
                            link(act.activation(dst[:, e, :], src[:, :], ACT.Copy, scale=der(HM + e)), done)
                if 0 <= i < PAIRS and s == 8:
                    if i >= 1:
                        act.wait_ge(sem("so_done"), NCH * i)
                        act.wait_ge(sem("s_taken"), NCH * i)
                    act.wait_ge(sem("prepared"), i + 1)
                    link(act.activation(Rc[:, :], Rf[:, :], ACT.Copy), "carried")
                    link(act.activation(DCc[:, :], DC[:, :], ACT.Copy), "carried")
                if 0 <= i < PAIRS and s == 15:
                    act.wait_ge(sem("g1_done"), g1_at[("gate", i)] + 1)
                    if i >= 1:
                        act.wait_ge(sem("y_ready"), i)
                    link(act.activation(gate[:, :], G1[:, :], ACT.Copy), "gate_taken")
                    link(act.activation(bonus_c[:, :], bonus[:, :], ACT.Copy), "bonus_carried")
                if 0 <= i < PAIRS and s in (9, 10, 11):
                    job, dst = (("tokA", Atok[:, :, :]), ("tokBK0", BK[:, 0:4, :]), ("tokBK1", BK[:, 4:8, :]))[s - 9]
                    act.wait_ge(sem("g1_done"), g1_at[(job, i)] + 1)
                    link(act.activation(dst, blk(G1[:, :]), ACT.Copy), "tok_taken")
                if 0 <= i < PAIRS and s in (12, 14):
                    half = (s - 12) // 2
                    act.wait_ge(sem("g1_done"), g1_at[(f"tokV{half}", i)] + 1)
                    link(act.activation(SV[C:P, 4 * half:4 * half + 4, :], blk(G1[:, :])[C:P], ACT.Copy), "v_taken")
                if i >= 1:
                    if s == 9:
                        act.wait_ge(sem("centred"), i)
                        if i >= 2:
                            act.wait_ge(sem("y_lo_ready"), i - 1)
                        link(act.activation(SQ[:, :, :], OC[:, :, :], ACT.Square), "o_squared")
                    if s == 10:
                        act.wait_ge(sem("o_var"), i)
                        link(act.activation(gn[:, 2, :], gn[:, 1, :], ACT.Sqrt), "o_std")
                    if s == 13:
                        act.wait_ge(sem("g1_done"), g1_at[("outT", i - 1)] + 1)
                        link(act.activation(SQ[:, :, :], blk(G1[:, :]), ACT.Identity, scale=col(rows1["gn_g"] + i - 1),
                                            bias=params[:, P + rows2["gn_b"] + i - 1:P + rows2["gn_b"] + i]), "out_taken")
                    if s == 15:
                        act.wait_ge(sem("y_ready"), i)
                        link(act.activation(y_hi[:, i - 1, :], SQ[:, :, :].rearrange("p j t -> p (j t)"), ACT.Copy), "y_hi_ready")
                if (i, s) in SPLIT_AT and s == 14:
                    split_hi(SPLIT_AT[i, s])

            per_slot(slot)
            def square_of(n):
                act.wait_ge(sem("ln1_centred"), n + 1)
                if n >= 2:
                    act.wait_ge(sem("ln1_sq_used"), n - 1)
                link(act.activation((f1, f2)[n % 2][:, :], res[:, n, :], ACT.Square), "ln1_squared")

            act.wait_ge(sem("y_lo_ready"), PAIRS)

            def gates_of(n):
                for m, k in enumerate((K_GP[n], K_GR[n])):
                    if n >= 2:
                        split_hi(k + 3)
                    act.wait_ge(sem("w_used"), k + 1)
                    if n >= 1:
                        act.wait_ge(sem("mixed"), n)
                    link(act.activation((f1, f2)[m][:, :], GATE_BANKS[n][m][:, :], ACT.Sigmoid), "gated")

            def mixed_hi(n):
                act.wait_ge(sem("mix_sum"), n + 1)
                link(act.activation(mix_hi[:, n, :], f3[:, :], ACT.Copy), "mixed_hi")

            split_hi(K_WIDE - 1)
            gates_of(0)
            split_hi(K_WIDE)
            split_hi(K_WIDE + 1)
            for g in range(GP):
                act.wait_ge(sem("pool_mixed"), g + 1)
                if g >= 1:
                    act.wait_ge(sem("mp_ready"), g)
                link(act.activation(lnv[:, :], (G0, CH)[g % 2][:, :], ACT.Copy,
                                    scale=params[:, P + 8 + g:P + 9 + g]), "pool_scaled")
                link(act.activation(mp_hi[:, g, :], lnv[:, :], ACT.Copy), "mp_hi_ready")
            split_hi(K_WIDE + 2)
            split_hi(K_WIDE + 3)
            mixed_hi(0)
            gates_of(1)
            split_hi(K_WIDE + 4)
            mixed_hi(1)
            for n in range(2, KT):
                gates_of(n)
                if n == KT - 1:
                    for j in range(TB):
                        act.dma_start(x_again[:, j, :], x[0, j * P:(j + 1) * P, :]).then_inc(sem("x_again"), 16)
                split_hi(K_RU[n] + 3)
                split_hi(K_PU[n] + 3)
                mixed_hi(n)
            for n in range(KT):
                act.wait_ge(sem("x_turned2"), n + 1)
                link(act.activation(res[:, n, :], bank[6 + n % 2][:, :], ACT.Copy, scale=ALPHA), "res_ready")
                split_hi(K_OUT + n + 3)
                if n >= 1:
                    square_of(n - 1)
            square_of(KT - 1)
            link(act.activation(small[:, 56:57], rec[:, 0:1], ACT.Sqrt))
            act.wait_ge(sem("ln1_eps"), 1)
            link(act.activation(lnv[:, :], lnv[:, :], ACT.Sqrt), "ln1_std")
            for f in range(KT):
                hb = (f1, f2)[f % 2]
                act.wait_ge(sem("ln1_normed"), f + 1)
                if f >= 2:
                    act.wait_ge(sem(("h2_lo_by_dve", "h2_lo_by_pool")[f % 2]), f // 2)
                link(act.activation(hb[:, :], res[:, f, :], ACT.Identity, scale=mod[:, 32 + f:33 + f], bias=mod[:, 24 + f:25 + f]))
                link(act.activation(h_hi[:, f, :], hb[:, :], ACT.Copy), "h2_hi")
            for f in range(KT):
                link(act.activation(res[:, f, :], res[:, f, :], ACT.Identity, scale=small[:, f:f + 1], bias=small[:, 8 + f:9 + f]),
                     "res_scaled")
            for q in range(NQ):
                for n in range(KT):
                    k, m = K_FF + 2 * KT * q + n, KT * q + n
                    if k + 3 < NALL:
                        split_hi(k + 3)
                    act.wait_ge(sem("w_used"), k + 1)
                    if m >= 2:
                        act.wait_ge(sem("hidden"), m - 1)
                    link(act.activation((f1, f2)[m % 2][:, :], bank[k % 4][:, :], ACT.Relu), "relu")
                    link(act.activation(y_hi[:, n, :], (f1, f2)[m % 2][:, :], ACT.Square), "hidden_hi")
                for n in range(KT):
                    k = K_FF + 2 * KT * q + KT + n
                    if k + 3 < NALL:
                        split_hi(k + 3)
                    if q == NQ - 1:
                        act.wait_ge(sem("turned_back"), n + 1)
                        link(act.activation(xt2[:, :, n * P:(n + 1) * P], blk(bank[4 + n % 2][:, :]), ACT.Copy), "out_tokens")
            act.wait_ge(sem("ln2_eps"), 1)
            link(act.activation(small[:, 32:36], small[:, 28:32], ACT.Sqrt), "ln2_std")
            act.wait_ge(sem("ln2_cols"), 1)
            link(act.activation(xt2[:, TB - 1, :], xt2[:, TB - 1, :], ACT.Identity, scale=small[:, 36 + TB - 1:36 + TB],
                                bias=small[:, 40:41]), "ln2_normed")

        @block.vector
        def _(dve):
            counts = {}

            def link(ins, name=None):
                key = name or "dve_step"
                counts[key] = counts.get(key, 0) + 1
                ins.then_inc(sem(key), 1)
                dve.wait_ge(sem(key), counts[key])

            dve.wait_ge(sem("c_turned"), 1)
            link(dve.tensor_copy(derived[:, CCOL:CCOL + KT], bank[0][:, 2 * P:2 * P + KT]), "c_cols")
            dve.wait_ge(sem("c_tanh"), 1)
            link(dve.tensor_scalar(derived[:, CS:CS + KT], derived[:, CS:CS + KT], 0.5, 0.5, ALU.mult, ALU.add))
            link(dve.tensor_tensor(derived[:, CS:CS + KT], derived[:, CS:CS + KT], derived[:, CCOL:CCOL + KT], ALU.mult))
            for q in range(2 * KT):
                kt, half = q % KT, q // KT
                dve.wait_ge(sem(f"ada_in{q % NADA}"), 16 * (q // NADA + 1))
                if kt == 0:
                    link(dve.tensor_scalar(acc[:, half, :], ada[q % NADA][:, :], der(CS), None, ALU.mult), "ada_used")
                else:
                    link(dve.scalar_tensor_tensor(out=acc[:, half, :], in0=ada[q % NADA][:, :], scalar=der(CS + kt),
                                                  in1=acc[:, half, :], op0=ALU.mult, op1=ALU.add), "ada_used")
            dve.wait_ge(sem("param_cols"), 1)
            link(dve.tensor_copy(params[:, 0:P], bank[0][:, 0:P]))
            link(dve.tensor_copy(params[:, P:2 * P], bank[0][:, P:2 * P]))
            link(dve.tensor_scalar(derived[:, OMM:OMM + 26], params[:, 48:74], -1.0, 1.0, ALU.mult, ALU.add))
            link(dve.tensor_scalar(der(OMM + 26), params[:, P + 44:P + 45], -1.0, 1.0, ALU.mult, ALU.add))
            link(dve.tensor_scalar(derived[:, OMKA:OMKA + 8], params[:, 98:106], -1.0, 1.0, ALU.mult, ALU.add))
            link(dve.tensor_scalar(derived[:, HW0:HW0 + 8], params[:, 74:82], 0.5, None, ALU.mult))
            link(dve.tensor_scalar(derived[:, HA0:HA0 + 8], params[:, 82:90], 0.5, None, ALU.mult))
            dve.wait_ge(sem("mod_done"), 1)
            link(dve.tensor_tensor(mod[:, 8:16], bank[1][:, 0:8], params[:, 8:16], ALU.add))
            link(dve.tensor_scalar(mod[:, 8:16], mod[:, 8:16], 1.0, None, ALU.add))
            link(dve.tensor_tensor(mod[:, 0:8], bank[1][:, 8:16], params[:, 0:8], ALU.add))
            for f in range(KT):
                dve.wait_ge(sem("x_turned"), f + 1)
                if f >= 4:
                    dve.wait_ge(sem("h_lo_by_pool"), f // 2 - 1)
                link(dve.tensor_scalar(hf[f % 4][:, :], bank[2 + f % 4][:, :], mod[:, 8 + f:9 + f], mod[:, f:f + 1], ALU.mult, ALU.add), "h_f32")
                if f % 2 == 1:
                    dve.wait_ge(sem("h_hi_ready"), f)
                    link(dve.tensor_tensor(h_lo[:, f - 1, :], hf[(f - 1) % 4][:, :], h_hi[:, f - 1, :].bitcast(F32), ALU.subtract),
                         "h_lo_by_dve")

            def shift_rest(k, dst, mu_ap, rows=P):
                dve.wait_ge(sem("kept"), k + 1)
                link(dve.scalar_tensor_tensor(out=dst[0:rows, 1:S], in0=in_bank(k)[0:rows, 0:S - 1], scalar=mu_ap,
                                              in1=dst[0:rows, 1:S], op0=ALU.mult, op1=ALU.add), "shifted")

            for k, (dst, mu_ap, rows) in enumerate(((xwa, col(48 + 24), P), (xg0, col(48 + 25), P),
                                                    (xg1, params[0:DG1, P + 44:P + 45], DG1))):
                shift_rest(k, dst, mu_ap, rows)
                dve.wait_ge(sem("lora_act"), k + 1)
                if k:
                    link(dve.tensor_scalar(dst[0:rows, :], dst[0:rows, :], 0.5, 0.5, ALU.mult, ALU.add), "lora_ready")
                else:
                    link(dve.memset(gn[:, :, :], 0.0), "lora_ready")

            def take(e, i, s):
                name = STAGES[s]
                dve.wait_ge(sem(f"multiplied{e}"), NS * i + s + 1)
                src = blk(stage_bank(e, NS * i + s)[:, :])
                key = f"taken_by_dve{e}"
                if name == "MabT":
                    if e == 0:
                        dve.wait_ge(sem("multiplied1"), NS * i + s + 1)
                        for head in range(2):
                            for half in range(2):
                                part = stage_bank(half, NS * i + s)[:, 0:4 * C].rearrange("p (j h c) -> p j h c", j=2, h=2)
                                link(dve.tensor_tensor(as_chunks(A0T[head][:, 2 * half:2 * half + 2, :]),
                                                       part[:, :, head, :].unsqueeze(2).to_broadcast([P, 2, 2, C]),
                                                       chunk_masks(m16T, 2), ALU.mult), f"taken_by_dve{half}" if head else None)
                elif name in PACKED:
                    if name == "Mak":
                        link(dve.tensor_tensor(TT[e][:, :, :], A0T[e][:, :, :], over_blocks(ident), ALU.add))
                    dst, mask = {"Mab": (MAB, mlow), "Mak": (MAK, mlow), "Mr0": (MR[:, 0:4], mupi), "Mr1": (MR[:, 4:8], mupi)}[name]
                    link(dve.tensor_tensor(halves(dst, e), stage_bank(e, NS * i + s)[:, 0:4 * C].rearrange("p (m c) -> p m c", c=C),
                                           mask[:, :].unsqueeze(1).to_broadcast([P, 4, C]), ALU.mult), key)
                else:
                    link(dve.tensor_tensor(TT[e][:, :, :], src, TT[e][:, :, :], ALU.add), key)

            def pool_step(g, step):
                w, u = 2 << g, UP[g]
                cur, nxt = (t2, t3) if step % 2 else (t3, t2)
                if step == 0:
                    dve.wait_ge(sem("pool_in"), g + 1)
                    link(dve.tensor_copy(nxt[:, 0:1], u[:, 0:1]))
                    link(dve.tensor_tensor(nxt[:, 1:S], u[:, 1:S], u[:, 0:S - 1], ALU.add))
                elif step <= g:
                    d = 1 << step
                    link(dve.tensor_copy(nxt[:, 0:d], cur[:, 0:d]))
                    link(dve.tensor_tensor(nxt[:, d:S], cur[:, d:S], cur[:, 0:S - d], ALU.add))
                else:
                    link(dve.tensor_tensor(cur[:, 0:w], cur[:, 0:w], rec[:, 0:w], ALU.mult))
                    link(dve.tensor_tensor(u[:, 0:w], cur[:, 0:w], u[:, 0:w], ALU.subtract))
                    link(dve.scalar_tensor_tensor(out=u[:, w:S], in0=cur[:, w:S], scalar=1.0 / w, in1=u[:, w:S],
                                                  op0=ALU.mult, op1=ALU.subtract), "pooled_up")

            def slot(i, s):
                name = STAGES[s]
                n = i + 1
                if n < PAIRS and s in (6, 12, 18):
                    k = 3 + 3 * n + s // 6 - 1
                    shift_rest(k, (xk, xr, xv)[s // 6 - 1], col(48 + (8, 0, 16)[s // 6 - 1] + n))
                if 0 <= i < PAIRS and name in BY_DVE:
                    for e in range(2):
                        take(e, i, s)
                if i >= 1 and s < NCH:
                    dve.wait_ge(sem("state_done"), NCH * (i - 1) + s + 1)
                    link(dve.tensor_tensor(Stmp[:, :], CH[:, 2 * P:3 * P], Sbd[:, :], ALU.add))
                    dve.wait_ge(sem("so_done"), NCH * (i - 1) + s + 1)
                    link(dve.scalar_tensor_tensor(out=Sbd[:, :], in0=Stmp[:, :], scalar=DCc[:, s:s + 1], in1=ones_head[:, :],
                                                  op0=ALU.mult, op1=ALU.mult), "s_taken")
                if n < PAIRS:
                    if s == 5:
                        dve.wait_ge(sem("decay_taken"), n + 1)
                        link(dve.tensor_scalar(sg[:, :], sg[:, :], 0.5, 0.5, ALU.mult, ALU.add))
                        link(dve.tensor_tensor_scan(t3[:, :], scanm[:, :], sg[:, :], 0.0, ALU.mult, ALU.add), "scanned")
                    if s == 6:
                        dve.wait_ge(sem("aaa_taken"), n + 1)
                        link(dve.tensor_scalar(aa[:, :], aa[:, :], 0.5, 0.5, ALU.mult, ALU.add))
                    if s == 9:
                        dve.wait_ge(sem("norm_taken"), n + 1)
                        link(dve.tensor_scalar(t1[:, :], t1[:, :], 1e-12, None, ALU.max))
                    if 9 <= s <= 12:
                        qq = slice((s - 9) * P, (s - 8) * P)
                        link(dve.reciprocal(t2[:, qq], t1[:, qq]))
                    if s == 13:
                        link(dve.scalar_tensor_tensor(out=t1[:, :], in0=xk[:, :], scalar=col(90 + n), in1=t2[:, :], op0=ALU.mult, op1=ALU.mult))
                        link(dve.tensor_scalar(t2[:, :], aa[:, :], col(98 + n), der(OMKA + n), ALU.mult, ALU.add))
                    if s == 14:
                        link(dve.tensor_tensor(t2[:, :], xk[:, :], t2[:, :], ALU.mult))
                        link(dve.scalar_tensor_tensor(out=xk[:, :], in0=xr[:, :], scalar=col(106 + n), in1=t2[:, :], op0=ALU.mult, op1=ALU.mult), "rk_ready")
                    if s == 15:
                        dve.wait_ge(sem("exps"), n + 1)
                        link(dve.scalar_tensor_tensor(out=At[:, :], in0=t1[:, :], scalar=-1.0, in1=sg[:, :], op0=ALU.mult, op1=ALU.mult))
                        for e in range(2):
                            link(dve.tensor_scalar(Apad[:, e, :], At[:, :], der(HM + e), None, ALU.mult))
                    if s == 16:
                        if n >= 1:
                            dve.wait_ge(sem("carried"), 2 * n)
                        link(dve.tensor_tensor(Rf[:, :], xr[:, :], t4[:, :], ALU.mult))
                        link(dve.tensor_copy(DC[:, :], t4[:, :].rearrange("p (c t) -> p c t", t=C)[:, :, C - 1]))
                        for e in range(2):
                            link(dve.tensor_scalar(Rpad[:, e, :], Rf[:, :], der(HM + e), None, ALU.mult))
                    if s == 17:
                        link(dve.tensor_tensor(aa[:, :], t1[:, :], aa[:, :], ALU.mult))
                        link(dve.tensor_tensor(Bt[:, :], aa[:, :], t3[:, :], ALU.mult), "b_made")
                    if s == 18:
                        dve.wait_ge(sem("g1_done"), g1_at[("bonus", n)] + 1)
                        if n >= 1:
                            dve.wait_ge(sem("bonus_carried"), n)
                        link(dve.tensor_tensor(bonus[:, :], G1[:, :], xv[:, :], ALU.mult), "bonus_taken")
                    if s == 19:
                        link(dve.tensor_tensor(Kt[:, :], t2[:, :], t3[:, :], ALU.mult), "prepared")
                if i >= 1:
                    g8 = lambda ap: ap.rearrange("p j (e v) -> p (j e) v", e=2)
                    ob = OB[:, :].rearrange("p (g v) -> p g v", v=N)
                    if s == 8:
                        link(dve.tensor_reduce(gn[:, 0, :], ob, AX_X, ALU.add))
                        link(dve.tensor_scalar(gn[:, 0, :], gn[:, 0, :], 1.0 / N, None, ALU.mult))
                        link(dve.tensor_tensor(OC[:, :, :].rearrange("p j (e v) -> p (j e) v", e=2), ob,
                                               gn[:, 0, :].unsqueeze(2).to_broadcast([P, 8, N]), ALU.subtract), "centred")
                    if s == 9:
                        dve.wait_ge(sem("o_squared"), i)
                        link(dve.tensor_reduce(gn[:, 1, :], SQ[:, :, :].rearrange("p j (e v) -> p (j e) v", e=2), AX_X, ALU.add))
                        link(dve.tensor_scalar(gn[:, 1, :], gn[:, 1, :], 1.0 / N, GN_EPS, ALU.mult, ALU.add), "o_var")
                    if s == 11:
                        dve.wait_ge(sem("o_std"), i)
                        link(dve.reciprocal(gn[:, 3, :], gn[:, 2, :]))
                        oc = OC[:, :, :].rearrange("p j (e v) -> p (j e) v", e=2)
                        link(dve.tensor_tensor(oc, oc, gn[:, 3, :].unsqueeze(2).to_broadcast([P, 8, N]), ALU.mult), "o_normed")
                    if s == 14:
                        dve.wait_ge(sem("out_taken"), i)
                        sq = SQ[:, :, :].rearrange("p j t -> p (j t)")
                        link(dve.tensor_tensor(sq, sq, bonus_c[:, :], ALU.add))
                        link(dve.tensor_tensor(sq, sq, gate[:, :], ALU.mult), "y_ready")
                if (i, s) in POOL_STEPS:
                    pool_step(*POOL_STEPS[i, s])
                if s == 20 and i >= 0 and i < PAIRS:
                    link(dve.memset(Sbd[:, :], 0.0), "s_zero")

            per_slot(slot)
            def mod_section(m):
                dve.wait_ge(sem("ada_turned"), m + 1)
                for half in range(2):
                    link(dve.tensor_reduce(mod[:, 16 + 8 * m + 4 * half:20 + 8 * m + 4 * half], blk(bank[4 + half][:, :]), AX_X, ALU.add))
                link(dve.tensor_tensor(mod[:, 16 + 8 * m:24 + 8 * m], mod[:, 16 + 8 * m:24 + 8 * m],
                                       params[:, 16 + 8 * m:24 + 8 * m], ALU.add), "mod2")

            def ada_tile(tile):
                kt = tile % KT
                if kt == 0 and tile:
                    dve.wait_ge(sem("ada_turned"), tile // KT)
                for half in range(2):
                    cols = slice(half * S, (half + 1) * S)
                    dve.wait_ge(sem(f"ada2_in{half}"), 16 * (tile + 1))
                    if kt == 0:
                        link(dve.tensor_scalar(acc2[:, cols], ada2[:, cols], der(CS), None, ALU.mult), "ada2_used")
                    else:
                        link(dve.scalar_tensor_tensor(out=acc2[:, cols], in0=ada2[:, cols], scalar=der(CS + kt), in1=acc2[:, cols],
                                                      op0=ALU.mult, op1=ALU.add), "ada2_used")

            for g in range(GP):
                dve.wait_ge(sem("mp_hi_ready"), g + 1)
                link(dve.tensor_tensor(mp_lo[:, g, :], lnv[:, :], mp_hi[:, g, :].bitcast(F32), ALU.subtract), "mp_ready")
            for n in range(KT):
                if n in (3, 5, 7):
                    mod_section((n - 3) // 2)
                if 1 <= n < KT - 1:
                    ada_tile(4 * n - 4)
                    ada_tile(4 * n - 3)
                dve.wait_ge(sem("gated"), 2 * n + 2)
                dve.wait_ge(sem("w_used"), K_RU[n] + 1)
                link(dve.tensor_tensor(f2[:, :], f2[:, :], GATE_BANKS[n][2][:, :], ALU.mult), "ru_taken")
                if 1 <= n < KT - 1:
                    ada_tile(4 * n - 2)
                dve.wait_ge(sem("w_used"), K_PU[n] + 1)
                link(dve.tensor_tensor(f1[:, :], f1[:, :], GATE_BANKS[n][3][:, :], ALU.mult), "pu_taken")
                link(dve.tensor_tensor(f3[:, :], f1[:, :], f2[:, :], ALU.add), "mix_sum")
                if 1 <= n < KT - 1:
                    ada_tile(4 * n - 1)
                dve.wait_ge(sem("mixed_hi"), n + 1)
                link(dve.tensor_tensor(mix_lo[:, n, :], f3[:, :], mix_hi[:, n, :].bitcast(F32), ALU.subtract), "mixed")
            for tile in range(4 * KT - 8, 4 * KT - 4):
                ada_tile(tile)
            link(dve.tensor_scalar(mod[:, 16:24], mod[:, 16:24], 1.0, None, ALU.add))
            link(dve.tensor_scalar(mod[:, 32:40], mod[:, 32:40], 1.0, None, ALU.add))
            link(dve.tensor_scalar(small[:, 0:8], params[:, P + 12:P + 20], ALPHA, None, ALU.mult))
            link(dve.tensor_scalar(small[:, 8:16], params[:, P + 20:P + 28], ALPHA, None, ALU.mult))
            link(dve.tensor_tensor(small[:, 16:24], params[:, P + 20:P + 28], mod[:, 32:40], ALU.mult))
            link(dve.tensor_tensor(mod[:, 24:32], small[:, 16:24], mod[:, 24:32], ALU.add))
            link(dve.tensor_tensor(mod[:, 32:40], params[:, P + 12:P + 20], mod[:, 32:40], ALU.mult))
            m0, sum1, sum2 = f3, SUM1[:, :], SUM2[:, :]

            def add_square(n):
                dve.wait_ge(sem("ln1_squared"), n + 1)
                if n == 0:
                    link(dve.tensor_copy(sum2, f1[:, :]), "ln1_sq_used")
                else:
                    link(dve.tensor_tensor(sum2, sum2, (f1, f2)[n % 2][:, :], ALU.add), "ln1_sq_used")

            for n in range(KT):
                dve.wait_ge(sem("w_used"), K_OUT + n + 1)
                dve.wait_ge(sem("res_ready"), n + 1)
                link(dve.scalar_tensor_tensor(out=res[:, n, :], in0=OUT_BANKS[n % 4][:, :], scalar=mod[:, 16 + n:17 + n],
                                              in1=res[:, n, :], op0=ALU.mult, op1=ALU.add), "out_taken2")
                if n == 0:
                    dve.wait_ge(sem("ln1_m0"), 1)
                    link(dve.tensor_scalar(m0[:, :], bank[5][:, :], float(D // P), None, ALU.mult), "m0_taken")
                link(dve.tensor_tensor(res[:, n, :], res[:, n, :], m0[:, :], ALU.subtract), "ln1_centred")
                if n == 0:
                    link(dve.tensor_copy(sum1, res[:, 0, :]))
                else:
                    link(dve.tensor_tensor(sum1, sum1, res[:, n, :], ALU.add), "ln1_summed")
                    add_square(n - 1)
                if n < 4:
                    ada_tile(4 * KT - 4 + n)
                if n == 5:
                    mod_section(3)
                    link(dve.tensor_scalar(mod[:, 40:48], mod[:, 40:48], 1.0, None, ALU.add))
            add_square(KT - 1)
            dve.wait_ge(sem("ln1_sums"), 1)
            link(dve.tensor_copy(lnv[:, :], bank[4][:, :]))
            link(dve.tensor_tensor(f3[:, :], bank[4][:, :], lnv[:, :], ALU.mult))
            dve.wait_ge(sem("ln1_sums"), 2)
            link(dve.tensor_tensor(lnv[:, :], bank[5][:, :], f3[:, :], ALU.subtract))
            link(dve.tensor_scalar(lnv[:, :], lnv[:, :], 0.0, LN_EPS, ALU.max, ALU.add), "ln1_eps")

            def centre(f):
                link(dve.tensor_tensor(res[:, f, :], res[:, f, :], bank[4][:, :], ALU.subtract))

            for f in range(2):
                centre(f)
            dve.wait_ge(sem("ln1_std"), 1)
            link(dve.reciprocal(f3[:, :], lnv[:, :]))
            for f in range(KT):
                if f >= 2:
                    centre(f)
                link(dve.tensor_tensor(res[:, f, :], res[:, f, :], f3[:, :], ALU.mult), "ln1_normed")
                if f % 2:
                    dve.wait_ge(sem("h2_hi"), f)
                    link(dve.tensor_tensor(h_lo[:, f - 1, :], f1[:, :], h_hi[:, f - 1, :].bitcast(F32), ALU.subtract), "h2_lo_by_dve")

            PARTS = ((0, S), (S, D - P), (D - P, D))

            def statistics(part):
                a, b = PARTS[part]
                for j in range(TB):
                    link(dve.bn_stats(stat[:, 3 * j + part, :], xt2[:, j, a:b]))

            for q in range(NQ):
                for n in range(KT):
                    m = KT * q + n
                    dve.wait_ge(sem("relu"), m + 1)
                    r = (f1, f2)[m % 2]
                    link(dve.tensor_tensor(f3[:, :], r[:, :], r[:, :], ALU.mult))
                    dve.wait_ge(sem("hidden_hi"), m + 1)
                    link(dve.tensor_tensor(y_lo[:, n, :], f3[:, :], y_hi[:, n, :].bitcast(F32), ALU.subtract), "hidden")
                for n in range(KT):
                    k = K_FF + 2 * KT * q + KT + n
                    dve.wait_ge(sem("w_used"), k + 1)
                    dve.wait_ge(sem("res_scaled"), n + 1)
                    link(dve.scalar_tensor_tensor(out=res[:, n, :], in0=bank[k % 4][:, :], scalar=mod[:, 40 + n:41 + n],
                                                  in1=res[:, n, :], op0=ALU.mult, op1=ALU.add), "ff_taken")
                    if q == NQ - 1 and n == KT - 2:
                        dve.wait_ge(sem("out_tokens"), KT // 2)
                        statistics(0)
            dve.wait_ge(sem("out_tokens"), KT - 1)
            statistics(1)
            dve.wait_ge(sem("out_tokens"), KT)
            statistics(2)
            for j in range(TB):
                link(dve.bn_aggr(small[:, 20 + 2 * j:22 + 2 * j], stat[:, 3 * j:3 * j + 3, :]))
            mv = small[:, 20:28].rearrange("p (j two) -> p j two", two=2)
            link(dve.tensor_scalar(small[:, 28:32], mv[:, :, 1], LN_EPS, None, ALU.add), "ln2_eps")
            dve.wait_ge(sem("ln2_std"), 1)
            link(dve.reciprocal(small[:, 36:40], small[:, 32:36]))
            link(dve.scalar_tensor_tensor(out=small[:, 40:41], in0=small[:, 18 + 2 * TB:19 + 2 * TB], scalar=-1.0,
                                          in1=small[:, 35 + TB:36 + TB], op0=ALU.mult, op1=ALU.mult), "ln2_cols")
            dve.wait_ge(sem("ln2_in"), 32)
            for j in range(TB - 1):
                link(dve.scalar_tensor_tensor(out=xt2[:, j, :], in0=xt2[:, j, :], scalar=small[:, 20 + 2 * j:21 + 2 * j], in1=acc2[:, :],
                                              op0=ALU.subtract, op1=ALU.mult))
                link(dve.scalar_tensor_tensor(out=xt2[:, j, :], in0=xt2[:, j, :], scalar=small[:, 36 + j:37 + j], in1=ada2[:, :],
                                              op0=ALU.mult, op1=ALU.add), "out_ready")

        @block.tensor
        def _(pe):
            pe.wait_ge(sem("ident_ready"), 1)
            pe.wait_ge(sem("c_in"), 16)
            pe.transpose(bank[0][:, 2 * P:2 * P + KT], crow[:, :], ident[0:KT, 0:KT]).then_inc(sem("c_turned"), 1)
            pe.wait_ge(sem("consts_ready"), 1)

            def turn_x(f):
                if f >= 4:
                    pe.wait_ge(sem("h_f32"), f - 3)
                for j in range(TB):
                    mm = pe.transpose(bank[2 + f % 4][:, j * P:(j + 1) * P], xtok[:, j, f * P:(f + 1) * P], ident[:, :])
                mm.then_inc(sem("x_turned"), 1)

            pe.wait_ge(sem("x_in"), 16 * TB)
            for f in range(4):
                turn_x(f)
            pe.wait_ge(sem("params_in"), 16 * 15)
            pe.wait_ge(sem("c_cols"), 1)
            for tab in range(2):
                mm = pe.transpose(bank[0][:, tab * P:(tab + 1) * P], ptab[:, tab, :], ident[:, :])
            mm.then_inc(sem("param_cols"), 1)
            for half in range(2):
                pe.wait_ge(sem("ada_used"), KT * (half + 1))
                for f in range(KT):
                    mm = pe.matmul(bank[1][:, 8 * half + f:8 * half + f + 1], acc[:, half, f * P:(f + 1) * P],
                                   ones_col[:, :], start=True, stop=True)
            mm.then_inc(sem("mod_done"), 1)
            for f in range(4, KT):
                turn_x(f)

            def gemm(k, kts):
                width = chunk_cols[k][1]
                pe.wait_ge(sem("lo_ready"), k + 1)
                if k == 2:
                    pe.wait_ge(sem("h_f32"), 1)
                for kt in kts:
                    pe.wait_ge(sem(("h_lo_by_dve", "h_lo_by_pool")[kt % 2]), kt // 2 + 1)
                    terms = [(w_hi, h_hi), (w_hi, h_lo), (w_lo, h_hi)]
                    for m, (w, hx) in enumerate(terms):
                        mm = pe.matmul(in_bank(k)[0:width, :], w[k % RING][:, kt, 0:width], hx[:, kt, :],
                                       start=(kt == 0 and m == 0), stop=(kt == KT - 1 and m == 2))
                mm.then_inc(sem("w_used"), 1)

            G1_TAKEN = {"decay": ("decay_taken", 1), "aaa": ("aaa_taken", 1), "norm": ("norm_taken", 1), "tokA": ("tok_taken", 3, 1),
                        "tokBK0": ("tok_taken", 3, 2), "tokBK1": ("tok_taken", 3, 3), "tokV0": ("v_taken", 2, 1),
                        "tokV1": ("v_taken", 2, 2), "outT": ("out_taken", 1),
                        "gate": ("gate_taken", 1), "bonus": ("bonus_taken", 1)}

            def g1_free(job, n):
                at = g1_at[(job, n)]
                if at:
                    before, m = g1_jobs[at - 1]
                    name, per, *k = G1_TAKEN[before]
                    pe.wait_ge(sem(name), per * m + (k[0] if k else 1))

            for k in range(3):
                gemm(k, range(KT))

            def stage(e, i, s):
                name = STAGES[s]
                if s >= 2:
                    evacuated(pe, e, i, STAGES[s - 2])
                elif i >= 1:
                    evacuated(pe, e, i - 1, STAGES[NS + s - 2])
                dep = {"Q2": ["Q1"], "Q3": ["Q2"], "Q4": ["Q3"], "Q5": ["Q4"], "U1": ["Mak"], "U2": ["U1"], "U3": ["U2", "Q5"], "X1": ["U3"],
                       "Tr1": [], "Y1": ["Tr1"], "X2": ["Y1"], "Tr2": [], "Y2": ["Tr2"], "PT": ["Y2"], "AHT": []}
                for d in dep.get(name, []):
                    evacuated(pe, e, i, d)
                if name == "MabT":
                    pe.wait_ge(sem("prepared"), i + 1)
                if name == "Mab":
                    pe.wait_ge(sem("b_padded"), 2 * (i + 1))
                if name == "Mak":
                    pe.wait_ge(sem("k_padded"), 2 * (i + 1))
                if name == "Q1":
                    evacuated(pe, 1, i, "MabT")
                    pe.wait_ge(sem(f"pooled{e}"), 3 * i + 1)
                if name == "X1":
                    pe.wait_ge(sem(f"pooled{e}"), 3 * i + 2)
                if name == "X2":
                    pe.wait_ge(sem(f"pooled{e}"), 3 * i + 3)
                if name == "AHT":
                    pe.wait_ge(sem("tok_taken"), 3 * i + 1)
                b = stage_bank(e, NS * i + s)
                if name in PACKED:
                    if name in ("Mr0", "Mr1"):
                        for m in range(2):
                            c = 4 * (name == "Mr1") + 2 * e + m
                            ts = slice(c * C, (c + 1) * C)
                            for rows, tokens in ((slice(0, C), Bt), (slice(C, P), Kt)):
                                mm = pe.matmul(b[rows, m * P:(m + 1) * P], tokens[:, ts], Rpad[:, :, ts],
                                               start=True, stop=True, skip_group_check=True)
                        mm.then_inc(sem(f"multiplied{e}"), 1)
                        return
                    tokens, both = {"MabT": (Bt, Apad), "Mab": (At, Bpad), "Mak": (At, Kpad)}[name]
                    for m in range(4):
                        j, z = 2 * e + m // 2, m % 2
                        ts = slice(j * P + z * C, j * P + (z + 1) * C)
                        mm = pe.matmul(b[z * C:(z + 1) * C, (m // 2) * P:(m // 2 + 1) * P], tokens[:, ts], both[:, :, ts],
                                       start=True, stop=True, skip_group_check=True)
                    mm.then_inc(sem(f"multiplied{e}"), 1)
                    return
                if name == "PT":
                    for m in range(2 * TB):
                        j, z = m // 2, m % 2
                        mm = pe.matmul(b[C:P, m * C:(m + 1) * C], MAK[:, j, e, :], TT[e][:, j, z * C:(z + 1) * C],
                                       start=True, stop=True, skip_group_check=True)
                    mm.then_inc(sem(f"multiplied{e}"), 1)
                    return
                for j in range(TB):
                    tb = slice(j * P, (j + 1) * P)
                    o = b[:, tb]
                    if name in ("Q2", "Q4", "Tr1", "Tr2"):
                        src = {"Q2": A1, "Q4": A0}.get(name, TT)
                        mm = pe.transpose(o, src[e][:, j, :], ident[:, :])
                        continue
                    if name == "AHT":
                        o = b[N * e:N * e + N, tb]
                    lhs, rhs = {
                        "Q1": (A0T[e][:, j, :], A0[e][:, j, :]), 
                        "Q3": (A1T[e][:, j, :], A1[e][:, j, :]),
                        "U1": (A1[e][:, j, :], TT[e][:, j, :]), "Q5": (A0T[e][:, j, :], A0[e][:, j, :]),
                        "U2": (A0[e][:, j, :], TT[e][:, j, :]), "U3": (A1[e][:, j, :], TT[e][:, j, :]),
                        "X1": (A0[e][:, j, :], TT[e][:, j, :]), "X2": (A0[e][:, j, :], TT[e][:, j, :]),
                        "Y1": (A1[e][:, j, :], A1T[e][:, j, :]), "Y2": (A1[e][:, j, :], A1T[e][:, j, :]),
                        "AHT": (Atok[:, j, N * e:N * e + N], TT[e][:, j, :]),
                    }[name]
                    mm = pe.matmul(o, lhs, rhs, start=True, stop=True)
                mm.then_inc(sem(f"multiplied{e}"), 1)

            def chain_sa(i, c):
                j, z = c // 2, c % 2
                if c == 0:
                    pe.wait_ge(sem("s_zero"), i + 1)
                    evacuated(pe, 0, i, "AHT")
                    evacuated(pe, 1, i, "AHT")
                    pe.wait_ge(sem("v_taken"), 2 * i + 2)
                if NCH * i + c:
                    pe.wait_ge(sem("s_taken"), NCH * i + c)
                pe.matmul(CH[0:C, 0:P], AHT[:, j, C * z:C * z + C], Sbd[:, :], start=True, stop=False, skip_group_check=True)
                for e in range(2):
                    mm = pe.matmul(CH[0:C, N * e:N * e + N], PT[e][C:P, c, :], SV[C:P, c, N * e:N * e + N],
                                   start=False, stop=(e == 1), skip_group_check=True)
                mm.then_inc(sem("sa_done"), 1)

            def chain_so(i, c):
                j, z = c // 2, c % 2
                rows, cols = slice(C * z, C * z + C), slice(c * C, (c + 1) * C)
                tb = slice(j * P, (j + 1) * P)
                pe.wait_ge(sem("sa_taken"), NCH * i + c + 1)
                pe.matmul(CH[:, 2 * P:3 * P], BK[:, c, :], SV[:, c, :], start=True, stop=True,
                          skip_group_check=True).then_inc(sem("state_done"), 1)
                if c == 0 and i >= 1:
                    pe.wait_ge(sem("centred"), i)
                pe.matmul(OB[rows, tb], Rc[:, cols], Sbd[:, :], start=True, stop=False, skip_group_check=True)
                for e in range(2):
                    mm = pe.matmul(OB[rows, j * P + N * e:j * P + N * e + N], MR[:, c, e, :], SV[:, c, N * e:N * e + N],
                                   start=False, stop=(e == 1), skip_group_check=True)
                mm.then_inc(sem("so_done"), 1)

            def slot(i, s):
                n = i + 1
                early = s < 3
                if i >= 1 and s < NCH and not early:
                    chain_sa(i - 1, s)
                if 0 <= i < PAIRS:
                    for e in range(2):
                        stage(e, i, s)
                if i >= 1 and s < NCH and early:
                    chain_sa(i - 1, s)
                    if i < PAIRS and 3 + 3 * n + s // 6 < FIRST_B:
                        gemm_piece(3 + 3 * n + s // 6, s % 6)
                if i == PAIRS and s < NCH:
                    late_piece(9 * s, 5)
                if i >= 1 and s < NCH:
                    chain_so(i - 1, s)
                if n < PAIRS:
                    if s == 4:
                        pe.wait_ge(sem("lup_in"), 32 * (n + 1))
                        pe.wait_ge(sem("lora_ready"), 3)
                        g1_free("decay", n)
                        pe.matmul(G1[:, :], lup[0:DW, 0, :], xwa[0:DW, :], start=True, stop=True).then_inc(sem("g1_done"), 1)
                    if s == 5:
                        g1_free("aaa", n)
                        pe.matmul(G1[:, :], lup[DW:P, 0, :], xwa[DW:P, :], start=True, stop=True).then_inc(sem("g1_done"), 1)
                    if s == 8:
                        g1_free("norm", n)
                        pe.wait_ge(sem("squared"), n + 1)
                        pe.matmul(G1[:, :], ones_head[:, :], t1[:, :], start=True, stop=True).then_inc(sem("g1_done"), 1)
                    if s == 18:
                        g1_free("bonus", n)
                        pe.wait_ge(sem("rk_ready"), n + 1)
                        pe.matmul(G1[:, :], ones_head[:, :], xk[:, :], start=True, stop=True).then_inc(sem("g1_done"), 1)
                if 0 <= i < PAIRS and s in (9, 10, 11, 12, 14):
                    job = {9: "tokA", 10: "tokBK0", 11: "tokBK1", 12: "tokV0", 14: "tokV1"}[s]
                    g1_free(job, i)
                    for m in range(TB):
                        o = slice(m * P, (m + 1) * P)
                        if job == "tokA":
                            mm = pe.transpose(G1[:, o], At[:, o], ident[:, :])
                            continue
                        c = 4 * int(job[-1]) + m
                        ts = slice(c * C, (c + 1) * C)
                        if job[:-1] == "tokBK":
                            pe.transpose(G1[0:C, o], Bt[:, ts], ident[:, :])
                        mm = pe.matmul(G1[C:P, o], (xv if job[:-1] == "tokV" else Kt)[:, ts], ident[:, :], start=True, stop=True,
                                       skip_group_check=True)
                    mm.then_inc(sem("g1_done"), 1)
                if i >= 1 and s == 13:
                    g1_free("outT", i - 1)
                    pe.wait_ge(sem("o_normed"), i)
                    for j in range(TB):
                        mm = pe.transpose(G1[:, j * P:(j + 1) * P], OC[:, j, :], ident[:, :])
                    mm.then_inc(sem("g1_done"), 1)
                if 0 <= i < PAIRS and s == 15:
                    g1_free("gate", i)
                    pe.wait_ge(sem("gup_in"), 32 * (i + 1))
                    pe.matmul(G1[:, :], lup[:, 1, :], xg0[:, :], start=True, stop=False)
                    pe.matmul(G1[:, :], lup[0:DG1, 2, :], xg1[:, :], start=False, stop=True).then_inc(sem("g1_done"), 1)
                if i == PAIRS:
                    if s in (8, 14):
                        late_piece(72 + 24 * (s == 14), 24)
                    elif s < NCH:
                        late_piece(9 * s + 5, 4)
                elif s < 18 and 3 + 3 * n + s // 6 < FIRST_B and not (early and i >= 1):
                    gemm_piece(3 + 3 * n + s // 6, s % 6)

            LATE = [G0] + GATE_BANKS[0][:2] + GATE_BANKS[1][:2]

            def late_piece(first, count):
                for at in range(first, first + count):
                    k, m = FIRST_B - 1 + at // 24, at % 24
                    if m == 0:
                        pe.wait_ge(sem("lo_ready"), k + 1)
                    if at == 0:
                        pe.wait_ge(sem("pool_in"), GP - 1)
                    if at == 24:
                        for e in range(2):
                            evacuated(pe, e, PAIRS - 1, "PT")
                            evacuated(pe, e, PAIRS - 1, "AHT")
                    kt, term = m // 3, m % 3
                    w, hx = ((w_hi, h_hi), (w_hi, h_lo), (w_lo, h_hi))[term]
                    mm = pe.matmul(LATE[at // 24][:, :], w[slot_of(k)][:, kt, :], hx[:, kt, :], start=(m == 0), stop=(m == 23))
                    if m == 23:
                        mm.then_inc(sem("w_used"), 1)

            def gemm_piece(k, part):
                if part == 0:
                    pe.wait_ge(sem("lo_ready"), k + 1)
                    if k > NCHUNK:
                        pe.wait_ge(sem("pool_in"), k - NCHUNK)
                    elif k >= len(IN_BANKS):
                        pe.wait_ge(sem("shifted"), k)
                    else:
                        pe.wait_ge(sem("h_f32"), KT)
                for m in range(4 * part, 4 * part + 4):
                    kt, term = m // 3, m % 3
                    w, hx = ((w_hi, h_hi), (w_hi, h_lo), (w_lo, h_hi))[term]
                    mm = pe.matmul(in_bank(k)[:, :], w[k % RING][:, kt, :], hx[:, kt, :], start=(m == 0), stop=(m == 23))
                if part == 5:
                    mm.then_inc(sem("w_used"), 1)

            per_slot(slot)
            def turn_back(n):
                pe.wait_ge(sem("ff_taken"), KT * (NQ - 1) + n + 1)
                if n >= 2:
                    pe.wait_ge(sem("out_tokens"), n - 1)
                for j in range(TB):
                    mm = pe.transpose(bank[4 + n % 2][:, j * P:(j + 1) * P], res[:, n, j * P:(j + 1) * P], ident[:, :])
                mm.then_inc(sem("turned_back"), 1)

            def product(k, o, hi, lo, free, ready=None):
                kts = chunks[k][0].shape[1]
                pe.wait_ge(sem("lo_ready"), k + 1)
                free()
                for kt in range(kts):
                    if ready:
                        ready(kt)
                    for m, (w, hx) in enumerate(((w_hi, hi), (w_hi, lo), (w_lo, hi))):
                        mm = pe.matmul(o, w[chunks[k][1]][:, kt, :], hx[:, kt, :], start=(kt == 0 and m == 0),
                                       stop=(kt == kts - 1 and m == 2))
                mm.then_inc(sem("w_used"), 1)

            def taken(name, n):
                return lambda: pe.wait_ge(sem(name), n) if n > 0 else None

            def turn_section(m):
                pe.wait_ge(sem("ada2_used"), 2 * KT * (m + 1))
                if m:
                    pe.wait_ge(sem("mod2"), m)
                else:
                    pe.wait_ge(sem("gated"), 4)
                if m == 3:
                    pe.wait_ge(sem("m0_taken"), 1)
                for f in range(KT):
                    mm = pe.transpose(bank[4 + f // 4][:, f % 4 * P:(f % 4 + 1) * P], acc2[:, f * P:(f + 1) * P], ident[:, :])
                mm.then_inc(sem("ada_turned"), 1)

            def gate_free(n, name, per, at):
                last = 0 if n == 2 else n - 1
                return taken(name, per * last + at + 1) if n >= 2 else lambda: None

            def rwkv_up(n):
                product(K_RU[n], GATE_BANKS[n][2][:, :], y_hi, y_lo, gate_free(n, "ru_taken", 1, 0))

            def pool_up(n):
                product(K_PU[n], GATE_BANKS[n][3][:, :], mp_hi, mp_lo, gate_free(n, "pu_taken", 1, 0),
                        lambda kt: pe.wait_ge(sem("mp_ready"), kt + 1))

            pe.wait_ge(sem("y_lo_ready"), PAIRS)
            rwkv_up(0)
            pe.wait_ge(sem("wmix_in"), 16 * GP)
            for g in range(GP):
                pe.wait_ge(sem("pooled_up"), g + 1)
                if g >= 2:
                    pe.wait_ge(sem("pool_scaled"), g - 1)
                pe.matmul((G0, CH)[g % 2][:, :], wmix[:, g, :], UP[g][:, :], start=True, stop=True).then_inc(sem("pool_mixed"), 1)
            rwkv_up(1)
            pe.wait_ge(sem("pool_scaled"), GP)
            pool_up(0)
            pool_up(1)
            for n in range(2, KT):
                product(K_GP[n], GATE_BANKS[n][0][:, :], h_hi, h_lo, gate_free(n, "gated", 2, 0))
                product(K_GR[n], GATE_BANKS[n][1][:, :], h_hi, h_lo, gate_free(n, "gated", 2, 1))
                if n in (3, 5, 7):
                    turn_section((n - 3) // 2)
                rwkv_up(n)
                pool_up(n)

            for n in range(KT):
                for f in {2: (0, 1), 3: (2,), 4: (3,), 5: (4,), 6: (5,), 7: (6, 7)}.get(n, ()):
                    pe.wait_ge(sem("x_again"), 16 * TB)
                    if f >= 2:
                        pe.wait_ge(sem("res_ready"), f - 1)
                    for j in range(TB):
                        mm = pe.transpose(bank[6 + f % 2][:, j * P:(j + 1) * P], x_again[:, j, f * P:(f + 1) * P], ident[:, :])
                    mm.then_inc(sem("x_turned2"), 1)

                def free(n=n):
                    if n < 2:
                        pe.wait_ge(sem("gated"), 2 * KT)
                    elif n < 4:
                        pe.wait_ge(sem("pu_taken"), KT)
                    else:
                        pe.wait_ge(sem("out_taken2"), n - 3)
                product(K_OUT + n, OUT_BANKS[n % 4][:, :], mix_hi, mix_lo, free,
                        (lambda kt: pe.wait_ge(sem("mixed"), kt + 1)) if n == 0 else None)
                if n == 5:
                    turn_section(3)
                if n == 2:
                    pe.wait_ge(sem("mod2"), 3)
                    pe.wait_ge(sem("out_taken2"), 1)
                    pe.matmul(bank[5][:, :], ones_all[:, :], res[:, 0, :], start=True, stop=True).then_inc(sem("ln1_m0"), 1)
            pe.wait_ge(sem("ln1_summed"), KT - 1)
            pe.wait_ge(sem("mod2"), 4)
            pe.matmul(bank[4][:, :], ones_all[:, :], SUM1[:, :], start=True, stop=True).then_inc(sem("ln1_sums"), 1)
            pe.wait_ge(sem("ln1_sq_used"), KT)
            pe.matmul(bank[5][:, :], ones_all[:, :], SUM2[:, :], start=True, stop=True).then_inc(sem("ln1_sums"), 1)
            for q in range(NQ):
                for n in range(KT):
                    k = K_FF + 2 * KT * q + n
                    def free(q=q, n=n):
                        if n >= 4:
                            pe.wait_ge(sem("relu"), KT * q + n - 3)
                        elif q:
                            pe.wait_ge(sem("ff_taken"), KT * (q - 1) + KT + n - 3)
                    product(k, bank[k % 4][:, :], h_hi, h_lo, free, (lambda kt: pe.wait_ge(sem(("h2_lo_by_dve", "h2_lo_by_pool")[kt % 2]), kt // 2 + 1)) if q + n == 0 else None)
                for n in range(KT):
                    k = K_FF + 2 * KT * q + KT + n
                    def free(q=q, n=n):
                        if n >= 4:
                            pe.wait_ge(sem("ff_taken"), KT * q + n - 3)
                        else:
                            pe.wait_ge(sem("relu"), KT * q + KT + n - 3)
                    product(k, bank[k % 4][:, :], y_hi, y_lo, free,
                            (lambda kt, q=q: pe.wait_ge(sem("hidden"), KT * q + kt + 1)) if n == 0 else None)
                    if q == NQ - 1 and n >= 1:
                        turn_back(n - 1)
            turn_back(KT - 1)


_INS = ['x', 'c', 'w_ada', 'b_ada', 'w_in', 'mu_shift', 'pool_mix', 'pool_scale', 'w_pool_up', 'w0', 'w_decay_up', 'a0',
        'w_aaa_up', 'w_gate_up', 'k_k', 'k_a', 'r_k', 'gn_g', 'gn_b', 'w_rwkv_up', 'w_out', 'ln1_g', 'ln1_b', 'w_ff1',
        'w_ff2', 'ln2_g', 'ln2_b']
_OUTS = [((1, 512, 1024), 'float32')]


def kernel(**inputs):
    import numpy as _np
    import concourse.bacc as _bacc
    from concourse import mybir as _mybir
    from concourse.bass_utils import run_bass_kernel_spmd as _run

    nc = _bacc.Bacc("TRN2", target_bir_lowering=False, num_devices=1)
    arrays, args = {}, []
    for name in _INS:
        a = _np.ascontiguousarray(inputs[name])
        arrays[f"in_{name}_dram"] = a
        args.append(nc.dram_tensor(f"in_{name}_dram", a.shape, _mybir.dt.from_np(a.dtype), kind="ExternalInput").ap())
    for i, (shape, dtype) in enumerate(_OUTS):
        dt = _mybir.dt.from_np(_np.dtype(dtype))
        args.append(nc.dram_tensor(f"out_{i}_dram", shape, dt, kind="ExternalOutput").ap())
    build(nc, *args)
    r = _run(nc, [arrays], core_ids=[0])
    got = tuple(r.results[0][f"out_{i}_dram"] for i in range(len(_OUTS)))
    return got[0]
```

```python
from contextlib import ExitStack

import concourse.bass as bass
from concourse import mybir

P = 128
ALU = mybir.AluOpType
ACT = mybir.ActivationFunctionType
AX_X = mybir.AxisListType.X
F32 = mybir.dt.float32
F32R = mybir.dt.float32r


def build(nc, x, c, w_ada, b_ada, w_in, mu_shift, pool_mix, pool_scale, w_pool_up, w0, w_decay_up, a0,
          w_aaa_up, w_gate_up, k_k, k_a, r_k, gn_g, gn_b, w_rwkv_up, w_out, ln1_g, ln1_b, w_ff1, w_ff2,
          ln2_g, ln2_b, out):
    S, D = x.shape[1], x.shape[2]
    KT = D // P
    TB = S // P
    H = r_k.shape[1]
    N = r_k.shape[2]
    PAIRS = H * N // P
    C = 64
    NCH = S // C
    DP = pool_scale.shape[1]
    DW, DG = w_decay_up.shape[1], w_gate_up.shape[1]
    DG1 = DG - P
    COL_R = DP
    COL_K, COL_V = COL_R + D, COL_R + 2 * D
    COL_WA = COL_R + 3 * D
    COL_G0 = COL_WA + 2 * DW
    COL_G1 = COL_G0 + P
    EXPM = float(2.718281828459045 ** -0.5)
    ALPHA = 2.0 ** 0.25
    GN_EPS, LN_EPS = 64e-5, 1e-5
    SHIFT_TAIL = COL_G1 + DG1 - DP - 26 * P

    rows1 = dict(b_ada=0, mu=48, w0=74, a0=82, k_k=90, k_a=98, r_k=106, gn_g=114)
    rows2 = dict(gn_b=0, pool_scale=8, ln1_g=12, ln1_b=20, ln2_g=28, ln2_b=36, mu_tail=44)
    NP1, NP2 = 122, 45

    ctx = ExitStack()
    with ctx:
        def sb(name, shape, dt=F32):
            return ctx.enter_context(nc.sbuf_tensor(name, shape, dt))

        sems = {}

        def sem(name):
            if name not in sems:
                sems[name] = ctx.enter_context(nc.semaphore(name))
            return sems[name]

        over = ExitStack()
        x_again = over.enter_context(nc.sbuf_tensor("x_again", [P, TB, D], F32))
        over.close()
        h_hi, h_lo = sb("h_hi", [P, KT, S], F32R), sb("h_lo", [P, KT, S], F32R)
        y_hi, y_lo = sb("y_hi", [P, KT, S], F32R), sb("y_lo", [P, KT, S], F32R)
        RING = 2
        w_raw = [sb(f"w_raw{s}", [P, KT, P]) for s in range(RING)]
        w_hi = [sb(f"w_hi{s}", [P, KT, P], F32R) for s in range(RING)]
        w_lo = [sb(f"w_lo{s}", [P, KT, P], F32R) for s in range(RING)]
        lup = sb("lup", [P, 3, P])
        ident = sb("ident", [P, P])
        ones_all = sb("ones_all", [P, P])
        ones_col = sb("ones_col", [P, 1])
        ones_head = sb("ones_head", [P, P])
        params = sb("params", [P, 2 * P])
        p2 = P
        derived = sb("derived", [P, 96])
        mod = sb("mod", [P, 48])
        OMM, OMKA, HW0, HA0, CCOL, CS = 0, 27, 35, 43, 51, 59
        HM = 67
        rec = sb("rec", [P, 16])
        xk, xr, aa, t1 = (sb(n, [P, S]) for n in ("xk", "xr", "aa", "t1"))
        wk = ExitStack()

        def wb(name, shape, dt=F32):
            return wk.enter_context(nc.sbuf_tensor(name, shape, dt))

        m16T = wb("m16T", [P, P])
        m16 = wb("m16", [P, P])
        m32 = wb("m32", [P, P])
        m64 = wb("m64", [P, P])
        mlow = wb("mlow", [P, C])
        mupi = wb("mupi", [P, C])
        scanm = wb("scanm", [P, S])
        xwa, xg0, xg1 = wb("xwa", [P, S]), wb("xg0", [P, S]), wb("xg1", [DG1, S])
        xv, sg, t2, t3, t4 = (wb(n, [P, S]) for n in ("xv", "sg", "t2", "t3", "t4"))
        At, Bt, Kt, Rf = (wb(n, [P, S]) for n in ("At", "Bt", "Kt", "Rf"))
        Apad, Rpad, Bpad, Kpad = (wb(n, [P, 2, S]) for n in ("Apad", "Rpad", "Bpad", "Kpad"))
        DC = wb("DC", [P, NCH])
        Rc, DCc, bonus_c = wb("Rc", [P, S]), wb("DCc", [P, NCH]), wb("bonus_c", [P, S])
        A0, A0T, A1, A1T, TT = ([wb(f"{n}{e}", [P, TB, P]) for e in range(2)] for n in ("A0", "A0T", "A1", "A1T", "TT"))
        MAB, MAK = (wb(n, [P, TB, 2, C]) for n in ("MAB", "MAK"))
        AHT, Atok = (wb(n, [P, TB, P]) for n in ("AHT", "Atok"))
        SV = wb("SV", [P, NCH, P])
        BK = wb("BK", [P, NCH, P])
        MR = wb("MR", [P, NCH, 2, C])
        PT = [wb(f"PT{e}", [P, NCH, C]) for e in range(2)]
        bonus, gate = wb("bonus", [P, S]), wb("gate", [P, S])
        OC, SQ = wb("OC", [P, TB, P]), wb("SQ", [P, TB, P])
        Sbd, Stmp = wb("Sbd", [P, P]), wb("Stmp", [P, P])
        gn = wb("gn", [P, 4, 8])
        wk.close()
        st = ExitStack()
        NADA = 10

        def stb(name, shape, dt=F32):
            return st.enter_context(nc.sbuf_tensor(name, shape, dt))

        skip = stb("skip", [P, 6 * P + S])
        xtok = stb("xtok", [P, TB, D])
        ptab = stb("ptab", [P, 2, P])
        ada = [stb(f"ada{s}", [P, D]) for s in range(NADA)]
        acc = stb("acc", [P, 2, D])
        hf = [stb(f"hf{s}", [P, S]) for s in range(4)]
        crow = stb("crow", [KT, P])
        st.close()
        pt = ExitStack()

        def pb(name, shape, dt=F32):
            return pt.enter_context(nc.sbuf_tensor(name, shape, dt))

        for s in (2, 3):
            w_raw.append(pb(f"w_raw{s}", [P, KT, P]))
            w_hi.append(pb(f"w_hi{s}", [P, KT, P], F32R))
            w_lo.append(pb(f"w_lo{s}", [P, KT, P], F32R))
        mix_hi, mix_lo = pb("mix_hi", [P, KT, S], F32R), pb("mix_lo", [P, KT, S], F32R)
        res = pb("res", [P, KT, S])
        GP = DP // P
        wmix = pb("wmix", [P, GP, P])
        f1, f2, f3 = (pb(n, [P, S]) for n in ("f1", "f2", "f3"))
        lnv = pb("lnv", [P, S])
        small = pb("small", [P, 64])
        stat = pb("stat", [P, 3 * TB, 6])
        ada2 = pb("ada_late", [P, D])
        acc2 = pb("acc2", [P, D])
        tail = ExitStack()
        mp_hi, mp_lo = (tail.enter_context(nc.sbuf_tensor(n, [P, GP, S], F32R)) for n in ("mp_hi", "mp_lo"))
        tail.close()
        xt2 = pb("xt2", [P, TB, D])
        pt.close()

        bank = [ctx.enter_context(nc.psum_tensor(f"bank{b}", [P, 512], F32)) for b in range(8)]
        G0, G1, CH, OB = bank[0], bank[1], bank[6], bank[7]
        GATE_BANKS = [[bank[b] for b in ((4, 5, 7, 6) if n == 1 else (2, 3, 1, 0))] for n in range(KT)]
        OUT_BANKS = [bank[2], bank[3], bank[0], bank[1]]
        IN_BANKS = [bank[6], bank[7], bank[1], G0, bank[2], bank[3]]

        def in_bank(k):
            return IN_BANKS[k] if k < len(IN_BANKS) else G0

        def stage_bank(e, s_global):
            return bank[2 + 2 * e + s_global % 2]

        def blk(ap):
            return ap.rearrange("p (j t) -> p j t", j=TB)

        def halves(t, e):
            return t[:, 2 * e:2 * e + 2, :, :].rearrange("p j h c -> p (j h) c")

        def both_chunks(t, h):
            return t[:, :, h, :].unsqueeze(2).to_broadcast([P, TB, 2, C])

        def as_chunks(m):
            return m.rearrange("p j (z c) -> p j z c", z=2)

        def chunk_masks(m, blocks):
            return m[:, :].rearrange("p (z c) -> p z c", z=2).unsqueeze(1).to_broadcast([P, blocks, 2, C])

        def over_blocks(mask):
            return mask[:, :].unsqueeze(1).to_broadcast([P, TB, P])

        STAGES = ["MabT", "Mab", "Mak", "Q1", "Q2", "Q3", "Q4", "U1", "Q5", "Mr0", "Mr1", "U2", "U3",
                  "X1", "Tr1", "Y1", "X2", "Tr2", "Y2", "PT", "AHT"]
        NS = len(STAGES)
        BY_DVE = {"MabT", "Mab", "Mak", "Mr0", "Mr1", "U1", "U2", "U3", "Y1", "Y2"}
        ND = len(BY_DVE)
        PACKED = ("MabT", "Mab", "Mak", "Mr0", "Mr1")
        NA = NS - ND

        def evacuated(eng, e, i, name):
            at = STAGES.index(name)
            n = sum((m in BY_DVE) == (name in BY_DVE) for m in STAGES[:at + 1])
            if name in BY_DVE:
                eng.wait_ge(sem(f"taken_by_dve{e}"), due(f"taken_by_dve{e}", ND * i + n))
            else:
                eng.wait_ge(sem(f"taken_by_act{e}"), due(f"taken_by_act{e}", NA * i + n))

        chunk_cols = [(COL_WA, P), (COL_G0, P), (COL_G1, DG1)]
        for n in range(PAIRS):
            chunk_cols += [(col + n * P, P) for col in (COL_K, COL_R, COL_V)]
        NCHUNK = len(chunk_cols)
        def w_cols(w, c0, width=P, r0=0, kts=KT):
            return w[0, r0:r0 + kts * P, c0:c0 + width].rearrange("(kt p) n -> p kt n", p=P)

        chunks = [(w_cols(w_in, c0, width), k % 2) for k, (c0, width) in enumerate(chunk_cols)]
        for g in range(GP):
            chunks.append((w_cols(w_in, g * P), len(chunks) % 2))
        FIRST_B = len(chunks)
        COL_GP = COL_G1 + DG1
        K_GP, K_GR, K_RU, K_PU = ([FIRST_B + at for at in first] + [FIRST_B + 4 * n + m for n in range(2, KT)]
                                  for m, first in enumerate(((0, 2), (1, 3), (4, 5), (6, 7))))
        gate_src = {}
        for n in range(KT):
            gate_src[K_GP[n]] = w_cols(w_in, COL_GP + n * P)
            gate_src[K_GR[n]] = w_cols(w_in, COL_GP + D + n * P)
            gate_src[K_RU[n]] = w_cols(w_rwkv_up, n * P)
            gate_src[K_PU[n]] = w_cols(w_pool_up, n * P, kts=GP)
        K_WIDE = FIRST_B + 6

        def slot_of(k):
            return k % 2 if k < K_WIDE else (2, 3, 1, 0)[(k - K_WIDE) % 4]

        for k in range(FIRST_B, FIRST_B + 4 * KT):
            chunks.append((gate_src[k], slot_of(k)))
        K_OUT = len(chunks)
        for n in range(KT):
            chunks.append((w_cols(w_out, n * P), slot_of(len(chunks))))
        K_FF = len(chunks)
        K_H2 = K_FF + 3
        DFF = w_ff1.shape[2]
        NQ = DFF // D
        for q in range(NQ):
            for n in range(KT):
                chunks.append((w_cols(w_ff1, (q * KT + n) * P), slot_of(len(chunks))))
            for n in range(KT):
                chunks.append((w_cols(w_ff2, n * P, r0=q * D), slot_of(len(chunks))))
        NALL = len(chunks)
        before, uses, seen = [], [], {}
        for k, (_, slot) in enumerate(chunks):
            before.append(seen[slot][0] if slot in seen else None)
            uses.append(seen[slot][1] + 1 if slot in seen else 1)
            seen[slot] = (k, uses[-1])

        g1_jobs = []
        for i in range(-1, PAIRS + 1):
            for s, job in ((4, "decay"), (5, "aaa"), (8, "norm"), (9, "tokA"), (10, "tokBK0"), (11, "tokBK1"),
                           (12, "tokV0"), (13, "outT"), (14, "tokV1"), (15, "gate"), (18, "bonus")):
                n = i + {"t": 0, "g": 0, "o": -1}.get(job[0], 1)
                if 0 <= n < PAIRS:
                    g1_jobs.append((job, n))
        g1_at = {key: k for k, key in enumerate(g1_jobs)}

        POOLED_AT = [(PAIRS, 6), (PAIRS, 12), (PAIRS, 18), (PAIRS + 1, 3)]
        POOL_STEPS = {}
        for g, (i, first) in enumerate(((PAIRS - 1, 7), (PAIRS - 1, 13), (PAIRS - 1, 19), (PAIRS, 3))):
            for step in range(g + 2):
                at = i * NS + first + step
                POOL_STEPS[at // NS, at % NS] = (g, step)
        SPLIT_AT = {(PAIRS, slot): FIRST_B + m for m, slot in enumerate((0, 3, 6, 8, 14))}
        UP = [xk, xr, aa, t1]
        SUM1, SUM2 = UP[0], UP[1]

        FIRST, ROUND = 1, 2
        ROUNDS = (PAIRS - 2) // ROUND
        ahead = [0]

        RATE = {"hi_ready": 3, "lo_ready": 3, "w_used": 3, "w_in0": 24, "w_in1": 24, "kept": 3, "shifted": 3,
                "g1_done": len(g1_jobs) // PAIRS, "tok_taken": 3, "v_taken": 2, "lup_in": 32, "gup_in": 32,
                "carried": 2, "b_padded": 2, "k_padded": 2}
        for e in range(2):
            RATE.update({f"multiplied{e}": NS, f"taken_by_act{e}": NA, f"taken_by_dve{e}": ND, f"pooled{e}": 3})
        for name in ("sa_done", "sa_taken", "so_done", "s_taken", "state_done"):
            RATE[name] = NCH
        for name in ("decay_taken", "aaa_taken", "norm_taken", "out_taken", "gate_taken", "bonus_taken", "squared", "rk_ready",
                     "scanned", "before_sum", "exps", "b_made", "prepared", "bonus_carried", "centred", "o_squared", "o_var",
                     "o_std", "o_normed", "y_ready", "y_hi_ready", "y_lo_ready", "s_zero"):
            RATE[name] = 1
        RATE.update({"act_step": 2, "dve_step": 35})

        def due(name, value):
            if isinstance(ahead[0], int) or name not in RATE:
                return value
            return ahead[0] * RATE[name] + value

        def of_pair(table, idx, rows=P):
            return table[0:rows, idx:idx + 1] if isinstance(ahead[0], int) else table[0:rows, bass.ds(ahead[0] + idx, 1)]

        def pair_block(t, i):
            return t[:, i, :] if isinstance(ahead[0], int) else t[:, bass.ds(ahead[0] + i, 1), :].rearrange("p o s -> p (o s)")

        def per_slot(eng, emit, counts):
            for i in (-1, 0):
                for s in range(NS):
                    emit(i, s)
            with eng.Fori(0, ROUND * ROUNDS, ROUND) as pairs:
                ahead[0] = pairs
                for i in range(FIRST, FIRST + ROUND):
                    for s in range(NS):
                        emit(i, s)
            ahead[0] = 0
            for name in counts:
                if name in RATE:
                    counts[name] += RATE[name] * ROUND * (ROUNDS - 1)
            for i in (PAIRS - 1, PAIRS):
                for s in range(NS):
                    emit(i, s)

        block = ctx.enter_context(nc.Block())

        def col(idx):
            return params[:, idx:idx + 1]

        def der(idx):
            return derived[:, idx:idx + 1]

        def part_of(k, buf):
            src, slot = chunks[k]
            return buf[slot][:, 0:src.shape[1], 0:src.shape[2]]

        def load_chunk(sp, k):
            src, slot = chunks[k]
            if before[k] is not None:
                sp.wait_ge(sem("lo_ready"), before[k] + 1)
            sp.dma_start(part_of(k, w_raw), src).then_inc(sem(f"w_in{slot}"), 16)

        def lup_next(sp, n):
            if n >= 1:
                sp.wait_ge(sem("g1_done"), g1_at[("aaa", n - 1)] + 1)
            cols = slice(n * P, (n + 1) * P)
            sp.dma_start(lup[0:DW, 0, :], w_decay_up[0, :, cols]).then_inc(sem("lup_in"), 16)
            sp.dma_start(lup[DW:P, 0, :], w_aaa_up[0, :, cols]).then_inc(sem("lup_in"), 16)

        def gup_next(sp, n):
            if n >= 1:
                sp.wait_ge(sem("g1_done"), g1_at[("gate", n - 1)] + 1)
            cols = slice(n * P, (n + 1) * P)
            sp.dma_start(lup[:, 1, :], w_gate_up[0, 0:P, cols]).then_inc(sem("gup_in"), 16)
            sp.dma_start(lup[0:DG1, 2, :], w_gate_up[0, P:DG, cols]).then_inc(sem("gup_in"), 16)

        NFF = 2 * KT

        def loop_link(eng, counts, q, per, step):
            base, seen = {name: counts.get(name, 0) for name in per}, {}

            def link(ins, name=None):
                name = name or step
                seen[name] = seen.get(name, 0) + 1
                ins.then_inc(sem(name), 1)
                eng.wait_ge(sem(name), q * per[name] + (base[name] + seen[name]))

            return link

        def rounds_done(counts, per, rounds):
            for name, n in per.items():
                counts[name] = counts.get(name, 0) + n * rounds

        @block.sync
        def _(sp):
            def prow(ap):
                return ap.rearrange("o (r f) -> (o r) f", f=P)

            rows = [(0, rows1["b_ada"], prow(b_ada)), (0, rows1["mu"], prow(mu_shift[:, 0:26 * P])), (0, rows1["w0"], prow(w0)),
                    (0, rows1["a0"], prow(a0)), (0, rows1["k_k"], prow(k_k)), (0, rows1["k_a"], prow(k_a)),
                    (0, rows1["r_k"], r_k.rearrange("o (r h) n -> (o r) (h n)", h=2)), (0, rows1["gn_g"], prow(gn_g)),
                    (1, rows2["gn_b"], prow(gn_b)), (1, rows2["pool_scale"], prow(pool_scale)), (1, rows2["ln1_g"], prow(ln1_g)),
                    (1, rows2["ln1_b"], prow(ln1_b)), (1, rows2["ln2_g"], prow(ln2_g)), (1, rows2["ln2_b"], prow(ln2_b)),
                    (1, rows2["mu_tail"], mu_shift[:, 26 * P:26 * P + DG1])]
            for q in range(2 * KT):
                sec, kt = (1, 0)[q // KT], q % KT
                if q >= NADA:
                    sp.wait_ge(sem("ada_used"), q - NADA + 1)
                if q == 2:
                    sp.wait_ge(sem("ptab_zero"), 1)
                if 2 <= q < 2 + len(rows):
                    tab, at, src = rows[q - 2]
                    sp.dma_start(ptab[at:at + src.shape[0], tab, 0:src.shape[1]], src).then_inc(sem("params_in"), 16)
                sp.dma_start(ada[q % NADA][:, :], w_ada[0, kt * P:(kt + 1) * P, sec * D:(sec + 1) * D]).then_inc(sem(f"ada_in{q % NADA}"), 16)
                if q == KT - 1:
                    for j in range(TB):
                        sp.dma_start(xtok[:, j, :], x[0, j * P:(j + 1) * P, :]).then_inc(sem("x_in"), 16)
            for tab, at, src in rows[2 * KT - 2:]:
                sp.dma_start(ptab[at:at + src.shape[0], tab, 0:src.shape[1]], src).then_inc(sem("params_in"), 16)
            for k in range(RING):
                load_chunk(sp, k)
            lup_next(sp, 0)
            gup_next(sp, 0)
            for k in range(RING, K_WIDE):
                load_chunk(sp, k)
                if k >= 6 and k % 3 == 0 and k < NCHUNK:
                    lup_next(sp, k // 3 - 1)
                if k >= 9 and k % 3 == 0 and k < NCHUNK:
                    gup_next(sp, k // 3 - 2)
                if k == FIRST_B:
                    gup_next(sp, PAIRS - 1)
            sp.wait_ge(sem("y_lo_ready"), PAIRS)
            for g in range(GP):
                sp.dma_start(wmix[:, g, :], pool_mix[0, g]).then_inc(sem("wmix_in"), 16)
            na = 0
            for k in range(K_WIDE, K_FF + 2 * KT):
                load_chunk(sp, k)
                for _ in range(2 if k >= FIRST_B + 9 else 0):
                    if na < 8 * KT:
                        sec, kt, half = 2 + na // (2 * KT), na // 2 % KT, na % 2
                        if na >= 2:
                            sp.wait_ge(sem("ada2_used"), na - 1)
                        sp.dma_start(ada2[:, half * S:(half + 1) * S],
                                     w_ada[0, kt * P:(kt + 1) * P, sec * D + half * S:sec * D + (half + 1) * S]
                                     ).then_inc(sem(f"ada2_in{half}"), 16)
                        na += 1
            with sp.Fori(1, NQ) as q:
                for m in range(2 * KT):
                    k = K_FF + m
                    sp.wait_ge(sem("lo_ready"), q * (2 * KT) + (k - 4 + 1))
                    if m < KT:
                        src = w_ff1[0, :, bass.ds(q * D + m * P, P)]
                    else:
                        src = w_ff2[0, bass.ds(q * D, D), (m - KT) * P:(m - KT + 1) * P]
                    sp.dma_start(w_raw[slot_of(k)][:, :, :], src.rearrange("(kt p) n -> p kt n", p=P)).then_inc(sem(f"w_in{slot_of(k)}"), 16)
            sp.wait_ge(sem("ada2_used"), 8 * KT)
            sp.wait_ge(sem("mod2"), 4)
            sp.dma_start(acc2[:, :], ln2_g.to_broadcast([P, D])).then_inc(sem("ln2_in"), 16)
            sp.dma_start(ada2[:, :], ln2_b.to_broadcast([P, D])).then_inc(sem("ln2_in"), 16)
            for j in (0, 1, 3, 2):
                if j < TB - 1:
                    sp.wait_ge(sem("out_ready"), j + 1)
                else:
                    sp.wait_ge(sem("last_out_ready"), 1)
                sp.dma_start(out[0, j * P:(j + 1) * P, :], xt2[:, j, :]).then_inc(sem("stored"), 16)
            sp.wait_ge(sem("stored"), 16 * TB)

        @block.gpsimd
        def _(pool):
            def link(ins, name=None):
                s = sem(name or "pool_step")
                key = name or "pool_step"
                counts[key] = counts.get(key, 0) + 1
                ins.then_inc(s, 1)
                pool.wait_ge(s, due(key, counts[key]))

            counts = {}
            link(pool.memset(ptab[:, :, :], 0.0), "ptab_zero")
            link(pool.memset(ident[:, :], 0.0))
            link(pool.affine_select(out=ident[:, :], in_=ident[:, :], compare_op=ALU.not_equal, fill=1.0, base=0,
                                    pattern=[[-1, P]], channel_multiplier=1), "ident_ready")

            def blocks(m, size, fill=0.0):
                v = m[:, :].rearrange("p (b t) -> p b t", t=size)
                link(pool.affine_select(out=v, in_=v, compare_op=ALU.is_ge, fill=fill, base=0,
                                        pattern=[[-size, P // size], [0, size]], channel_multiplier=1))
                link(pool.affine_select(out=v, in_=v, compare_op=ALU.is_ge, fill=fill, base=size - 1,
                                        pattern=[[size, P // size], [0, size]], channel_multiplier=-1))

            def below(m, base):
                link(pool.affine_select(out=m[:, :], in_=m[:, :], compare_op=ALU.is_ge, fill=0.0, base=base,
                                        pattern=[[-1, P]], channel_multiplier=1))

            def above(m, base):
                link(pool.affine_select(out=m[:, :], in_=m[:, :], compare_op=ALU.is_ge, fill=0.0, base=base,
                                        pattern=[[1, P]], channel_multiplier=-1))

            for m in (m16T, m16, m32, m64, mlow, mupi, ones_head):
                link(pool.memset(m[:, :], 1.0))
            link(pool.memset(ones_all[:, :], 1.0 / D))
            link(pool.memset(ones_col[:, :], 1.0))
            for t in range(16):
                link(pool.memset(rec[:, t:t + 1], 1.0 / (t + 1)))
            blocks(m16T, 16)
            above(m16T, -1)
            blocks(m16, 16)
            below(m16, -1)
            blocks(m32, 32)
            blocks(m64, 64)
            for z in range(P // C):
                for m, sign, base in ((mlow, 1, -1), (mupi, -1, 0)):
                    part = m[z * C:(z + 1) * C, :]
                    link(pool.affine_select(out=part, in_=part, compare_op=ALU.is_ge, fill=0.0, base=base,
                                            pattern=[[-sign, C]], channel_multiplier=sign))
            blocks(ones_head, N)
            for m, size in ((m32, 32), (m64, 64)):
                v = m[:, :].rearrange("p (b h t) -> p b h t", h=2, t=size // 2)
                link(pool.memset(v[:, :, 1, :], 0.0))
                w = m[:, :].rearrange("p (b t) -> p b t", t=size)
                link(pool.affine_select(out=w, in_=w, compare_op=ALU.is_ge, fill=0.0, base=-(size // 2),
                                        pattern=[[-size, P // size], [0, size]], channel_multiplier=1))
            link(pool.memset(scanm[:, :], 1.0))
            link(pool.memset(scanm[:, :].rearrange("p (c t) -> p c t", t=C)[:, :, 0:1], 0.0))
            hm = derived[:, HM:HM + 2]
            link(pool.memset(hm, 1.0))
            link(pool.affine_select(out=hm[:, 0:1], in_=hm[:, 0:1], compare_op=ALU.is_ge, fill=0.0, base=N - 1,
                                    pattern=[[0, 1]], channel_multiplier=-1))
            link(pool.affine_select(out=hm[:, 1:2], in_=hm[:, 1:2], compare_op=ALU.is_ge, fill=0.0, base=-N,
                                    pattern=[[0, 1]], channel_multiplier=1), "consts_ready")

            def split_lo(k):
                pool.wait_ge(sem("hi_ready"), due("hi_ready", k + 1))
                link(pool.tensor_tensor(part_of(k, w_lo), part_of(k, w_raw), part_of(k, w_hi).bitcast(F32), ALU.subtract),
                     "lo_ready")

            for k in range(2):
                split_lo(k)
            for f in range(1, KT, 2):
                pool.wait_ge(sem("h_f32"), due("h_f32", f + 1))
                pool.wait_ge(sem("h_hi_ready"), due("h_hi_ready", f + 1))
                link(pool.tensor_tensor(h_lo[:, f, :], hf[f % 4][:, :], h_hi[:, f, :].bitcast(F32), ALU.subtract), "h_lo_by_pool")
            pool.wait_ge(sem("h_lo_by_dve"), due("h_lo_by_dve", KT // 2))
            split_lo(2)
            split_lo(3)

            def slot(i, s):
                name = STAGES[s]
                for e in range(2):
                    if 0 <= i < PAIRS and name == "Q1":
                        for half in range(2):
                            evacuated(pool, half, i, "Mab")
                        link(pool.tensor_tensor(as_chunks(A0[e][:, :, :]), both_chunks(MAB, e), chunk_masks(m16, TB), ALU.mult), f"pooled{e}")
                    if 0 <= i < PAIRS and name == "U3":
                        pool.wait_ge(sem(f"multiplied{e}"), due(f"multiplied{e}", NS * i + STAGES.index("U2") + 1))
                        link(pool.tensor_tensor(as_chunks(A0[e][:, :, :]), both_chunks(MAB, e), chunk_masks(m32, TB), ALU.mult), f"pooled{e}")
                    if 0 <= i < PAIRS and name == "Y1":
                        pool.wait_ge(sem(f"multiplied{e}"), due(f"multiplied{e}", NS * i + STAGES.index("X1") + 1))
                        link(pool.tensor_tensor(as_chunks(A0[e][:, :, :]), both_chunks(MAB, e), chunk_masks(m64, TB), ALU.mult), f"pooled{e}")
                n = i + 1
                if n < PAIRS:
                    if s == 7:
                        pool.wait_ge(sem("scanned"), due("scanned", n + 1))
                        link(pool.tensor_tensor(sg[:, :], t3[:, :], sg[:, :], ALU.subtract), "before_sum")
                if s in (0, 7, 12) and 3 * n + 4 + s // 6 < FIRST_B:
                    split_lo(3 * n + 4 + s // 6)
                if (i, s) in SPLIT_AT:
                    split_lo(SPLIT_AT[i, s])
                if i >= 1 and s == 16:
                    pool.wait_ge(sem("y_hi_ready"), due("y_hi_ready", i))
                    link(pool.tensor_tensor(pair_block(y_lo, i - 1), SQ[:, :, :].rearrange("p j t -> p (j t)"), pair_block(y_hi, i - 1).bitcast(F32), ALU.subtract), "y_lo_ready")

            per_slot(pool, slot, counts)
            for k in range(K_WIDE - 1, K_H2):
                split_lo(k)
            for f in range(1, KT, 2):
                pool.wait_ge(sem("h2_hi"), f + 1)
                link(pool.tensor_tensor(h_lo[:, f, :], (f1, f2)[f % 2][:, :], h_hi[:, f, :].bitcast(F32), ALU.subtract), "h2_lo_by_pool")
            with pool.Fori(0, NQ - 1) as q:
                again = loop_link(pool, counts, q, {"lo_ready": NFF}, "pool_step")
                for k in range(K_H2, K_H2 + NFF):
                    pool.wait_ge(sem("hi_ready"), q * NFF + (k + 1))
                    again(pool.tensor_tensor(part_of(k, w_lo), part_of(k, w_raw), part_of(k, w_hi).bitcast(F32), ALU.subtract), "lo_ready")
            rounds_done(counts, {"lo_ready": NFF}, NQ - 1)
            for k in range(K_H2 + (NQ - 1) * NFF, NALL):
                split_lo(k)
            pool.wait_ge(sem("ln2_in"), 32)
            pool.wait_ge(sem("ln2_normed"), 1)
            link(pool.tensor_tensor(xt2[:, TB - 1, :], xt2[:, TB - 1, :], acc2[:, :], ALU.mult))
            link(pool.tensor_tensor(xt2[:, TB - 1, :], xt2[:, TB - 1, :], ada2[:, :], ALU.add), "last_out_ready")

        @block.scalar
        def _(act):
            counts = {}

            def link(ins, name=None):
                key = name or "act_step"
                counts[key] = counts.get(key, 0) + 1
                ins.then_inc(sem(key), 1)
                act.wait_ge(sem(key), due(key, counts[key]))

            def split_hi(k):
                slot = chunks[k][1]
                act.wait_ge(sem(f"w_in{slot}"), due(f"w_in{slot}", 16 * uses[k]))
                if before[k] is not None:
                    act.wait_ge(sem("w_used"), due("w_used", before[k] + 1))
                link(act.activation(part_of(k, w_hi), part_of(k, w_raw), ACT.Copy), "hi_ready")

            def shift_first(k, dst, mucol, rows=P):
                act.wait_ge(sem("w_used"), due("w_used", k + 1))
                link(act.activation(dst[0:rows, :], in_bank(k)[0:rows, :], ACT.Copy, scale=of_pair(derived, OMM + mucol, rows)), "kept")

            act.dma_start(crow[:, :], c.rearrange("o (r f) -> (o r) f", f=P)).then_inc(sem("c_in"), 16)
            act.wait_ge(sem("c_cols"), due("c_cols", 1))
            link(act.activation(derived[:, CS:CS + KT], derived[:, CCOL:CCOL + KT], ACT.Tanh, scale=0.5), "c_tanh")
            for k in range(2):
                split_hi(k)
            for f in range(KT):
                act.wait_ge(sem("h_f32"), due("h_f32", f + 1))
                link(act.activation(h_hi[:, f, :], hf[f % 4][:, :], ACT.Copy), "h_hi_ready")
            for k, (dst, mucol, rows) in enumerate(((xwa, 24, P), (xg0, 25, P), (xg1, 26, DG1))):
                shift_first(k, dst, mucol, rows)
                if k < 2:
                    split_hi(2 + k)
                act.wait_ge(sem("shifted"), due("shifted", k + 1))
                if k == 0:
                    link(act.activation(xwa[0:DW, :], xwa[0:DW, :], ACT.Tanh), "lora_act")
                else:
                    link(act.activation(dst[0:rows, :], dst[0:rows, :], ACT.Tanh, scale=0.5), "lora_act")

            def take(e, i, s):
                name = STAGES[s]
                dst = {"Q1": A1, "Q2": A1T, "Q3": A0, "Q4": A0T, "Q5": A1, "X1": A1T, "Tr1": A1, "X2": A1T,
                       "Tr2": A1}.get(name)
                act.wait_ge(sem(f"multiplied{e}"), due(f"multiplied{e}", NS * i + s + 1))
                src = blk(stage_bank(e, NS * i + s)[:, :])
                if name == "PT":
                    link(act.activation(PT[e][C:P, :, :], stage_bank(e, NS * i + s)[C:P, :].rearrange("p (m c) -> p m c", c=C),
                                        ACT.Copy), f"taken_by_act{e}")
                elif name == "AHT":
                    rows = slice(N * e, N * e + N)
                    link(act.activation(AHT[rows, :, :], src[rows], ACT.Copy), f"taken_by_act{e}")
                else:
                    link(act.activation(dst[e][:, :, :], src, ACT.Copy), f"taken_by_act{e}")

            def slot(i, s):
                name = STAGES[s]
                n = i + 1
                if n < PAIRS and s in (6, 12, 18):
                    k = 3 + 3 * n + s // 6 - 1
                    shift_first(k, (xk, xr, xv)[s // 6 - 1], ((8, 0, 16)[s // 6 - 1]) + n)
                if i >= 1 and s < NCH:
                    act.wait_ge(sem("sa_done"), due("sa_done", NCH * (i - 1) + s + 1))
                    link(act.activation(SV[0:C, s, :], CH[0:C, 0:P], ACT.Copy), "sa_taken")
                if (n, s) in POOLED_AT:
                    g = POOLED_AT.index((n, s))
                    act.wait_ge(sem("w_used"), due("w_used", NCHUNK + g + 1))
                    link(act.activation(UP[g][:, :], G0[:, :], ACT.Copy), "pool_in")
                if 0 <= i < PAIRS and name not in BY_DVE:
                    for e in range(2):
                        take(e, i, s)
                if s in (0, 7, 12) and 3 * n + 4 + s // 6 < FIRST_B:
                    split_hi(3 * n + 4 + s // 6)
                if (i, s) in SPLIT_AT and s < 14:
                    split_hi(SPLIT_AT[i, s])
                if n < PAIRS:
                    if s == 4:
                        act.wait_ge(sem("g1_done"), due("g1_done", g1_at[("decay", n)] + 1))
                        link(act.activation(sg[:, :], G1[:, :], ACT.Tanh, bias=of_pair(derived, HW0 + n), scale=0.5), "decay_taken")
                    if s == 5:
                        act.wait_ge(sem("g1_done"), due("g1_done", g1_at[("aaa", n)] + 1))
                        link(act.activation(aa[:, :], G1[:, :], ACT.Tanh, bias=of_pair(derived, HA0 + n), scale=0.5), "aaa_taken")
                    if s == 7:
                        act.wait_ge(sem("shifted"), due("shifted", 3 + 3 * n + 1))
                        link(act.activation(t1[:, :], xk[:, :], ACT.Square, scale=of_pair(params, rows1["k_k"] + n)), "squared")
                    if s == 8:
                        act.wait_ge(sem("g1_done"), due("g1_done", g1_at[("norm", n)] + 1))
                        link(act.activation(t1[:, :], G1[:, :], ACT.Sqrt), "norm_taken")
                    if s == 11:
                        act.wait_ge(sem("before_sum"), due("before_sum", n + 1))
                        link(act.activation(sg[:, :], sg[:, :], ACT.Exp, scale=-EXPM))
                        link(act.activation(t4[:, :], t3[:, :], ACT.Exp, scale=-EXPM))
                        link(act.activation(t3[:, :], t3[:, :], ACT.Exp, scale=EXPM), "exps")
                    if s in (18, 20):
                        src, dst, made, done = ((Bt, Bpad, "b_made", "b_padded"), (Kt, Kpad, "prepared", "k_padded"))[s // 20]
                        act.wait_ge(sem(made), due(made, n + 1))
                        for e in range(2):
                            link(act.activation(dst[:, e, :], src[:, :], ACT.Copy, scale=der(HM + e)), done)
                if 0 <= i < PAIRS and s == 8:
                    if i >= 1:
                        act.wait_ge(sem("so_done"), due("so_done", NCH * i))
                        act.wait_ge(sem("s_taken"), due("s_taken", NCH * i))
                    act.wait_ge(sem("prepared"), due("prepared", i + 1))
                    link(act.activation(Rc[:, :], Rf[:, :], ACT.Copy), "carried")
                    link(act.activation(DCc[:, :], DC[:, :], ACT.Copy), "carried")
                if 0 <= i < PAIRS and s == 15:
                    act.wait_ge(sem("g1_done"), due("g1_done", g1_at[("gate", i)] + 1))
                    if i >= 1:
                        act.wait_ge(sem("y_ready"), due("y_ready", i))
                    link(act.activation(gate[:, :], G1[:, :], ACT.Copy), "gate_taken")
                    link(act.activation(bonus_c[:, :], bonus[:, :], ACT.Copy), "bonus_carried")
                if 0 <= i < PAIRS and s in (9, 10, 11):
                    job, dst = (("tokA", Atok[:, :, :]), ("tokBK0", BK[:, 0:4, :]), ("tokBK1", BK[:, 4:8, :]))[s - 9]
                    act.wait_ge(sem("g1_done"), due("g1_done", g1_at[(job, i)] + 1))
                    link(act.activation(dst, blk(G1[:, :]), ACT.Copy), "tok_taken")
                if 0 <= i < PAIRS and s in (12, 14):
                    half = (s - 12) // 2
                    act.wait_ge(sem("g1_done"), due("g1_done", g1_at[(f"tokV{half}", i)] + 1))
                    link(act.activation(SV[C:P, 4 * half:4 * half + 4, :], blk(G1[:, :])[C:P], ACT.Copy), "v_taken")
                if i >= 1:
                    if s == 9:
                        act.wait_ge(sem("centred"), due("centred", i))
                        link(act.activation(SQ[:, :, :], OC[:, :, :], ACT.Square), "o_squared")
                    if s == 9:
                        act.wait_ge(sem("o_var"), due("o_var", i))
                        link(act.activation(gn[:, 2, :], gn[:, 1, :], ACT.Sqrt), "o_std")
                    if s == 13:
                        act.wait_ge(sem("g1_done"), due("g1_done", g1_at[("outT", i - 1)] + 1))
                        link(act.activation(SQ[:, :, :], blk(G1[:, :]), ACT.Identity, scale=of_pair(params, rows1["gn_g"] + i - 1),
                                            bias=of_pair(params, P + rows2["gn_b"] + i - 1)), "out_taken")
                    if s == 15:
                        act.wait_ge(sem("y_ready"), due("y_ready", i))
                        link(act.activation(pair_block(y_hi, i - 1), SQ[:, :, :].rearrange("p j t -> p (j t)"), ACT.Copy), "y_hi_ready")
                if (i, s) in SPLIT_AT and s == 14:
                    split_hi(SPLIT_AT[i, s])

            per_slot(act, slot, counts)
            def square_of(n):
                act.wait_ge(sem("ln1_centred"), n + 1)
                if n >= 2:
                    act.wait_ge(sem("ln1_sq_used"), n - 1)
                link(act.activation((f1, f2)[n % 2][:, :], res[:, n, :], ACT.Square), "ln1_squared")

            act.wait_ge(sem("y_lo_ready"), PAIRS)

            def gates_of(n):
                for m, k in enumerate((K_GP[n], K_GR[n])):
                    if n >= 2:
                        split_hi(k + 3)
                    act.wait_ge(sem("w_used"), k + 1)
                    if n >= 1:
                        act.wait_ge(sem("mixed"), n)
                    link(act.activation((f1, f2)[m][:, :], GATE_BANKS[n][m][:, :], ACT.Sigmoid), "gated")

            def mixed_hi(n):
                act.wait_ge(sem("mix_sum"), n + 1)
                link(act.activation(mix_hi[:, n, :], f3[:, :], ACT.Copy), "mixed_hi")

            split_hi(K_WIDE - 1)
            gates_of(0)
            split_hi(K_WIDE)
            split_hi(K_WIDE + 1)
            for g in range(GP):
                act.wait_ge(sem("pool_mixed"), g + 1)
                if g >= 1:
                    act.wait_ge(sem("mp_ready"), g)
                link(act.activation(lnv[:, :], (G0, CH)[g % 2][:, :], ACT.Copy,
                                    scale=params[:, P + 8 + g:P + 9 + g]), "pool_scaled")
                link(act.activation(mp_hi[:, g, :], lnv[:, :], ACT.Copy), "mp_hi_ready")
            split_hi(K_WIDE + 2)
            split_hi(K_WIDE + 3)
            mixed_hi(0)
            gates_of(1)
            split_hi(K_WIDE + 4)
            mixed_hi(1)
            for n in range(2, KT):
                gates_of(n)
                if n == KT - 1:
                    for j in range(TB):
                        act.dma_start(x_again[:, j, :], x[0, j * P:(j + 1) * P, :]).then_inc(sem("x_again"), 16)
                split_hi(K_RU[n] + 3)
                split_hi(K_PU[n] + 3)
                mixed_hi(n)
            for n in range(KT):
                act.wait_ge(sem("x_turned2"), n + 1)
                link(act.activation(res[:, n, :], bank[6 + n % 2][:, :], ACT.Copy, scale=ALPHA), "res_ready")
                split_hi(K_OUT + n + 3)
                if n >= 1:
                    square_of(n - 1)
            square_of(KT - 1)
            link(act.activation(small[:, 56:57], rec[:, 0:1], ACT.Sqrt))
            act.wait_ge(sem("ln1_eps"), 1)
            link(act.activation(lnv[:, :], lnv[:, :], ACT.Sqrt), "ln1_std")
            for f in range(KT):
                hb = (f1, f2)[f % 2]
                act.wait_ge(sem("ln1_normed"), f + 1)
                if f >= 2:
                    act.wait_ge(sem(("h2_lo_by_dve", "h2_lo_by_pool")[f % 2]), f // 2)
                link(act.activation(hb[:, :], res[:, f, :], ACT.Identity, scale=mod[:, 32 + f:33 + f], bias=mod[:, 24 + f:25 + f]))
                link(act.activation(h_hi[:, f, :], hb[:, :], ACT.Copy), "h2_hi")
            for f in range(KT):
                link(act.activation(res[:, f, :], res[:, f, :], ACT.Identity, scale=small[:, f:f + 1], bias=small[:, 8 + f:9 + f]),
                     "res_scaled")

            def split_again(link, k, q):
                act.wait_ge(sem(f"w_in{slot_of(k)}"), q * (16 * NFF // 4) + 16 * uses[k])
                act.wait_ge(sem("w_used"), q * NFF + (before[k] + 1))
                link(act.activation(part_of(k, w_hi), part_of(k, w_raw), ACT.Copy), "hi_ready")

            def ff_quarter(link, q, last):
                for n in range(KT):
                    k = K_FF + n
                    split_again(link, k + 3, q)
                    act.wait_ge(sem("w_used"), q * NFF + (k + 1))
                    if n >= 2:
                        act.wait_ge(sem("hidden"), q * KT + (n - 1))
                    link(act.activation((f1, f2)[n % 2][:, :], bank[k % 4][:, :], ACT.Relu), "relu")
                    link(act.activation(y_hi[:, n, :], (f1, f2)[n % 2][:, :], ACT.Square), "hidden_hi")
                for n in range(KT):
                    if not last or n + 3 < KT:
                        split_again(link, K_FF + KT + n + 3, q)
                    if last:
                        act.wait_ge(sem("turned_back"), n + 1)
                        link(act.activation(xt2[:, :, n * P:(n + 1) * P], blk(bank[4 + n % 2][:, :]), ACT.Copy), "out_tokens")

            per = {"hi_ready": NFF, "relu": KT, "hidden_hi": KT}
            with act.Fori(0, NQ - 1) as q:
                ff_quarter(loop_link(act, counts, q, per, "act_step"), q, False)
            rounds_done(counts, per, NQ - 1)
            ff_quarter(link, NQ - 1, True)
            act.wait_ge(sem("ln2_eps"), 1)
            link(act.activation(small[:, 32:36], small[:, 28:32], ACT.Sqrt), "ln2_std")
            act.wait_ge(sem("ln2_cols"), 1)
            link(act.activation(xt2[:, TB - 1, :], xt2[:, TB - 1, :], ACT.Identity, scale=small[:, 36 + TB - 1:36 + TB],
                                bias=small[:, 40:41]), "ln2_normed")

        @block.vector
        def _(dve):
            counts = {}

            def link(ins, name=None):
                key = name or "dve_step"
                counts[key] = counts.get(key, 0) + 1
                ins.then_inc(sem(key), 1)
                dve.wait_ge(sem(key), due(key, counts[key]))

            dve.wait_ge(sem("c_turned"), due("c_turned", 1))
            link(dve.tensor_copy(derived[:, CCOL:CCOL + KT], bank[0][:, 2 * P:2 * P + KT]), "c_cols")
            dve.wait_ge(sem("c_tanh"), due("c_tanh", 1))
            link(dve.tensor_scalar(derived[:, CS:CS + KT], derived[:, CS:CS + KT], 0.5, 0.5, ALU.mult, ALU.add))
            link(dve.tensor_tensor(derived[:, CS:CS + KT], derived[:, CS:CS + KT], derived[:, CCOL:CCOL + KT], ALU.mult))
            for q in range(2 * KT):
                kt, half = q % KT, q // KT
                dve.wait_ge(sem(f"ada_in{q % NADA}"), due(f"ada_in{q % NADA}", 16 * (q // NADA + 1)))
                if kt == 0:
                    link(dve.tensor_scalar(acc[:, half, :], ada[q % NADA][:, :], der(CS), None, ALU.mult), "ada_used")
                else:
                    link(dve.scalar_tensor_tensor(out=acc[:, half, :], in0=ada[q % NADA][:, :], scalar=der(CS + kt),
                                                  in1=acc[:, half, :], op0=ALU.mult, op1=ALU.add), "ada_used")
            dve.wait_ge(sem("param_cols"), due("param_cols", 1))
            link(dve.tensor_copy(params[:, 0:P], bank[0][:, 0:P]))
            link(dve.tensor_copy(params[:, P:2 * P], bank[0][:, P:2 * P]))
            link(dve.tensor_scalar(derived[:, OMM:OMM + 26], params[:, 48:74], -1.0, 1.0, ALU.mult, ALU.add))
            link(dve.tensor_scalar(der(OMM + 26), params[:, P + 44:P + 45], -1.0, 1.0, ALU.mult, ALU.add))
            link(dve.tensor_scalar(derived[:, OMKA:OMKA + 8], params[:, 98:106], -1.0, 1.0, ALU.mult, ALU.add))
            link(dve.tensor_scalar(derived[:, HW0:HW0 + 8], params[:, 74:82], 0.5, None, ALU.mult))
            link(dve.tensor_scalar(derived[:, HA0:HA0 + 8], params[:, 82:90], 0.5, None, ALU.mult))
            dve.wait_ge(sem("mod_done"), due("mod_done", 1))
            link(dve.tensor_tensor(mod[:, 8:16], bank[1][:, 0:8], params[:, 8:16], ALU.add))
            link(dve.tensor_scalar(mod[:, 8:16], mod[:, 8:16], 1.0, None, ALU.add))
            link(dve.tensor_tensor(mod[:, 0:8], bank[1][:, 8:16], params[:, 0:8], ALU.add))
            for f in range(KT):
                dve.wait_ge(sem("x_turned"), due("x_turned", f + 1))
                if f >= 4:
                    dve.wait_ge(sem("h_lo_by_pool"), due("h_lo_by_pool", f // 2 - 1))
                link(dve.tensor_scalar(hf[f % 4][:, :], bank[2 + f % 4][:, :], mod[:, 8 + f:9 + f], mod[:, f:f + 1], ALU.mult, ALU.add), "h_f32")
                if f % 2 == 1:
                    dve.wait_ge(sem("h_hi_ready"), due("h_hi_ready", f))
                    link(dve.tensor_tensor(h_lo[:, f - 1, :], hf[(f - 1) % 4][:, :], h_hi[:, f - 1, :].bitcast(F32), ALU.subtract),
                         "h_lo_by_dve")

            def shift_rest(k, dst, mu_ap, rows=P):
                dve.wait_ge(sem("kept"), due("kept", k + 1))
                link(dve.scalar_tensor_tensor(out=dst[0:rows, 1:S], in0=in_bank(k)[0:rows, 0:S - 1], scalar=mu_ap,
                                              in1=dst[0:rows, 1:S], op0=ALU.mult, op1=ALU.add), "shifted")

            for k, (dst, mu_ap, rows) in enumerate(((xwa, col(48 + 24), P), (xg0, col(48 + 25), P),
                                                    (xg1, params[0:DG1, P + 44:P + 45], DG1))):
                shift_rest(k, dst, mu_ap, rows)
                dve.wait_ge(sem("lora_act"), due("lora_act", k + 1))
                if k:
                    link(dve.tensor_scalar(dst[0:rows, :], dst[0:rows, :], 0.5, 0.5, ALU.mult, ALU.add), "lora_ready")
                else:
                    link(dve.memset(gn[:, :, :], 0.0), "lora_ready")

            def take(e, i, s):
                name = STAGES[s]
                dve.wait_ge(sem(f"multiplied{e}"), due(f"multiplied{e}", NS * i + s + 1))
                src = blk(stage_bank(e, NS * i + s)[:, :])
                key = f"taken_by_dve{e}"
                if name == "MabT":
                    if e == 0:
                        dve.wait_ge(sem("multiplied1"), due("multiplied1", NS * i + s + 1))
                        for head in range(2):
                            for half in range(2):
                                part = stage_bank(half, NS * i + s)[:, 0:4 * C].rearrange("p (j h c) -> p j h c", j=2, h=2)
                                link(dve.tensor_tensor(as_chunks(A0T[head][:, 2 * half:2 * half + 2, :]),
                                                       part[:, :, head, :].unsqueeze(2).to_broadcast([P, 2, 2, C]),
                                                       chunk_masks(m16T, 2), ALU.mult), f"taken_by_dve{half}" if head else None)
                elif name in PACKED:
                    if name == "Mak":
                        link(dve.tensor_tensor(TT[e][:, :, :], A0T[e][:, :, :], over_blocks(ident), ALU.add))
                    dst, mask = {"Mab": (MAB, mlow), "Mak": (MAK, mlow), "Mr0": (MR[:, 0:4], mupi), "Mr1": (MR[:, 4:8], mupi)}[name]
                    link(dve.tensor_tensor(halves(dst, e), stage_bank(e, NS * i + s)[:, 0:4 * C].rearrange("p (m c) -> p m c", c=C),
                                           mask[:, :].unsqueeze(1).to_broadcast([P, 4, C]), ALU.mult), key)
                else:
                    link(dve.tensor_tensor(TT[e][:, :, :], src, TT[e][:, :, :], ALU.add), key)

            def pool_step(g, step):
                w, u = 2 << g, UP[g]
                cur, nxt = (t2, t3) if step % 2 else (t3, t2)
                if step == 0:
                    dve.wait_ge(sem("pool_in"), due("pool_in", g + 1))
                    link(dve.tensor_copy(nxt[:, 0:1], u[:, 0:1]))
                    link(dve.tensor_tensor(nxt[:, 1:S], u[:, 1:S], u[:, 0:S - 1], ALU.add))
                elif step <= g:
                    d = 1 << step
                    link(dve.tensor_copy(nxt[:, 0:d], cur[:, 0:d]))
                    link(dve.tensor_tensor(nxt[:, d:S], cur[:, d:S], cur[:, 0:S - d], ALU.add))
                else:
                    link(dve.tensor_tensor(cur[:, 0:w], cur[:, 0:w], rec[:, 0:w], ALU.mult))
                    link(dve.tensor_tensor(u[:, 0:w], cur[:, 0:w], u[:, 0:w], ALU.subtract))
                    link(dve.scalar_tensor_tensor(out=u[:, w:S], in0=cur[:, w:S], scalar=1.0 / w, in1=u[:, w:S],
                                                  op0=ALU.mult, op1=ALU.subtract), "pooled_up")

            def slot(i, s):
                name = STAGES[s]
                n = i + 1
                if n < PAIRS and s in (6, 12, 18):
                    k = 3 + 3 * n + s // 6 - 1
                    shift_rest(k, (xk, xr, xv)[s // 6 - 1], of_pair(params, 48 + (8, 0, 16)[s // 6 - 1] + n))
                if 0 <= i < PAIRS and name in BY_DVE:
                    for e in range(2):
                        take(e, i, s)
                if i >= 1 and s < NCH:
                    dve.wait_ge(sem("state_done"), due("state_done", NCH * (i - 1) + s + 1))
                    link(dve.tensor_tensor(Stmp[:, :], CH[:, 2 * P:3 * P], Sbd[:, :], ALU.add))
                    dve.wait_ge(sem("so_done"), due("so_done", NCH * (i - 1) + s + 1))
                    link(dve.scalar_tensor_tensor(out=Sbd[:, :], in0=Stmp[:, :], scalar=DCc[:, s:s + 1], in1=ones_head[:, :],
                                                  op0=ALU.mult, op1=ALU.mult), "s_taken")
                if n < PAIRS:
                    if s == 5:
                        dve.wait_ge(sem("decay_taken"), due("decay_taken", n + 1))
                        link(dve.tensor_scalar(sg[:, :], sg[:, :], 0.5, 0.5, ALU.mult, ALU.add))
                        link(dve.tensor_tensor_scan(t3[:, :], scanm[:, :], sg[:, :], 0.0, ALU.mult, ALU.add), "scanned")
                    if s == 6:
                        dve.wait_ge(sem("aaa_taken"), due("aaa_taken", n + 1))
                        link(dve.tensor_scalar(aa[:, :], aa[:, :], 0.5, 0.5, ALU.mult, ALU.add))
                    if s == 9:
                        dve.wait_ge(sem("norm_taken"), due("norm_taken", n + 1))
                        link(dve.tensor_scalar(t1[:, :], t1[:, :], 1e-12, None, ALU.max))
                    if 9 <= s <= 12:
                        qq = slice((s - 9) * P, (s - 8) * P)
                        link(dve.reciprocal(t2[:, qq], t1[:, qq]))
                    if s == 13:
                        link(dve.scalar_tensor_tensor(out=t1[:, :], in0=xk[:, :], scalar=of_pair(params, 90 + n), in1=t2[:, :], op0=ALU.mult, op1=ALU.mult))
                        link(dve.tensor_scalar(t2[:, :], aa[:, :], of_pair(params, 98 + n), of_pair(derived, OMKA + n), ALU.mult, ALU.add))
                    if s == 14:
                        link(dve.tensor_tensor(t2[:, :], xk[:, :], t2[:, :], ALU.mult))
                        link(dve.scalar_tensor_tensor(out=xk[:, :], in0=xr[:, :], scalar=of_pair(params, 106 + n), in1=t2[:, :], op0=ALU.mult, op1=ALU.mult), "rk_ready")
                    if s == 15:
                        dve.wait_ge(sem("exps"), due("exps", n + 1))
                        link(dve.scalar_tensor_tensor(out=At[:, :], in0=t1[:, :], scalar=-1.0, in1=sg[:, :], op0=ALU.mult, op1=ALU.mult))
                        for e in range(2):
                            link(dve.tensor_scalar(Apad[:, e, :], At[:, :], der(HM + e), None, ALU.mult))
                    if s == 16:
                        if n >= 1:
                            dve.wait_ge(sem("carried"), due("carried", 2 * n))
                        link(dve.tensor_tensor(Rf[:, :], xr[:, :], t4[:, :], ALU.mult))
                        link(dve.tensor_copy(DC[:, :], t4[:, :].rearrange("p (c t) -> p c t", t=C)[:, :, C - 1]))
                        for e in range(2):
                            link(dve.tensor_scalar(Rpad[:, e, :], Rf[:, :], der(HM + e), None, ALU.mult))
                    if s == 17:
                        link(dve.tensor_tensor(aa[:, :], t1[:, :], aa[:, :], ALU.mult))
                        link(dve.tensor_tensor(Bt[:, :], aa[:, :], t3[:, :], ALU.mult), "b_made")
                    if s == 18:
                        dve.wait_ge(sem("g1_done"), due("g1_done", g1_at[("bonus", n)] + 1))
                        if n >= 1:
                            dve.wait_ge(sem("bonus_carried"), due("bonus_carried", n))
                        link(dve.tensor_tensor(bonus[:, :], G1[:, :], xv[:, :], ALU.mult), "bonus_taken")
                    if s == 19:
                        link(dve.tensor_tensor(Kt[:, :], t2[:, :], t3[:, :], ALU.mult), "prepared")
                if i >= 1:
                    g8 = lambda ap: ap.rearrange("p j (e v) -> p (j e) v", e=2)
                    ob = OB[:, :].rearrange("p (g v) -> p g v", v=N)
                    if s == 8:
                        link(dve.tensor_reduce(gn[:, 0, :], ob, AX_X, ALU.add))
                        link(dve.tensor_scalar(gn[:, 0, :], gn[:, 0, :], 1.0 / N, None, ALU.mult))
                        link(dve.tensor_tensor(OC[:, :, :].rearrange("p j (e v) -> p (j e) v", e=2), ob,
                                               gn[:, 0, :].unsqueeze(2).to_broadcast([P, 8, N]), ALU.subtract), "centred")
                    if s == 9:
                        dve.wait_ge(sem("o_squared"), due("o_squared", i))
                        link(dve.tensor_reduce(gn[:, 1, :], SQ[:, :, :].rearrange("p j (e v) -> p (j e) v", e=2), AX_X, ALU.add))
                        link(dve.tensor_scalar(gn[:, 1, :], gn[:, 1, :], 1.0 / N, GN_EPS, ALU.mult, ALU.add), "o_var")
                    if s == 11:
                        dve.wait_ge(sem("o_std"), due("o_std", i))
                        link(dve.reciprocal(gn[:, 3, :], gn[:, 2, :]))
                        oc = OC[:, :, :].rearrange("p j (e v) -> p (j e) v", e=2)
                        link(dve.tensor_tensor(oc, oc, gn[:, 3, :].unsqueeze(2).to_broadcast([P, 8, N]), ALU.mult), "o_normed")
                    if s == 14:
                        dve.wait_ge(sem("out_taken"), due("out_taken", i))
                        sq = SQ[:, :, :].rearrange("p j t -> p (j t)")
                        link(dve.tensor_tensor(sq, sq, bonus_c[:, :], ALU.add))
                        link(dve.tensor_tensor(sq, sq, gate[:, :], ALU.mult), "y_ready")
                if (i, s) in POOL_STEPS:
                    pool_step(*POOL_STEPS[i, s])
                if s == 20 and i >= 0 and i < PAIRS:
                    link(dve.memset(Sbd[:, :], 0.0), "s_zero")

            per_slot(dve, slot, counts)
            def mod_section(m):
                dve.wait_ge(sem("ada_turned"), m + 1)
                for half in range(2):
                    link(dve.tensor_reduce(mod[:, 16 + 8 * m + 4 * half:20 + 8 * m + 4 * half], blk(bank[4 + half][:, :]), AX_X, ALU.add))
                link(dve.tensor_tensor(mod[:, 16 + 8 * m:24 + 8 * m], mod[:, 16 + 8 * m:24 + 8 * m],
                                       params[:, 16 + 8 * m:24 + 8 * m], ALU.add), "mod2")

            def ada_tile(tile):
                kt = tile % KT
                if kt == 0 and tile:
                    dve.wait_ge(sem("ada_turned"), tile // KT)
                for half in range(2):
                    cols = slice(half * S, (half + 1) * S)
                    dve.wait_ge(sem(f"ada2_in{half}"), 16 * (tile + 1))
                    if kt == 0:
                        link(dve.tensor_scalar(acc2[:, cols], ada2[:, cols], der(CS), None, ALU.mult), "ada2_used")
                    else:
                        link(dve.scalar_tensor_tensor(out=acc2[:, cols], in0=ada2[:, cols], scalar=der(CS + kt), in1=acc2[:, cols],
                                                      op0=ALU.mult, op1=ALU.add), "ada2_used")

            for g in range(GP):
                dve.wait_ge(sem("mp_hi_ready"), g + 1)
                link(dve.tensor_tensor(mp_lo[:, g, :], lnv[:, :], mp_hi[:, g, :].bitcast(F32), ALU.subtract), "mp_ready")
            for n in range(KT):
                if n in (3, 5, 7):
                    mod_section((n - 3) // 2)
                if 1 <= n < KT - 1:
                    ada_tile(4 * n - 4)
                    ada_tile(4 * n - 3)
                dve.wait_ge(sem("gated"), 2 * n + 2)
                dve.wait_ge(sem("w_used"), K_RU[n] + 1)
                link(dve.tensor_tensor(f2[:, :], f2[:, :], GATE_BANKS[n][2][:, :], ALU.mult), "ru_taken")
                if 1 <= n < KT - 1:
                    ada_tile(4 * n - 2)
                dve.wait_ge(sem("w_used"), K_PU[n] + 1)
                link(dve.tensor_tensor(f1[:, :], f1[:, :], GATE_BANKS[n][3][:, :], ALU.mult), "pu_taken")
                link(dve.tensor_tensor(f3[:, :], f1[:, :], f2[:, :], ALU.add), "mix_sum")
                if 1 <= n < KT - 1:
                    ada_tile(4 * n - 1)
                dve.wait_ge(sem("mixed_hi"), n + 1)
                link(dve.tensor_tensor(mix_lo[:, n, :], f3[:, :], mix_hi[:, n, :].bitcast(F32), ALU.subtract), "mixed")
            for tile in range(4 * KT - 8, 4 * KT - 4):
                ada_tile(tile)
            link(dve.tensor_scalar(mod[:, 16:24], mod[:, 16:24], 1.0, None, ALU.add))
            link(dve.tensor_scalar(mod[:, 32:40], mod[:, 32:40], 1.0, None, ALU.add))
            link(dve.tensor_scalar(small[:, 0:8], params[:, P + 12:P + 20], ALPHA, None, ALU.mult))
            link(dve.tensor_scalar(small[:, 8:16], params[:, P + 20:P + 28], ALPHA, None, ALU.mult))
            link(dve.tensor_tensor(small[:, 16:24], params[:, P + 20:P + 28], mod[:, 32:40], ALU.mult))
            link(dve.tensor_tensor(mod[:, 24:32], small[:, 16:24], mod[:, 24:32], ALU.add))
            link(dve.tensor_tensor(mod[:, 32:40], params[:, P + 12:P + 20], mod[:, 32:40], ALU.mult))
            m0, sum1, sum2 = f3, SUM1[:, :], SUM2[:, :]

            def add_square(n):
                dve.wait_ge(sem("ln1_squared"), n + 1)
                if n == 0:
                    link(dve.tensor_copy(sum2, f1[:, :]), "ln1_sq_used")
                else:
                    link(dve.tensor_tensor(sum2, sum2, (f1, f2)[n % 2][:, :], ALU.add), "ln1_sq_used")

            for n in range(KT):
                dve.wait_ge(sem("w_used"), K_OUT + n + 1)
                dve.wait_ge(sem("res_ready"), n + 1)
                link(dve.scalar_tensor_tensor(out=res[:, n, :], in0=OUT_BANKS[n % 4][:, :], scalar=mod[:, 16 + n:17 + n],
                                              in1=res[:, n, :], op0=ALU.mult, op1=ALU.add), "sum_taken")
                if n == 0:
                    dve.wait_ge(sem("ln1_m0"), 1)
                    link(dve.tensor_scalar(m0[:, :], bank[5][:, :], float(D // P), None, ALU.mult), "m0_taken")
                link(dve.tensor_tensor(res[:, n, :], res[:, n, :], m0[:, :], ALU.subtract), "ln1_centred")
                if n == 0:
                    link(dve.tensor_copy(sum1, res[:, 0, :]))
                else:
                    link(dve.tensor_tensor(sum1, sum1, res[:, n, :], ALU.add), "ln1_summed")
                    add_square(n - 1)
                if n < 4:
                    ada_tile(4 * KT - 4 + n)
                if n == 5:
                    mod_section(3)
                    link(dve.tensor_scalar(mod[:, 40:48], mod[:, 40:48], 1.0, None, ALU.add))
            add_square(KT - 1)
            dve.wait_ge(sem("ln1_sums"), 1)
            link(dve.tensor_copy(lnv[:, :], bank[4][:, :]))
            link(dve.tensor_tensor(f3[:, :], bank[4][:, :], lnv[:, :], ALU.mult))
            dve.wait_ge(sem("ln1_sums"), 2)
            link(dve.tensor_tensor(lnv[:, :], bank[5][:, :], f3[:, :], ALU.subtract))
            link(dve.tensor_scalar(lnv[:, :], lnv[:, :], 0.0, LN_EPS, ALU.max, ALU.add), "ln1_eps")

            def centre(f):
                link(dve.tensor_tensor(res[:, f, :], res[:, f, :], bank[4][:, :], ALU.subtract))

            centre(0)
            dve.wait_ge(sem("ln1_std"), 1)
            link(dve.reciprocal(f3[:, :], lnv[:, :]))
            for f in range(KT):
                if f >= 1:
                    centre(f)
                link(dve.tensor_tensor(res[:, f, :], res[:, f, :], f3[:, :], ALU.mult), "ln1_normed")
                if f % 2:
                    dve.wait_ge(sem("h2_hi"), f)
                    link(dve.tensor_tensor(h_lo[:, f - 1, :], f1[:, :], h_hi[:, f - 1, :].bitcast(F32), ALU.subtract), "h2_lo_by_dve")

            PARTS = ((0, S), (S, D - P), (D - P, D))

            def statistics(part):
                a, b = PARTS[part]
                for j in range(TB):
                    link(dve.bn_stats(stat[:, 3 * j + part, :], xt2[:, j, a:b]))

            def ff_quarter(link, q, last):
                for n in range(KT):
                    dve.wait_ge(sem("relu"), q * KT + (n + 1))
                    r = (f1, f2)[n % 2]
                    link(dve.tensor_tensor(f3[:, :], r[:, :], r[:, :], ALU.mult))
                    dve.wait_ge(sem("hidden_hi"), q * KT + (n + 1))
                    link(dve.tensor_tensor(y_lo[:, n, :], f3[:, :], y_hi[:, n, :].bitcast(F32), ALU.subtract), "hidden")
                for n in range(KT):
                    k = K_FF + KT + n
                    dve.wait_ge(sem("w_used"), q * NFF + (k + 1))
                    dve.wait_ge(sem("res_scaled"), n + 1)
                    link(dve.scalar_tensor_tensor(out=res[:, n, :], in0=bank[k % 4][:, :], scalar=mod[:, 40 + n:41 + n],
                                                  in1=res[:, n, :], op0=ALU.mult, op1=ALU.add), "sum_taken")
                    if last and n == KT - 2:
                        dve.wait_ge(sem("out_tokens"), KT // 2)
                        statistics(0)

            per = {"dve_step": KT, "hidden": KT, "sum_taken": KT}
            with dve.Fori(0, NQ - 1) as q:
                ff_quarter(loop_link(dve, counts, q, per, "dve_step"), q, False)
            rounds_done(counts, per, NQ - 1)
            ff_quarter(link, NQ - 1, True)
            dve.wait_ge(sem("out_tokens"), KT - 1)
            statistics(1)
            dve.wait_ge(sem("out_tokens"), KT)
            statistics(2)
            for j in range(TB):
                link(dve.bn_aggr(small[:, 20 + 2 * j:22 + 2 * j], stat[:, 3 * j:3 * j + 3, :]))
            mv = small[:, 20:28].rearrange("p (j two) -> p j two", two=2)
            link(dve.tensor_scalar(small[:, 28:32], mv[:, :, 1], LN_EPS, None, ALU.add), "ln2_eps")
            dve.wait_ge(sem("ln2_std"), 1)
            link(dve.reciprocal(small[:, 36:40], small[:, 32:36]))
            link(dve.scalar_tensor_tensor(out=small[:, 40:41], in0=small[:, 18 + 2 * TB:19 + 2 * TB], scalar=-1.0,
                                          in1=small[:, 35 + TB:36 + TB], op0=ALU.mult, op1=ALU.mult), "ln2_cols")
            dve.wait_ge(sem("ln2_in"), 32)
            for j in range(TB - 1):
                link(dve.scalar_tensor_tensor(out=xt2[:, j, :], in0=xt2[:, j, :], scalar=small[:, 20 + 2 * j:21 + 2 * j], in1=acc2[:, :],
                                              op0=ALU.subtract, op1=ALU.mult))
                link(dve.scalar_tensor_tensor(out=xt2[:, j, :], in0=xt2[:, j, :], scalar=small[:, 36 + j:37 + j], in1=ada2[:, :],
                                              op0=ALU.mult, op1=ALU.add), "out_ready")

        @block.tensor
        def _(pe):
            pe.wait_ge(sem("ident_ready"), due("ident_ready", 1))
            pe.wait_ge(sem("c_in"), due("c_in", 16))
            pe.transpose(bank[0][:, 2 * P:2 * P + KT], crow[:, :], ident[0:KT, 0:KT]).then_inc(sem("c_turned"), 1)
            pe.wait_ge(sem("consts_ready"), due("consts_ready", 1))

            def turn_x(f):
                if f >= 4:
                    pe.wait_ge(sem("h_f32"), due("h_f32", f - 3))
                for j in range(TB):
                    mm = pe.transpose(bank[2 + f % 4][:, j * P:(j + 1) * P], xtok[:, j, f * P:(f + 1) * P], ident[:, :])
                mm.then_inc(sem("x_turned"), 1)

            pe.wait_ge(sem("x_in"), due("x_in", 16 * TB))
            for f in range(4):
                turn_x(f)
            pe.wait_ge(sem("params_in"), due("params_in", 16 * 15))
            pe.wait_ge(sem("c_cols"), due("c_cols", 1))
            for tab in range(2):
                mm = pe.transpose(bank[0][:, tab * P:(tab + 1) * P], ptab[:, tab, :], ident[:, :])
            mm.then_inc(sem("param_cols"), 1)
            for half in range(2):
                pe.wait_ge(sem("ada_used"), due("ada_used", KT * (half + 1)))
                for f in range(KT):
                    mm = pe.matmul(bank[1][:, 8 * half + f:8 * half + f + 1], acc[:, half, f * P:(f + 1) * P],
                                   ones_col[:, :], start=True, stop=True)
            mm.then_inc(sem("mod_done"), 1)
            for f in range(4, KT):
                turn_x(f)

            def gemm(k, kts):
                width = chunk_cols[k][1]
                pe.wait_ge(sem("lo_ready"), due("lo_ready", k + 1))
                if k == 2:
                    pe.wait_ge(sem("h_f32"), due("h_f32", 1))
                for kt in kts:
                    pe.wait_ge(sem(("h_lo_by_dve", "h_lo_by_pool")[kt % 2]), kt // 2 + 1)
                    terms = [(w_hi, h_hi), (w_hi, h_lo), (w_lo, h_hi)]
                    for m, (w, hx) in enumerate(terms):
                        mm = pe.matmul(in_bank(k)[0:width, :], w[k % RING][:, kt, 0:width], hx[:, kt, :],
                                       start=(kt == 0 and m == 0), stop=(kt == KT - 1 and m == 2))
                mm.then_inc(sem("w_used"), 1)

            G1_TAKEN = {"decay": ("decay_taken", 1), "aaa": ("aaa_taken", 1), "norm": ("norm_taken", 1), "tokA": ("tok_taken", 3, 1),
                        "tokBK0": ("tok_taken", 3, 2), "tokBK1": ("tok_taken", 3, 3), "tokV0": ("v_taken", 2, 1),
                        "tokV1": ("v_taken", 2, 2), "outT": ("out_taken", 1),
                        "gate": ("gate_taken", 1), "bonus": ("bonus_taken", 1)}

            def g1_free(job, n):
                at = g1_at[(job, n)]
                if at:
                    before, m = g1_jobs[at - 1]
                    name, per, *k = G1_TAKEN[before]
                    pe.wait_ge(sem(name), due(name, per * m + (k[0] if k else 1)))

            for k in range(3):
                gemm(k, range(KT))

            def stage(e, i, s):
                name = STAGES[s]
                if s >= 2:
                    evacuated(pe, e, i, STAGES[s - 2])
                elif i >= 1:
                    evacuated(pe, e, i - 1, STAGES[NS + s - 2])
                dep = {"Q2": ["Q1"], "Q3": ["Q2"], "Q4": ["Q3"], "Q5": ["Q4"], "U1": ["Mak"], "U2": ["U1"], "U3": ["U2", "Q5"], "X1": ["U3"],
                       "Tr1": [], "Y1": ["Tr1"], "X2": ["Y1"], "Tr2": [], "Y2": ["Tr2"], "PT": ["Y2"], "AHT": []}
                for d in dep.get(name, []):
                    evacuated(pe, e, i, d)
                if name == "MabT":
                    pe.wait_ge(sem("b_made"), due("b_made", i + 1))
                if name == "Mab":
                    pe.wait_ge(sem("b_padded"), due("b_padded", 2 * (i + 1)))
                if name == "Mak":
                    pe.wait_ge(sem("k_padded"), due("k_padded", 2 * (i + 1)))
                if name == "Q1":
                    evacuated(pe, 1, i, "MabT")
                    pe.wait_ge(sem(f"pooled{e}"), due(f"pooled{e}", 3 * i + 1))
                if name == "X1":
                    pe.wait_ge(sem(f"pooled{e}"), due(f"pooled{e}", 3 * i + 2))
                if name == "X2":
                    pe.wait_ge(sem(f"pooled{e}"), due(f"pooled{e}", 3 * i + 3))
                if name == "AHT":
                    pe.wait_ge(sem("tok_taken"), due("tok_taken", 3 * i + 1))
                b = stage_bank(e, NS * i + s)
                if name in PACKED:
                    if name in ("Mr0", "Mr1"):
                        for m in range(2):
                            c = 4 * (name == "Mr1") + 2 * e + m
                            ts = slice(c * C, (c + 1) * C)
                            for rows, tokens in ((slice(0, C), Bt), (slice(C, P), Kt)):
                                mm = pe.matmul(b[rows, m * P:(m + 1) * P], tokens[:, ts], Rpad[:, :, ts],
                                               start=True, stop=True, skip_group_check=True)
                        mm.then_inc(sem(f"multiplied{e}"), 1)
                        return
                    tokens, both = {"MabT": (Bt, Apad), "Mab": (At, Bpad), "Mak": (At, Kpad)}[name]
                    for m in range(4):
                        j, z = 2 * e + m // 2, m % 2
                        ts = slice(j * P + z * C, j * P + (z + 1) * C)
                        mm = pe.matmul(b[z * C:(z + 1) * C, (m // 2) * P:(m // 2 + 1) * P], tokens[:, ts], both[:, :, ts],
                                       start=True, stop=True, skip_group_check=True)
                    mm.then_inc(sem(f"multiplied{e}"), 1)
                    return
                if name == "PT":
                    for m in range(2 * TB):
                        j, z = m // 2, m % 2
                        mm = pe.matmul(b[C:P, m * C:(m + 1) * C], MAK[:, j, e, :], TT[e][:, j, z * C:(z + 1) * C],
                                       start=True, stop=True, skip_group_check=True)
                    mm.then_inc(sem(f"multiplied{e}"), 1)
                    return
                for j in range(TB):
                    tb = slice(j * P, (j + 1) * P)
                    o = b[:, tb]
                    if name in ("Q2", "Q4", "Tr1", "Tr2"):
                        src = {"Q2": A1, "Q4": A0}.get(name, TT)
                        mm = pe.transpose(o, src[e][:, j, :], ident[:, :])
                        continue
                    if name == "AHT":
                        o = b[N * e:N * e + N, tb]
                    lhs, rhs = {
                        "Q1": (A0T[e][:, j, :], A0[e][:, j, :]), 
                        "Q3": (A1T[e][:, j, :], A1[e][:, j, :]),
                        "U1": (A1[e][:, j, :], TT[e][:, j, :]), "Q5": (A0T[e][:, j, :], A0[e][:, j, :]),
                        "U2": (A0[e][:, j, :], TT[e][:, j, :]), "U3": (A1[e][:, j, :], TT[e][:, j, :]),
                        "X1": (A0[e][:, j, :], TT[e][:, j, :]), "X2": (A0[e][:, j, :], TT[e][:, j, :]),
                        "Y1": (A1[e][:, j, :], A1T[e][:, j, :]), "Y2": (A1[e][:, j, :], A1T[e][:, j, :]),
                        "AHT": (Atok[:, j, N * e:N * e + N], TT[e][:, j, :]),
                    }[name]
                    mm = pe.matmul(o, lhs, rhs, start=True, stop=True)
                mm.then_inc(sem(f"multiplied{e}"), 1)

            def chain_sa(i, c):
                j, z = c // 2, c % 2
                if c == 0:
                    pe.wait_ge(sem("s_zero"), due("s_zero", i + 1))
                    evacuated(pe, 0, i, "AHT")
                    evacuated(pe, 1, i, "AHT")
                    pe.wait_ge(sem("v_taken"), due("v_taken", 2 * i + 2))
                if NCH * i + c:
                    pe.wait_ge(sem("s_taken"), due("s_taken", NCH * i + c))
                pe.matmul(CH[0:C, 0:P], AHT[:, j, C * z:C * z + C], Sbd[:, :], start=True, stop=False, skip_group_check=True)
                for e in range(2):
                    mm = pe.matmul(CH[0:C, N * e:N * e + N], PT[e][C:P, c, :], SV[C:P, c, N * e:N * e + N],
                                   start=False, stop=(e == 1), skip_group_check=True)
                mm.then_inc(sem("sa_done"), 1)

            def chain_so(i, c):
                j, z = c // 2, c % 2
                rows, cols = slice(C * z, C * z + C), slice(c * C, (c + 1) * C)
                tb = slice(j * P, (j + 1) * P)
                pe.wait_ge(sem("sa_taken"), due("sa_taken", NCH * i + c + 1))
                pe.matmul(CH[:, 2 * P:3 * P], BK[:, c, :], SV[:, c, :], start=True, stop=True,
                          skip_group_check=True).then_inc(sem("state_done"), 1)
                pe.matmul(OB[rows, tb], Rc[:, cols], Sbd[:, :], start=True, stop=False, skip_group_check=True)
                for e in range(2):
                    mm = pe.matmul(OB[rows, j * P + N * e:j * P + N * e + N], MR[:, c, e, :], SV[:, c, N * e:N * e + N],
                                   start=False, stop=(e == 1), skip_group_check=True)
                mm.then_inc(sem("so_done"), 1)

            def slot(i, s):
                n = i + 1
                early = s < 5
                if i >= 1 and s < NCH and not early:
                    chain_sa(i - 1, s)
                if 0 <= i < PAIRS:
                    for e in range(2):
                        stage(e, i, s)
                if i >= 1 and s < NCH and early:
                    chain_sa(i - 1, s)
                    if i < PAIRS and 3 + 3 * n + s // 6 < FIRST_B:
                        gemm_piece(3 + 3 * n + s // 6, s % 6)
                if i == PAIRS and s < NCH:
                    late_piece(9 * s, 5)
                if i >= 1 and s < NCH:
                    chain_so(i - 1, s)
                if n < PAIRS:
                    if s == 4:
                        pe.wait_ge(sem("lup_in"), due("lup_in", 32 * (n + 1)))
                        pe.wait_ge(sem("lora_ready"), due("lora_ready", 3))
                        g1_free("decay", n)
                        pe.matmul(G1[:, :], lup[0:DW, 0, :], xwa[0:DW, :], start=True, stop=True).then_inc(sem("g1_done"), 1)
                    if s == 5:
                        g1_free("aaa", n)
                        pe.matmul(G1[:, :], lup[DW:P, 0, :], xwa[DW:P, :], start=True, stop=True).then_inc(sem("g1_done"), 1)
                    if s == 8:
                        g1_free("norm", n)
                        pe.wait_ge(sem("squared"), due("squared", n + 1))
                        pe.matmul(G1[:, :], ones_head[:, :], t1[:, :], start=True, stop=True).then_inc(sem("g1_done"), 1)
                    if s == 18:
                        g1_free("bonus", n)
                        pe.wait_ge(sem("rk_ready"), due("rk_ready", n + 1))
                        pe.matmul(G1[:, :], ones_head[:, :], xk[:, :], start=True, stop=True).then_inc(sem("g1_done"), 1)
                if 0 <= i < PAIRS and s in (9, 10, 11, 12, 14):
                    job = {9: "tokA", 10: "tokBK0", 11: "tokBK1", 12: "tokV0", 14: "tokV1"}[s]
                    g1_free(job, i)
                    for m in range(TB):
                        o = slice(m * P, (m + 1) * P)
                        if job == "tokA":
                            mm = pe.transpose(G1[:, o], At[:, o], ident[:, :])
                            continue
                        c = 4 * int(job[-1]) + m
                        ts = slice(c * C, (c + 1) * C)
                        mm = pe.matmul(G1[C:P, o], (xv if job[:-1] == "tokV" else Kt)[:, ts], ident[:, :], start=True, stop=True,
                                       skip_group_check=True)
                        if job[:-1] == "tokBK":
                            mm = pe.transpose(G1[0:C, o], Bt[:, ts], ident[:, :])
                    mm.then_inc(sem("g1_done"), 1)
                if i >= 1 and s == 13:
                    g1_free("outT", i - 1)
                    pe.wait_ge(sem("o_normed"), due("o_normed", i))
                    for j in range(TB):
                        mm = pe.transpose(G1[:, j * P:(j + 1) * P], OC[:, j, :], ident[:, :])
                    mm.then_inc(sem("g1_done"), 1)
                if 0 <= i < PAIRS and s == 15:
                    g1_free("gate", i)
                    pe.wait_ge(sem("gup_in"), due("gup_in", 32 * (i + 1)))
                    pe.matmul(G1[:, :], lup[:, 1, :], xg0[:, :], start=True, stop=False)
                    pe.matmul(G1[:, :], lup[0:DG1, 2, :], xg1[:, :], start=False, stop=True).then_inc(sem("g1_done"), 1)
                if i == PAIRS:
                    if s in (8, 14):
                        late_piece(72 + 24 * (s == 14), 24)
                    elif s < NCH:
                        late_piece(9 * s + 5, 4)
                elif s < 18 and 3 + 3 * n + s // 6 < FIRST_B and not (early and i >= 1):
                    gemm_piece(3 + 3 * n + s // 6, s % 6)

            LATE = [G0] + GATE_BANKS[0][:2] + GATE_BANKS[1][:2]

            def late_piece(first, count):
                for at in range(first, first + count):
                    k, m = FIRST_B - 1 + at // 24, at % 24
                    if m == 0:
                        pe.wait_ge(sem("lo_ready"), due("lo_ready", k + 1))
                    if at == 0:
                        pe.wait_ge(sem("pool_in"), due("pool_in", GP - 1))
                    if at == 24:
                        for e in range(2):
                            evacuated(pe, e, PAIRS - 1, "PT")
                            evacuated(pe, e, PAIRS - 1, "AHT")
                    kt, term = m // 3, m % 3
                    w, hx = ((w_hi, h_hi), (w_hi, h_lo), (w_lo, h_hi))[term]
                    mm = pe.matmul(LATE[at // 24][:, :], w[slot_of(k)][:, kt, :], hx[:, kt, :], start=(m == 0), stop=(m == 23))
                    if m == 23:
                        mm.then_inc(sem("w_used"), 1)

            def gemm_piece(k, part):
                if part == 0:
                    pe.wait_ge(sem("lo_ready"), due("lo_ready", k + 1))
                    if k > NCHUNK:
                        pe.wait_ge(sem("pool_in"), due("pool_in", k - NCHUNK))
                    elif k >= len(IN_BANKS):
                        pe.wait_ge(sem("shifted"), due("shifted", k))
                    else:
                        pe.wait_ge(sem("h_f32"), due("h_f32", KT))
                for m in range(4 * part, 4 * part + 4):
                    kt, term = m // 3, m % 3
                    w, hx = ((w_hi, h_hi), (w_hi, h_lo), (w_lo, h_hi))[term]
                    mm = pe.matmul(in_bank(k)[:, :], w[k % RING][:, kt, :], hx[:, kt, :], start=(m == 0), stop=(m == 23))
                if part == 5:
                    mm.then_inc(sem("w_used"), 1)

            per_slot(pe, slot, {})
            def turn_back(n):
                pe.wait_ge(sem("sum_taken"), KT * NQ + n + 1)
                if n >= 2:
                    pe.wait_ge(sem("out_tokens"), n - 1)
                for j in range(TB):
                    mm = pe.transpose(bank[4 + n % 2][:, j * P:(j + 1) * P], res[:, n, j * P:(j + 1) * P], ident[:, :])
                mm.then_inc(sem("turned_back"), 1)

            def product(k, o, hi, lo, free, ready=None, more=0):
                kts = chunks[k][0].shape[1]
                pe.wait_ge(sem("lo_ready"), more + (k + 1))
                free()
                for kt in range(kts):
                    if ready:
                        ready(kt)
                    for m, (w, hx) in enumerate(((w_hi, hi), (w_hi, lo), (w_lo, hi))):
                        mm = pe.matmul(o, w[chunks[k][1]][:, kt, :], hx[:, kt, :], start=(kt == 0 and m == 0),
                                       stop=(kt == kts - 1 and m == 2))
                mm.then_inc(sem("w_used"), 1)

            def taken(name, n):
                return lambda: pe.wait_ge(sem(name), n) if n > 0 else None

            def turn_section(m):
                pe.wait_ge(sem("ada2_used"), 2 * KT * (m + 1))
                if m:
                    pe.wait_ge(sem("mod2"), m)
                else:
                    pe.wait_ge(sem("gated"), 4)
                if m == 3:
                    pe.wait_ge(sem("m0_taken"), 1)
                for f in range(KT):
                    mm = pe.transpose(bank[4 + f // 4][:, f % 4 * P:(f % 4 + 1) * P], acc2[:, f * P:(f + 1) * P], ident[:, :])
                mm.then_inc(sem("ada_turned"), 1)

            def gate_free(n, name, per, at):
                last = 0 if n == 2 else n - 1
                return taken(name, per * last + at + 1) if n >= 2 else lambda: None

            def rwkv_up(n):
                product(K_RU[n], GATE_BANKS[n][2][:, :], y_hi, y_lo, gate_free(n, "ru_taken", 1, 0))

            def pool_up(n):
                product(K_PU[n], GATE_BANKS[n][3][:, :], mp_hi, mp_lo, gate_free(n, "pu_taken", 1, 0),
                        lambda kt: pe.wait_ge(sem("mp_ready"), kt + 1))

            pe.wait_ge(sem("y_lo_ready"), PAIRS)
            rwkv_up(0)
            pe.wait_ge(sem("wmix_in"), 16 * GP)
            for g in range(GP):
                pe.wait_ge(sem("pooled_up"), g + 1)
                if g >= 2:
                    pe.wait_ge(sem("pool_scaled"), g - 1)
                pe.matmul((G0, CH)[g % 2][:, :], wmix[:, g, :], UP[g][:, :], start=True, stop=True).then_inc(sem("pool_mixed"), 1)
            rwkv_up(1)
            pe.wait_ge(sem("pool_scaled"), GP)
            pool_up(0)
            pool_up(1)
            for n in range(2, KT):
                product(K_GP[n], GATE_BANKS[n][0][:, :], h_hi, h_lo, gate_free(n, "gated", 2, 0))
                product(K_GR[n], GATE_BANKS[n][1][:, :], h_hi, h_lo, gate_free(n, "gated", 2, 1))
                if n in (3, 5, 7):
                    turn_section((n - 3) // 2)
                rwkv_up(n)
                pool_up(n)

            for n in range(KT):
                for f in {2: (0, 1), 3: (2,), 4: (3,), 5: (4,), 6: (5,), 7: (6, 7)}.get(n, ()):
                    pe.wait_ge(sem("x_again"), 16 * TB)
                    if f >= 2:
                        pe.wait_ge(sem("res_ready"), f - 1)
                    for j in range(TB):
                        mm = pe.transpose(bank[6 + f % 2][:, j * P:(j + 1) * P], x_again[:, j, f * P:(f + 1) * P], ident[:, :])
                    mm.then_inc(sem("x_turned2"), 1)

                def free(n=n):
                    if n < 2:
                        pe.wait_ge(sem("gated"), 2 * KT)
                    elif n < 4:
                        pe.wait_ge(sem("pu_taken"), KT)
                    else:
                        pe.wait_ge(sem("sum_taken"), n - 3)
                product(K_OUT + n, OUT_BANKS[n % 4][:, :], mix_hi, mix_lo, free,
                        (lambda kt: pe.wait_ge(sem("mixed"), kt + 1)) if n == 0 else None)
                if n == 5:
                    turn_section(3)
                if n == 2:
                    pe.wait_ge(sem("mod2"), 3)
                    pe.wait_ge(sem("sum_taken"), 1)
                    pe.matmul(bank[5][:, :], ones_all[:, :], res[:, 0, :], start=True, stop=True).then_inc(sem("ln1_m0"), 1)
            pe.wait_ge(sem("ln1_summed"), KT - 1)
            pe.wait_ge(sem("mod2"), 4)
            pe.matmul(bank[4][:, :], ones_all[:, :], SUM1[:, :], start=True, stop=True).then_inc(sem("ln1_sums"), 1)
            pe.wait_ge(sem("ln1_sq_used"), KT)
            pe.matmul(bank[5][:, :], ones_all[:, :], SUM2[:, :], start=True, stop=True).then_inc(sem("ln1_sums"), 1)
            def ff_quarter(q, last):
                for n in range(KT):
                    k = K_FF + n
                    pe.wait_ge(*((sem("relu"), q * KT + (n - 3)) if n >= 4 else (sem("sum_taken"), q * KT + (KT + n - 3))))
                    product(k, bank[k % 4][:, :], h_hi, h_lo, lambda: None,
                            lambda kt: pe.wait_ge(sem(("h2_lo_by_dve", "h2_lo_by_pool")[kt % 2]), kt // 2 + 1), q * NFF)
                for n in range(KT):
                    k = K_FF + KT + n
                    pe.wait_ge(*((sem("sum_taken"), q * KT + (KT + n - 3)) if n >= 4 else (sem("relu"), q * KT + (KT + n - 3))))
                    product(k, bank[k % 4][:, :], y_hi, y_lo, lambda: None,
                            (lambda kt: pe.wait_ge(sem("hidden"), q * KT + (kt + 1))) if n == 0 else None, q * NFF)
                    if last and n >= 1:
                        turn_back(n - 1)

            pe.wait_ge(sem("sum_taken"), KT)
            with pe.Fori(0, NQ - 1) as q:
                ff_quarter(q, False)
            ff_quarter(NQ - 1, True)
            turn_back(KT - 1)


_INS = ['x', 'c', 'w_ada', 'b_ada', 'w_in', 'mu_shift', 'pool_mix', 'pool_scale', 'w_pool_up', 'w0', 'w_decay_up', 'a0',
        'w_aaa_up', 'w_gate_up', 'k_k', 'k_a', 'r_k', 'gn_g', 'gn_b', 'w_rwkv_up', 'w_out', 'ln1_g', 'ln1_b', 'w_ff1',
        'w_ff2', 'ln2_g', 'ln2_b']
_OUTS = [((1, 512, 1024), 'float32')]


def kernel(**inputs):
    import numpy as _np
    import concourse.bacc as _bacc
    from concourse import mybir as _mybir
    from concourse.bass_utils import run_bass_kernel_spmd as _run

    nc = _bacc.Bacc("TRN2", target_bir_lowering=False, num_devices=1)
    arrays, args = {}, []
    for name in _INS:
        a = _np.ascontiguousarray(inputs[name])
        arrays[f"in_{name}_dram"] = a
        args.append(nc.dram_tensor(f"in_{name}_dram", a.shape, _mybir.dt.from_np(a.dtype), kind="ExternalInput").ap())
    for i, (shape, dtype) in enumerate(_OUTS):
        dt = _mybir.dt.from_np(_np.dtype(dtype))
        args.append(nc.dram_tensor(f"out_{i}_dram", shape, dt, kind="ExternalOutput").ap())
    build(nc, *args)
    r = _run(nc, [arrays], core_ids=[0])
    got = tuple(r.results[0][f"out_{i}_dram"] for i in range(len(_OUTS)))
    return got[0]
```
